# Optimizing a Trainium2 kernel written in Bass

```python
import math
import jax
import jax.numpy as jnp
from jax import lax
import numpy as np

D_MODEL = 1024
BATCH = 1
SEQ = 512
DEPTH = 2

DN_HEADS = 8
DN_HEAD_DIM = 128
DN_WIDTH = DN_HEADS * DN_HEAD_DIM
DN_CONV = 5
DN_CHUNK = 64
SW_HEADS = 16
SW_KV_HEADS = 4
SW_HEAD_DIM = 64
SW_WINDOW = 128
SW_BLOCK = 128
ROPE_THETA = 10000.0
FFN_HIDDEN = ((8 * D_MODEL // 3 + 255) // 256) * 256
DN_ALPHA = (2.0 * DEPTH) ** 0.25
DN_BETA = (8.0 * DEPTH) ** -0.25
LN_EPS = 1e-5
RMS_EPS = 1e-6

COL_SIZES = (
    3 * DN_WIDTH,
    DN_WIDTH,
    2 * DN_HEADS,
    2 * DN_HEADS,
    SW_HEADS * SW_HEAD_DIM,
    SW_KV_HEADS * SW_HEAD_DIM,
    SW_KV_HEADS * SW_HEAD_DIM,
    2 * D_MODEL,
)
IN_COLS = sum(COL_SIZES)

kernel_name = "hybrid_deltanet_swa_deepnorm_encoder"

def layer_norm(x, g, b):
    xf = x.astype(jnp.float32)
    mu = jnp.mean(xf, axis=-1, keepdims=True)
    var = jnp.mean(jnp.square(xf - mu), axis=-1, keepdims=True)
    y = (xf - mu) * lax.rsqrt(var + LN_EPS) * g.astype(jnp.float32) + b.astype(jnp.float32)
    return y.astype(x.dtype)

def l2_normalize(x):
    xf = x.astype(jnp.float32)
    return xf * lax.rsqrt(jnp.sum(xf * xf, axis=-1, keepdims=True) + RMS_EPS)

def depthwise_conv_centred(x, w):
    c = x.shape[-1]
    half = DN_CONV // 2
    return lax.conv_general_dilated(
        x, w[:, None, :].astype(x.dtype), window_strides=(1,),
        padding=[(half, half)], dimension_numbers=("NWC", "WIO", "NWC"),
        feature_group_count=c)

def rope_tables(seq_len):
    half = SW_HEAD_DIM // 2
    inv_freq = ROPE_THETA ** (-jnp.arange(half, dtype=jnp.float32) / half)
    pos = jnp.arange(seq_len, dtype=jnp.float32)
    ang = pos[:, None] * inv_freq[None, :]
    return jnp.cos(ang), jnp.sin(ang)

def apply_rope(x, cos, sin):
    x1, x2 = jnp.split(x, 2, axis=-1)
    c = cos[None, :, None, :].astype(x.dtype)
    s = sin[None, :, None, :].astype(x.dtype)
    return jnp.concatenate([x1 * c - x2 * s, x2 * c + x1 * s], axis=-1)

def chunk_gated_delta_rule(q, k, v, g, beta):
    b_, t_, h_, dk = q.shape
    dv = v.shape[-1]
    n_chunks = t_ // DN_CHUNK
    f32 = jnp.float32

    def chunks(a):
        a = a.astype(f32).reshape((b_, n_chunks, DN_CHUNK, h_) + a.shape[3:])
        return jnp.moveaxis(a, 3, 1)

    q, k, v, beta = chunks(q), chunks(k), chunks(v), chunks(beta)
    g = jnp.cumsum(chunks(g), axis=-1)
    idx = jnp.arange(DN_CHUNK)
    lower_incl = idx[:, None] >= idx[None, :]
    strict = idx[:, None] > idx[None, :]
    decay = jnp.exp(jnp.where(lower_incl, g[..., :, None] - g[..., None, :], -jnp.inf))

    kk = jnp.einsum("bhnid,bhnjd->bhnij", k, k)
    eye = jnp.eye(DN_CHUNK, dtype=f32)
    lmat = jnp.where(strict, beta[..., :, None] * kk * decay, 0.0) + eye
    t_inv = lax.linalg.triangular_solve(
        lmat, jnp.broadcast_to(eye, lmat.shape), left_side=True, lower=True,
        unit_diagonal=True)
    u = jnp.einsum("bhnij,bhnjd->bhnid", t_inv, v * beta[..., None])
    w = jnp.einsum("bhnij,bhnjd->bhnid", t_inv, k * (beta * jnp.exp(g))[..., None])
    qk = jnp.einsum("bhnid,bhnjd->bhnij", q, k) * decay
    q_dec = q * jnp.exp(g)[..., None]
    g_last = g[..., -1]
    k_dec = k * jnp.exp(g_last[..., None] - g)[..., None]

    xs = tuple(jnp.moveaxis(a, 2, 0) for a in (u, w, qk, q_dec, k_dec, g_last))

    def step(state, inp):
        u_n, w_n, qk_n, qd_n, kd_n, gl_n = inp
        v_new = u_n - jnp.einsum("bhcd,bhde->bhce", w_n, state)
        o_n = (jnp.einsum("bhcd,bhde->bhce", qd_n, state)
               + jnp.einsum("bhij,bhje->bhie", qk_n, v_new))
        state = (state * jnp.exp(gl_n)[..., None, None]
                 + jnp.einsum("bhcd,bhce->bhde", kd_n, v_new))
        return state, o_n

    s0 = jnp.zeros((b_, h_, dk, dv), f32)
    _, o = lax.scan(step, s0, xs)
    return jnp.transpose(o, (1, 0, 3, 2, 4)).reshape(b_, t_, h_, dv)

def windowed_gqa_sink(q, k, v, sinks):
    b_, t_, hq, d = q.shape
    hkv = k.shape[2]
    grp = hq // hkv
    nb = t_ // SW_BLOCK
    pad = ((0, 0), (SW_BLOCK, SW_BLOCK), (0, 0), (0, 0))

    def bands(a):
        ab = jnp.pad(a, pad).reshape(b_, nb + 2, SW_BLOCK, hkv, d)
        return jnp.concatenate([ab[:, :-2], ab[:, 1:-1], ab[:, 2:]], axis=2)

    kb, vb = bands(k), bands(v)
    qb = q.reshape(b_, nb, SW_BLOCK, hkv, grp, d)
    s = jnp.einsum("bnqhgd,bnkhd->bnhgqk", qb, kb).astype(jnp.float32) * (d ** -0.5)
    blk = jnp.arange(nb)[:, None, None] * SW_BLOCK
    qpos = blk + jnp.arange(SW_BLOCK)[None, :, None]
    kpos = blk - SW_BLOCK + jnp.arange(3 * SW_BLOCK)[None, None, :]
    valid = (jnp.abs(qpos - kpos) <= SW_WINDOW) & (kpos >= 0) & (kpos < t_)
    s = jnp.where(valid[None, :, None, None], s, -jnp.inf)
    sink = jnp.broadcast_to(
        sinks.astype(jnp.float32).reshape(hkv, grp)[None, None, :, :, None, None],
        s.shape[:-1] + (1,))
    p = jax.nn.softmax(jnp.concatenate([s, sink], axis=-1), axis=-1)[..., :-1]
    o = jnp.einsum("bnhgqk,bnkhd->bnqhgd", p.astype(v.dtype), vb)
    return o.reshape(b_, t_, hq * d)

def token_mixing(x, w_in, conv_w, a_log, dt_bias, dn_norm_w, sinks,
                 w_branch_a, w_branch_b, w_out, cos, sin):
    b_, t_, _ = x.shape
    proj = jnp.einsum("btd,de->bte", x, w_in)
    offs = [sum(COL_SIZES[:i + 1]) for i in range(len(COL_SIZES) - 1)]
    qkv_dn, z, b_dn, a_dn, q_sw, k_sw, v_sw, gates = jnp.split(proj, offs, axis=-1)

    qkv_dn = jax.nn.silu(depthwise_conv_centred(qkv_dn, conv_w))
    q_dn, k_dn, v_dn = [a.reshape(b_, t_, DN_HEADS, DN_HEAD_DIM)
                        for a in jnp.split(qkv_dn, 3, axis=-1)]
    q_dn = l2_normalize(q_dn) * (DN_HEAD_DIM ** -0.5)
    k_dn = l2_normalize(k_dn)
    beta = jax.nn.sigmoid(b_dn.astype(jnp.float32)).reshape(b_, t_, 2, DN_HEADS)
    g = -jnp.exp(a_log.astype(jnp.float32)) * jax.nn.softplus(
        a_dn.astype(jnp.float32).reshape(b_, t_, 2, DN_HEADS) + dt_bias.astype(jnp.float32))
    o_fwd = chunk_gated_delta_rule(q_dn, k_dn, v_dn, g[:, :, 0], beta[:, :, 0])
    flip = lambda a: jnp.flip(a, axis=1)
    o_bwd = flip(chunk_gated_delta_rule(flip(q_dn), flip(k_dn), flip(v_dn),
                                        flip(g[:, :, 1]), flip(beta[:, :, 1])))
    o_dn = o_fwd + o_bwd
    o_dn = (o_dn * lax.rsqrt(jnp.mean(o_dn * o_dn, axis=-1, keepdims=True) + RMS_EPS)
            * dn_norm_w.astype(jnp.float32)
            * jax.nn.silu(z.astype(jnp.float32)).reshape(b_, t_, DN_HEADS, DN_HEAD_DIM))
    o_dn = o_dn.reshape(b_, t_, DN_WIDTH).astype(x.dtype)

    q_sw = apply_rope(q_sw.reshape(b_, t_, SW_HEADS, SW_HEAD_DIM), cos, sin)
    k_sw = apply_rope(k_sw.reshape(b_, t_, SW_KV_HEADS, SW_HEAD_DIM), cos, sin)
    v_sw = v_sw.reshape(b_, t_, SW_KV_HEADS, SW_HEAD_DIM)
    o_sw = windowed_gqa_sink(q_sw, k_sw, v_sw, sinks)

    gate_a, gate_b = jnp.split(jax.nn.sigmoid(gates), 2, axis=-1)
    merged = (gate_a * jnp.einsum("bte,ed->btd", o_dn, w_branch_a)
              + gate_b * jnp.einsum("bte,ed->btd", o_sw, w_branch_b))
    return jnp.einsum("btd,de->bte", merged, w_out)

def swiglu_ffn(x, w_gate_up, w_down):
    gu = jnp.einsum("btd,df->btf", x, w_gate_up)
    gate, up = jnp.split(gu, 2, axis=-1)
    return jnp.einsum("btf,fd->btd", jax.nn.silu(gate) * up, w_down)

def setup_inputs(seed: int = 0) -> dict:
    key = jax.random.key(seed)
    ks = jax.random.split(key, 20)
    f32 = jnp.float32
    nrm = lambda k, shape, scale: jax.random.normal(k, shape, f32) * scale
    x = jax.random.normal(ks[0], (BATCH, SEQ, D_MODEL), f32)
    w_in = nrm(ks[1], (DEPTH, D_MODEL, IN_COLS), D_MODEL ** -0.5)
    conv_w = nrm(ks[2], (DEPTH, DN_CONV, 3 * DN_WIDTH), DN_CONV ** -0.5)
    a_log = jnp.log(jax.random.uniform(ks[3], (DEPTH, 2, DN_HEADS), f32, 1.0, 16.0))
    dt = jnp.exp(jax.random.uniform(ks[4], (DEPTH, 2, DN_HEADS), f32,
                                    math.log(1e-3), math.log(1e-1)))
    dt_bias = dt + jnp.log(-jnp.expm1(-dt))
    dn_norm_w = 1.0 + nrm(ks[5], (DEPTH, DN_HEAD_DIM), 0.02)
    sinks = nrm(ks[6], (DEPTH, SW_HEADS), 0.5)
    w_branch_a = nrm(ks[7], (DEPTH, DN_WIDTH, D_MODEL), DN_WIDTH ** -0.5)
    w_branch_b = nrm(ks[8], (DEPTH, SW_HEADS * SW_HEAD_DIM, D_MODEL),
                     (SW_HEADS * SW_HEAD_DIM) ** -0.5)
    w_out = nrm(ks[9], (DEPTH, D_MODEL, D_MODEL), D_MODEL ** -0.5 * DN_BETA)
    ln1_g = 1.0 + nrm(ks[10], (DEPTH, D_MODEL), 0.02)
    ln1_b = nrm(ks[11], (DEPTH, D_MODEL), 0.02)
    w_gate_up = nrm(ks[12], (DEPTH, D_MODEL, 2 * FFN_HIDDEN), D_MODEL ** -0.5)
    w_down = nrm(ks[13], (DEPTH, FFN_HIDDEN, D_MODEL), FFN_HIDDEN ** -0.5 * DN_BETA)
    ln2_g = 1.0 + nrm(ks[14], (DEPTH, D_MODEL), 0.02)
    ln2_b = nrm(ks[15], (DEPTH, D_MODEL), 0.02)
    return {"x": x, "w_in": w_in, "conv_w": conv_w, "a_log": a_log,
            "dt_bias": dt_bias, "dn_norm_w": dn_norm_w, "sinks": sinks,
            "w_branch_a": w_branch_a, "w_branch_b": w_branch_b, "w_out": w_out,
            "ln1_g": ln1_g, "ln1_b": ln1_b, "w_gate_up": w_gate_up,
            "w_down": w_down, "ln2_g": ln2_g, "ln2_b": ln2_b}

def reference(x, w_in, conv_w, a_log, dt_bias, dn_norm_w, sinks, w_branch_a,
              w_branch_b, w_out, ln1_g, ln1_b, w_gate_up, w_down, ln2_g, ln2_b):
    cos, sin = rope_tables(x.shape[1])
    for l in range(DEPTH):
        mix = token_mixing(x, w_in[l], conv_w[l], a_log[l], dt_bias[l], dn_norm_w[l],
                           sinks[l], w_branch_a[l], w_branch_b[l], w_out[l], cos, sin)
        x = layer_norm(DN_ALPHA * x + mix, ln1_g[l], ln1_b[l])
        x = layer_norm(DN_ALPHA * x + swiglu_ffn(x, w_gate_up[l], w_down[l]), ln2_g[l], ln2_b[l])
    return x


_drawn_inputs = setup_inputs


def setup_inputs(seed=0):
    import zlib

    import numpy as np

    out = dict(_drawn_inputs(seed))
    spreads = {}
    factors = {'dn_norm_w': 8.0, 'sinks': 8.0}
    for name, (base, spread) in spreads.items():
        noise = np.random.default_rng([zlib.crc32(name.encode()), seed]).standard_normal(out[name].shape)
        drawn = base * np.exp(spread * noise) if base else spread * noise
        out[name] = jnp.asarray(drawn.astype(out[name].dtype))
    for name, factor in factors.items():
        out[name] = (out[name] * factor).astype(out[name].dtype)
    return out
```

```python
from contextlib import ExitStack

import numpy as np

import concourse.bass as bass
from concourse import mybir

F32 = mybir.dt.float32
F32R = mybir.dt.float32r
BF16 = mybir.dt.bfloat16
I32 = mybir.dt.int32
ALU = mybir.AluOpType
ACT = mybir.ActivationFunctionType
AX_X = mybir.AxisListType.X

P = 128
SEQ = 512
D = 1024
DEPTH = 2
CHUNKS = SEQ // P
KT = D // P
HEADS = 8
CONV = 5
GROUPS = 4
HD = 64
GQ = 4
SWC = 1536
FF = 2816
FT = FF // P
ALPHA = (2.0 * DEPTH) ** 0.25
LN_EPS = 1e-5
RMS_EPS = 1e-6
ATT_SCALE = HD ** -0.5
NEG_BIG = 1.0e30
LEVELS = (1, 2, 4, 8, 16, 32, 64)

U_QKV = 3 * HEADS
U_Z = HEADS
U_SW = SWC // 512 * (KT // 2)
U_MERGE = 4 * KT
U_OUT = KT
U_GU = 2 * FT
U_DOWN = FT
UNITS = U_QKV + U_Z + U_SW + U_MERGE + U_OUT + U_GU + U_DOWN
PAIRS = UNITS // 2
AT_QKV = 0
AT_Z = AT_QKV + U_QKV // 2
AT_SW = AT_Z + U_Z // 2
AT_MERGE = AT_SW + U_SW // 2
AT_OUT = AT_MERGE + U_MERGE // 2
AT_GU = AT_OUT + U_OUT // 2
AT_DOWN = AT_GU + U_GU // 2

C_ID = 0
C_TRIF = P
C_TRIB = 2 * P
C_ONES = 3 * P
C_LOW = 4 * P
C_UP = C_LOW + len(LEVELS) * P
C_COS = C_UP + len(LEVELS) * P
C_SIN = C_COS + CHUNKS * HD // 2
C_ALL = C_SIN + CHUNKS * HD // 2

T_G, T_CUM, T_EG, T_NEG_EG, T_BETA, T_NEG_BETA = range(6)

BARRIERS = 10
SMALL = 7


def trunk(nc, x_in, stream, w_ba, conv_w, a_log, dt_bias, dn_norm, sinks, ln_rows, consts, out):
    with ExitStack() as ctx:
        base = [nc.sbuf_base + (-nc.sbuf_base) % 64]

        def place(name, shape, dt, at=None):
            size = int(np.prod(shape[1:])) * (2 if dt == BF16 else 4)
            if at is None:
                at = base[0]
                base[0] += size + (-size) % 32
            return nc.alloc_sbuf_tensor_at(name, shape, dt, offset=at)

        def sem(name):
            return ctx.enter_context(nc.semaphore(name))

        PS = ctx.enter_context(nc.psum_tensor("PS", [P, 8, 512], F32))

        x = place("x", [P, CHUNKS, D], F32)
        xh = place("xh", [P, KT, SEQ], F32R)
        xl = place("xl", [P, KT, SEQ], F32R)
        w_raw = [place(f"w_raw{s}", [P, 1024], F32) for s in range(2)]
        wh = [place(f"wh{s}", [P, 1024], F32R) for s in range(2)]
        wl = [place(f"wl{s}", [P, 1024], F32R) for s in range(2)]
        cst = place("cst", [P, C_ALL], F32)
        id_bf = place("id_bf", [P, P], BF16)
        neg_bf = [place(f"neg_bf{r}", [P, P], BF16) for r in range(2)]
        cw = place("cw", [P, DEPTH * U_QKV, CONV], F32)
        dn_w = place("dn_w", [P, DEPTH], F32)
        exp_a = place("exp_a", [P, DEPTH * 16], F32)
        dtb = place("dtb", [P, DEPTH * 16], F32)
        snk = place("snk", [P, DEPTH * 16], F32)
        tab = place("tab", [P, HEADS, 6, 2, CHUNKS], F32)
        rn = place("rn", [P, 2 * HEADS, CHUNKS], F32)
        rno = place("rno", [P, HEADS, CHUNKS], F32)
        ln_st = place("ln_st", [P, CHUNKS, 12], F32)
        ln_mv = place("ln_mv", [P, CHUNKS, 2], F32)
        ln_rs = place("ln_rs", [P, CHUNKS, 1], F32)
        big = base[0]
        KB = 1024

        raw = place("raw", [P, U_QKV, CHUNKS, P], F32, big)
        o_dn = place("o_dn", [P, HEADS, CHUNKS, P], F32, big + 48 * KB)
        conv_in = [place(f"conv_in{s}", [P, SEQ + CONV - 1], F32, big + 64 * KB + s * 2112) for s in range(2)]
        conv_acc = [place(f"conv_acc{s}", [P, SEQ], F32, big + 69 * KB + s * 2 * KB) for s in range(2)]
        conv_act = [place(f"conv_act{s}", [P, SEQ], F32, big + 73 * KB + s * 2 * KB) for s in range(2)]
        sq = place("sq", [P, CHUNKS, P], F32, big + 77 * KB)
        ba_raw = place("ba_raw", [P, KT, 32], F32, big + 80 * KB)
        bah = place("bah", [P, KT, 32], F32R, big + 81 * KB)
        bal = place("bal", [P, KT, 32], F32R, big + 82 * KB)
        ba = place("ba", [P, CHUNKS, 32], F32, big + 83 * KB)
        sm = [place(f"sm{n}", [P, CHUNKS, 16], F32, big + 84 * KB + 256 * n) for n in range(10)]

        work = [big + 64 * KB]

        def head_buf(name, shape):
            t = place(name, shape, F32, work[0])
            work[0] += -(-int(np.prod(shape[1:])) * 4 // 32) * 32
            return t
        blk = [P, CHUNKS, P]
        qn, kn, qT, kT = (head_buf(n, blk) for n in ("qn", "kn", "qT", "kT"))
        DT = [head_buf(f"DT{r}", blk) for r in range(2)]
        NLT = [head_buf(f"NLT{r}", blk) for r in range(2)]
        QKT = [head_buf(f"QKT{r}", blk) for r in range(2)]
        X = [head_buf(f"X{r}", blk) for r in range(2)]
        Y = [head_buf(f"Y{r}", blk) for r in range(2)]
        W = [head_buf(f"W{r}", blk) for r in range(2)]
        OD = [head_buf(f"OD{r}", blk) for r in range(2)]
        S = [head_buf(f"S{r}", [P, P]) for r in range(2)]
        R = [head_buf(f"R{r}", [P, P]) for r in range(2)]
        VN = [head_buf(f"VN{r}", [P, P]) for r in range(2)]
        VS = [head_buf(f"VS{r}", [P, P]) for r in range(2)]
        O1 = [head_buf(f"O1{r}", [P, P]) for r in range(2)]
        ht = head_buf("ht", [P, 6, 2, CHUNKS])
        egl = [head_buf(f"egl{r}", [P, CHUNKS]) for r in range(2)]
        bdl = [head_buf(f"bdl{r}", [P, CHUNKS]) for r in range(2)]
        assert work[0] <= big + 112 * KB

        ozh = place("ozh", [P, KT, SEQ], F32R, big + 64 * KB)
        ozl = place("ozl", [P, KT, SEQ], F32R, big + 80 * KB)
        on = [place(f"on{s}", blk, F32, big + s * 2 * KB) for s in range(2)]
        zs = [place(f"zs{s}", [P, SEQ], F32, big + (4 + s * 2) * KB) for s in range(2)]
        oz = [place(f"oz{s}", [P, SEQ], F32, big + (8 + s * 2) * KB) for s in range(2)]

        o_sw = place("o_sw", [P, CHUNKS, D], F32, big)
        sw = place("sw", [P, CHUNKS, SWC], F32, big + 16 * KB)
        qg = place("qg", [P, CHUNKS, GQ, HD], F32, big + 40 * KB)
        kg = place("kg", [P, CHUNKS, 1, HD], F32, big + 44 * KB)
        r1 = place("r1", [P, CHUNKS, GQ, HD // 2], F32, big + 45 * KB)
        r2 = place("r2", [P, CHUNKS, GQ, HD // 2], F32, big + 47 * KB)
        qgT = place("qgT", [HD, GQ, SEQ], F32, big + 49 * KB)
        kgT = place("kgT", [HD, SEQ], F32, big + 57 * KB)
        mx = place("mx", [P, GQ], F32, big + 59 * KB)
        mn = place("mn", [P, GQ], F32, big + 59 * KB + 32)
        es = place("es", [P, GQ], F32, big + 59 * KB + 64)
        den = place("den", [P, GQ], F32, big + 59 * KB + 96)
        rd = place("rd", [P, GQ], F32, big + 59 * KB + 128)
        pr = place("pr", [P, GQ, 3 * P], F32, big + 96 * KB)
        pT = place("pT", [P, 3, 512], F32, big + 102 * KB)
        swh = place("swh", [P, KT, SEQ], F32R, big + 16 * KB)
        swl = place("swl", [P, KT, SEQ], F32R, big + 32 * KB)

        mgh = place("mgh", [P, KT, SEQ], F32R, big + 48 * KB)
        mgl = place("mgl", [P, KT, SEQ], F32R, big + 96 * KB)
        gA = [place(f"gA{s}", [P, SEQ], F32, big + 2 * s * KB) for s in range(2)]
        gB = [place(f"gB{s}", [P, SEQ], F32, big + (4 + 2 * s) * KB) for s in range(2)]
        mA = place("mA", [P, SEQ], F32, big + 8 * KB)
        mB = place("mB", [P, SEQ], F32, big + 10 * KB)
        mS = place("mS", [P, SEQ], F32, big + 12 * KB)

        yT_a = place("yT_a", [P, KT, SEQ], F32, big + 64 * KB)
        yT_b = place("yT_b", [P, KT, SEQ], F32, big)
        ln_g = place("ln_g", [P, D], F32, big + 88 * KB)
        ln_b = place("ln_b", [P, D], F32, big + 92 * KB)
        hh = place("hh", [P, FT, SEQ], F32R, big)
        hl = place("hl", [P, FT, SEQ], F32R, big + 44 * KB)
        sg = [place(f"sg{s}", [P, SEQ], F32, big + (96 + 2 * s) * KB) for s in range(2)]
        hf = [place(f"hf{s}", [P, SEQ], F32, big + (100 + 2 * s) * KB) for s in range(2)]
        assert big + 112 * KB <= nc.sbuf_usable_end, (big + 112 * KB, nc.sbuf_usable_end)

        ident = cst[:, C_ID:C_ID + P]
        ones = cst[:, C_ONES:C_ONES + P]
        tri = [cst[:, C_TRIF:C_TRIF + P], cst[:, C_TRIB:C_TRIB + P]]
        low = [cst[:, C_LOW + n * P:C_LOW + (n + 1) * P] for n in range(len(LEVELS))]
        up = [cst[:, C_UP + n * P:C_UP + (n + 1) * P] for n in range(len(LEVELS))]
        x_mask = [low, up]
        y_mask = [up, low]

        def rows(ap):
            return ap.unsqueeze(1).broadcast_to([P, CHUNKS, P])

        def cols(ap, n=P):
            return ap.unsqueeze(2).broadcast_to([P, ap.shape[1], n])

        small_loaded = sem("small_loaded")
        settled = sem("settled")
        loaded = [sem(f"loaded{s}") for s in range(2)]
        split_done = [sem(f"split_done{s}") for s in range(2)]
        unit_done = [sem(f"unit_done{s}") for s in range(2)]
        w_hi_done = [sem(f"w_hi_done{s}") for s in range(2)]
        gate_pre = sem("gate_pre")
        on_used = [sem(f"on_used{s}") for s in range(2)]
        stage_done = sem("stage_done")
        ready_bf = sem("ready_bf")
        x_t = sem("x_t")
        x_hi = sem("x_hi")
        x_lo = sem("x_lo")
        conv_loaded = [sem(f"conv_loaded{s}") for s in range(2)]
        conv_step = [sem(f"conv_step{s}") for s in range(2)]
        conv_silu = [sem(f"conv_silu{s}") for s in range(2)]
        tok_ready = [sem(f"tok_ready{s}") for s in range(2)]
        tok_stored = [sem(f"tok_stored{s}") for s in range(2)]
        sq_done = sem("sq_done")
        sumsq_done = sem("sumsq_done")
        ba_loaded = sem("ba_loaded")
        ba_hi = sem("ba_hi")
        ba_lo = sem("ba_lo")
        ba_mm = sem("ba_mm")
        cum_mm = sem("cum_mm")
        gate_dve = sem("gate_dve")
        gate_act = sem("gate_act")
        head_cols = sem("head_cols")
        qk_normed = sem("qk_normed")
        qk_turned = sem("qk_turned")
        qT_ready = sem("qT_ready")
        kT_ready = sem("kT_ready")
        g_tri = sem("g_tri")
        g_rows = sem("g_rows")
        g_diff = sem("g_diff")
        decay_done = sem("decay_done")
        kk_done = sem("kk_done")
        kq_done = sem("kq_done")
        beta_decay = sem("beta_decay")
        bdl_done = sem("bdl_done")
        nlt_done = sem("nlt_done")
        qkt_done = sem("qkt_done")
        nl_done = sem("nl_done")
        x_ident = sem("x_ident")
        y_ident = sem("y_ident")
        x_upd = [sem(f"x_upd{r}") for r in range(2)]
        y_upd = [sem(f"y_upd{r}") for r in range(2)]
        w_mm = [sem(f"w_mm{r}") for r in range(2)]
        w_ready = [sem(f"w_ready{r}") for r in range(2)]
        p_mm = [sem(f"p_mm{r}") for r in range(2)]
        q_mm = [sem(f"q_mm{r}") for r in range(2)]
        ks_mm = [sem(f"ks_mm{r}") for r in range(2)]
        r_ready = [sem(f"r_ready{r}") for r in range(2)]
        tr_mm = [sem(f"tr_mm{r}") for r in range(2)]
        o1_ready = [sem(f"o1_ready{r}") for r in range(2)]
        vn_ready = [sem(f"vn_ready{r}") for r in range(2)]
        vs_ready = [sem(f"vs_ready{r}") for r in range(2)]
        o_mm = [sem(f"o_mm{r}") for r in range(2)]
        st_mm = [sem(f"st_mm{r}") for r in range(2)]
        o_out = [sem(f"o_out{r}") for r in range(2)]
        s_ready = [sem(f"s_ready{r}") for r in range(2)]
        o_sum = sem("o_sum")
        o_sq = sem("o_sq")
        o_ss = sem("o_ss")
        rno_dve = sem("rno_dve")
        rno_act = sem("rno_act")
        on_ready = [sem(f"on_ready{s}") for s in range(2)]
        on_turned = [sem(f"on_turned{s}") for s in range(2)]
        z_silu = [sem(f"z_silu{s}") for s in range(2)]
        oz_ready = [sem(f"oz_ready{s}") for s in range(2)]
        oz_hi = [sem(f"oz_hi{s}") for s in range(2)]
        oz_lo = [sem(f"oz_lo{s}") for s in range(2)]
        sw_mm = sem("sw_mm")
        sw_act = sem("sw_act")
        sw_dve = sem("sw_dve")
        rope_mul = sem("rope_mul")
        rope_half = sem("rope_half")
        qg_turned = sem("qg_turned")
        qgT_act = sem("qgT_act")
        qgT_dve = sem("qgT_dve")
        scores = sem("scores")
        max_raw = sem("max_raw")
        max_sink = sem("max_sink")
        max_neg = sem("max_neg")
        sink_off = sem("sink_off")
        probs = sem("probs")
        sink_exp = sem("sink_exp")
        den_sum = sem("den_sum")
        den_inv = sem("den_inv")
        p_turned = sem("p_turned")
        pT_act = sem("pT_act")
        pT_dve = sem("pT_dve")
        pv_mm = sem("pv_mm")
        o_scaled = sem("o_scaled")
        osw_t = sem("osw_t")
        osw_hi = sem("osw_hi")
        osw_lo = sem("osw_lo")
        gate_sig = sem("gate_sig")
        mg_mul = sem("mg_mul")
        mg_sum = sem("mg_sum")
        mg_hi = sem("mg_hi")
        mg_lo = sem("mg_lo")
        ln_loaded = sem("ln_loaded")
        y_mm = sem("y_mm")
        yT_act = sem("yT_act")
        yT_dve = sem("yT_dve")
        y_turned = sem("y_turned")
        res_done = sem("res_done")
        ln_stat = sem("ln_stat")
        ln_aggr = sem("ln_aggr")
        ln_eps = sem("ln_eps")
        ln_sqrt = sem("ln_sqrt")
        ln_inv = sem("ln_inv")
        ln_norm = sem("ln_norm")
        ln_gain = sem("ln_gain")
        ln_out = sem("ln_out")
        ff_silu = sem("ff_silu")
        ff_h = sem("ff_h")
        ff_hi = sem("ff_hi")
        ff_lo = sem("ff_lo")
        stored = sem("stored")

        def settle(eng):
            eng.sem_inc(settled, 1)

        def stage_end(eng, l, n):
            settle(eng)
            eng.drain().then_inc(stage_done, 1)
            eng.wait_ge(stage_done, (l * BARRIERS + n) * 3 + 3)
            settle(eng)

        block = ctx.enter_context(nc.Block())

        @block.sync
        def _(sp):
            for dst, src in ((x[:], x_in), (cst[:], consts), (cw[:], conv_w), (dn_w[:], dn_norm),
                             (exp_a[:], a_log.partition_broadcast(P)), (dtb[:], dt_bias.partition_broadcast(P)),
                             (snk[:], sinks.partition_broadcast(P))):
                sp.dma_start(dst, src).then_inc(small_loaded, 16)
            with sp.Fori(0, DEPTH * PAIRS) as p:
                for s in range(2):
                    sp.wait_ge(split_done[s], p + 1)
                    sp.dma_start(w_raw[s][:], stream[p, s, :, :]).then_inc(loaded[s], 16)
            sp.wait_ge(stage_done, DEPTH * BARRIERS * 3)
            sp.dma_start(out, x[:]).then_inc(stored, 16)
            sp.wait_ge(stored, 16)

        @block.gpsimd
        def _(pool):
            for s in range(2):
                pool.sem_inc(split_done[s], 1)
            with pool.Fori(0, DEPTH * PAIRS) as p:
                for s in range(2):
                    pool.wait_ge(loaded[s], p * 16 + 16)
                    pool.wait_ge(unit_done[s], p + 1)
                    settle(pool)
                    nc.gpsimd.tensor_copy(wh[s][:], w_raw[s][:]).then_inc(w_hi_done[s], 1)
                    pool.wait_ge(w_hi_done[s], p + 1)
                    nc.gpsimd.tensor_tensor(wl[s][:], w_raw[s][:], wh[s][:].bitcast(F32),
                                            ALU.subtract).then_inc(split_done[s], 1)

        @block.tensor
        def _(pe):
            mm = nc.tensor.matmul

            def unit_ready(pair, s):
                pe.wait_ge(split_done[s], pair + 2)

            def product(o, ah, al, bh, bl, first, last):
                mm(o, ah, bh, start=first, stop=False)
                mm(o, al, bh, start=False, stop=False)
                return mm(o, ah, bl, start=False, stop=last)

            def feature_unit(s, bank, bh, bl):
                for k in range(KT):
                    c = slice(k * P, (k + 1) * P)
                    ins = product(PS[:, bank, :], wh[s][:, c], wl[s][:, c], bh[:, k, :], bl[:, k, :],
                                  k == 0, k == KT - 1)
                ins.then_inc(unit_done[s], 1)

            def turn_to_features(l_count, src, turned, lo_done):
                for k in range(KT):
                    for c in range(CHUNKS):
                        ins = nc.tensor.transpose(PS[:, k, c * P:(c + 1) * P], src[:, c, k * P:(k + 1) * P], ident)
                    ins.then_inc(turned, 1)

            def down_units(l, first_pair, npairs, bh, bl):
                def pair_of(i, first, last):
                    for s in range(2):
                        unit_ready(l * PAIRS + first_pair + i, s)
                        k = i * 2 + s
                        for d in range(KT):
                            c = slice(d * P, (d + 1) * P)
                            ins = product(PS[:, d, :], wh[s][:, c], wl[s][:, c],
                                          bh[:, bass.ds(k, 1), :].rearrange("p a t -> p (a t)"),
                                          bl[:, bass.ds(k, 1), :].rearrange("p a t -> p (a t)"),
                                          first and s == 0, last and s == 1)
                        ins.then_inc(unit_done[s], 1)
                pair_of(0, True, False)
                with pe.Fori(1, npairs - 1) as i:
                    pair_of(i, False, False)
                pair_of(npairs - 1, False, True)

            def turn_back(l, src, n):
                pe.wait_ge(yT_act, (l * 2 + n) * 4 + 4)
                pe.wait_ge(yT_dve, (l * 2 + n) * 4 + 4)
                for c in range(CHUNKS):
                    for half in range(2):
                        for j in range(4):
                            ins = nc.tensor.transpose(PS[:, c * 2 + half, j * P:(j + 1) * P],
                                                      src[:, half * 4 + j, c * P:(c + 1) * P], ident)
                    ins.then_inc(y_turned, 1)

            pe.sem_inc(unit_done[0], 1)
            pe.sem_inc(unit_done[1], 1)
            pe.wait_ge(small_loaded, 16 * SMALL)
            pe.wait_ge(ready_bf, 5)
            with pe.Fori(0, DEPTH) as l:
                turn_to_features(l, x, x_t, None)
                stage_end(pe, l, 0)

                def qkv_unit(i, s):
                    unit_ready(l * PAIRS + AT_QKV + i, s)
                    feature_unit(s, s, xh, xl)

                def qkv_turn(i, s):
                    pe.wait_ge(conv_silu[s], l * 12 + i + 1)
                    for c in range(CHUNKS):
                        ins = nc.tensor.transpose(PS[:, 2 + s, c * P:(c + 1) * P],
                                                  conv_act[s][:, c * P:(c + 1) * P], ident)
                    ins.then_inc(tok_ready[s], 1)
                qkv_unit(0, 0)
                with pe.Fori(0, U_QKV // 2 - 1) as i:
                    qkv_unit(i, 1)
                    qkv_turn(i, 0)
                    qkv_unit(i + 1, 0)
                    qkv_turn(i, 1)
                last = U_QKV // 2 - 1
                qkv_unit(last, 1)
                qkv_turn(last, 0)
                qkv_turn(last, 1)

                pe.wait_ge(ba_lo, l + 1)
                for c in range(CHUNKS):
                    t = slice(c * P, (c + 1) * P)
                    for k in range(KT):
                        ins = product(PS[:, 4, c * 32:(c + 1) * 32], xh[:, k, t], xl[:, k, t],
                                      bah[:, k, :], bal[:, k, :], k == 0, k == KT - 1)
                ins.then_inc(ba_mm, 1)
                pe.wait_ge(gate_dve, l * 19 + 13)
                for r in range(2):
                    ins = mm(PS[:, 5, r * 32:(r + 1) * 32].rearrange("p (c h) -> p c h", c=CHUNKS), tri[r],
                             sm[8][:, :, r * 8:(r + 1) * 8], start=True, stop=True)
                ins.then_inc(cum_mm, 1)
                stage_end(pe, l, 1)

                with pe.Fori(0, HEADS) as h:
                    n = l * HEADS + h
                    pe.wait_ge(qk_normed, n * 2 + 1)
                    for c in range(CHUNKS):
                        ins = nc.tensor.transpose(PS[:, 0, c * P:(c + 1) * P], qn[:, c, :], ident)
                    ins.then_inc(qk_turned, 1)
                    pe.wait_ge(qk_normed, n * 2 + 2)
                    for c in range(CHUNKS):
                        ins = nc.tensor.transpose(PS[:, 1, c * P:(c + 1) * P], kn[:, c, :], ident)
                    ins.then_inc(qk_turned, 1)
                    for r in range(2):
                        pe.wait_ge(g_tri, n * 2 + r + 1)
                        mm(PS[:, 2 + r, :], ones, W[r][:].rearrange("p c t -> p (c t)"), start=True, stop=False)
                        mm(PS[:, 2 + r, :].rearrange("p (c t) -> p c t", c=CHUNKS), id_bf[:], rows(neg_bf[r][:]),
                           start=False, stop=True).then_inc(g_rows, 1)
                    pe.wait_ge(kT_ready, n + 1)
                    for c in range(CHUNKS):
                        ins = mm(PS[:, 4, c * P:(c + 1) * P], kT[:, c, :], kT[:, c, :], start=True, stop=True)
                    ins.then_inc(kk_done, 1)
                    pe.wait_ge(qT_ready, n + 1)
                    for c in range(CHUNKS):
                        ins = mm(PS[:, 5, c * P:(c + 1) * P], kT[:, c, :], qT[:, c, :], start=True, stop=True)
                    ins.then_inc(kq_done, 1)
                    for r in range(2):
                        pe.wait_ge(nlt_done, n * 2 + r + 1)
                        for c in range(CHUNKS):
                            ins = nc.tensor.transpose(PS[:, 2 + r, c * P:(c + 1) * P], NLT[r][:, c, :], ident)
                        ins.then_inc(nl_done, 1)
                    for lev in range(1, 7):
                        for r in range(2):
                            pe.wait_ge(x_upd[r], n * 6 + lev)
                            if lev == 1:
                                pe.wait_ge(x_upd[1], n * 6 + 1)
                                pe.wait_ge(qkt_done, n * 2 + 2)
                            for c in range(CHUNKS):
                                ins = mm(PS[:, 3 * r, c * P:(c + 1) * P], NLT[r][:, c, :], X[r][:, c, :],
                                         start=True, stop=True)
                            ins.then_inc(w_mm[r], 1)
                        for r in range(2):
                            pe.wait_ge(w_ready[r], n * 6 + lev)
                            pe.wait_ge(y_upd[r], n * 7 + lev)
                            if lev < 6:
                                for c in range(CHUNKS):
                                    ins = mm(PS[:, 3 * r + 1, c * P:(c + 1) * P], Y[r][:, c, :], W[r][:, c, :],
                                             start=True, stop=True)
                                ins.then_inc(p_mm[r], 1)
                            for c in range(CHUNKS):
                                ins = mm(PS[:, 3 * r + 2, c * P:(c + 1) * P], W[r][:, c, :], Y[r][:, c, :],
                                         start=True, stop=True)
                            ins.then_inc(q_mm[r], 1)
                    for step in range(CHUNKS):
                        for r in range(2):
                            c = step if r == 0 else CHUNKS - 1 - step
                            if step == 0:
                                pe.wait_ge(y_upd[0], n * 7 + 7)
                                pe.wait_ge(y_upd[1], n * 7 + 7)
                            else:
                                pe.wait_ge(s_ready[r], n * 3 + step)
                                mm(PS[:, r, 0:P], kT[:, c, :], S[r][:], start=True, stop=True).then_inc(ks_mm[r], 1)
                                mm(PS[:, 2 + r, 0:P], qT[:, c, :], S[r][:], start=True, stop=True)
                        for r in range(2):
                            c = step if r == 0 else CHUNKS - 1 - step
                            pe.wait_ge(r_ready[r], n * 4 + step + 1)
                            mm(PS[:, 4 + r, 0:P], Y[r][:, c, :], R[r][:], start=True, stop=True).then_inc(tr_mm[r], 1)
                        for r in range(2):
                            c = step if r == 0 else CHUNKS - 1 - step
                            pe.wait_ge(vn_ready[r], n * 4 + step + 1)
                            if step == 0:
                                pe.wait_ge(qkt_done, n * 2 + r + 1)
                            mm(PS[:, 6 + r, 0:P], QKT[r][:, c, :], VN[r][:], start=True, stop=True).then_inc(o_mm[r], 1)
                            if step < CHUNKS - 1:
                                pe.wait_ge(vs_ready[r], n * 3 + step + 1)
                                mm(PS[:, 6 + r, P:2 * P], kn[:, c, :], VS[r][:], start=True,
                                   stop=True).then_inc(st_mm[r], 1)
                    for r in range(2):
                        pe.wait_ge(o_out[r], n * 4 + 4)
                stage_end(pe, l, 2)

                with pe.Fori(0, HEADS // 2) as i:
                    for s in range(2):
                        unit_ready(l * PAIRS + AT_Z + i, s)
                        pe.wait_ge(oz_ready[s], l * 4 + i + 1)
                        feature_unit(s, s, xh, xl)
                        pe.wait_ge(on_ready[s], l * 4 + i + 1)
                        for c in range(CHUNKS):
                            ins = nc.tensor.transpose(PS[:, 2 + s, c * P:(c + 1) * P], on[s][:, c, :], ident)
                        ins.then_inc(on_turned[s], 1)
                stage_end(pe, l, 3)

                with pe.Fori(0, SWC // 512) as b:
                    pe.wait_ge(sw_act, (l * 3 + b) * 2 + 1)
                    pe.wait_ge(sw_dve, (l * 3 + b) * 2 + 1)
                    for u in range(KT // 2):
                        s = u % 2
                        unit_ready(l * PAIRS + AT_SW + b * 2 + u // 2, s)
                        for j in range(2):
                            k = u * 2 + j
                            for c in range(CHUNKS):
                                t = slice(c * P, (c + 1) * P)
                                w = slice(j * 512, (j + 1) * 512)
                                ins = product(PS[:, c, :], xh[:, k, t], xl[:, k, t], wh[s][:, w], wl[s][:, w],
                                              k == 0, k == KT - 1)
                        ins.then_inc(unit_done[s], 1)
                stage_end(pe, l, 4)

                with pe.Fori(0, GROUPS) as g:
                    n = l * GROUPS + g
                    pe.wait_ge(rope_half, n * 4 + 4)
                    settle(pe)
                    for q in range(GQ):
                        for c in range(CHUNKS):
                            ins = nc.tensor.transpose(PS[0:HD, q, c * P:(c + 1) * P], qg[:, c, q, :], ident)
                        ins.then_inc(qg_turned, 1)
                    for c in range(CHUNKS):
                        ins = nc.tensor.transpose(PS[0:HD, 4, c * P:(c + 1) * P], kg[:, c, 0, :], ident)
                    ins.then_inc(qg_turned, 1)

                    def score(b):
                        lo, hi = max(b - 1, 0), min(b + 2, CHUNKS)
                        width = (hi - lo) * P
                        if b == 0:
                            pe.wait_ge(qgT_act, n * 2 + 2)
                            pe.wait_ge(qgT_dve, n * 3 + 3)
                        else:
                            pe.wait_ge(probs, n * 16 + b * 4)
                        for q in range(GQ):
                            mm(PS[:, q, 0:width], qgT[:, q, b * P:(b + 1) * P], kgT[:, lo * P:hi * P],
                               start=True, stop=False)
                            if b > 0:
                                ins = mm(PS[:, q, 0:P], id_bf[:], neg_bf[0][:], start=False, stop=b == CHUNKS - 1)
                            if b < CHUNKS - 1:
                                ins = mm(PS[:, q, width - P:width], id_bf[:], neg_bf[1][:], start=False, stop=True)
                        ins.then_inc(scores, 1)
                    score(0)
                    for b in range(CHUNKS):
                        lo, hi = max(b - 1, 0), min(b + 2, CHUNKS)
                        pe.wait_ge(probs, n * 16 + b * 4 + 4)
                        for j in range(hi - lo):
                            for q in range(GQ):
                                ins = nc.tensor.transpose(PS[:, 4 + j, q * P:(q + 1) * P],
                                                          pr[:, q, j * P:(j + 1) * P], ident)
                        ins.then_inc(p_turned, 1)
                        if b < CHUNKS - 1:
                            score(b + 1)
                        pe.wait_ge(pT_act, n * 4 + b + 1)
                        pe.wait_ge(pT_dve, n * 4 + b + 1)
                        if b > 0:
                            pe.wait_ge(o_scaled, n * 4 + b)
                        for q in range(GQ):
                            for j in range(hi - lo):
                                v = sw[:, lo + j, bass.ds(1280 + g * HD, HD)]
                                ins = mm(PS[:, 7, q * HD:(q + 1) * HD], pT[:, j, q * P:(q + 1) * P], v,
                                         start=j == 0, stop=j == hi - lo - 1)
                        ins.then_inc(pv_mm, 1)
                    pe.wait_ge(o_scaled, n * 4 + 4)
                turn_to_features(l, o_sw, osw_t, None)
                stage_end(pe, l, 5)

                with pe.Fori(0, KT // 2) as i:
                    for j in range(2):
                        if j == 0:
                            pe.wait_ge(mg_mul, (l * 4 + i) * 4 + 2)
                        else:
                            pe.wait_ge(mg_mul, (l * 4 + i) * 4 + 4)
                        for half, (b_hi, b_lo) in enumerate(((ozh, ozl), (swh, swl))):
                            pair = l * PAIRS + AT_MERGE + i * 4 + j * 2 + half
                            unit_ready(pair, 0)
                            feature_unit(0, 4 * j + 2 * half, xh, xl)
                            unit_ready(pair, 1)
                            feature_unit(1, 4 * j + 2 * half + 1, b_hi, b_lo)
                stage_end(pe, l, 6)

                down_units(l, AT_OUT, U_OUT // 2, mgh, mgl)
                pe.drain().then_inc(y_mm, 1)
                turn_back(l, yT_a, 0)
                stage_end(pe, l, 7)

                turn_to_features(l, x, x_t, None)
                stage_end(pe, l, 8)

                with pe.Fori(0, FT // 2) as i:
                    for j in range(2):
                        pair = l * PAIRS + AT_GU + i * 2 + j
                        pe.wait_ge(ff_h, (l * 11 + i) * 2 + j + 1)
                        for s in range(2):
                            unit_ready(pair, s)
                            feature_unit(s, 2 * j + s, xh, xl)
                pe.wait_ge(ff_lo, (l + 1) * FT)
                settle(pe)
                down_units(l, AT_DOWN, U_DOWN // 2, hh, hl)
                pe.drain().then_inc(y_mm, 1)
                turn_back(l, yT_b, 1)
                stage_end(pe, l, 9)

        @block.scalar
        def _(act):
            A = nc.scalar.activation

            def unit_full(pair, s):
                act.wait_ge(unit_done[s], pair + 2)

            def store_hi(turned, base_count, hi, done):
                for k in range(KT):
                    act.wait_ge(turned, base_count + k + 1)
                    A(hi[:, k, :], PS[:, k, :], ACT.Copy).then_inc(done, 1)

            act.wait_ge(small_loaded, 16 * SMALL)
            A(exp_a[:], exp_a[:], ACT.Exp).then_inc(ready_bf, 1)
            act.sem_inc(sw_act, 1)
            with act.Fori(0, DEPTH) as l:
                act.dma_start(ba_raw[:], w_ba[l, :, :, :]).then_inc(ba_loaded, 16)
                store_hi(x_t, l * 16, xh, x_hi)
                stage_end(act, l, 0)

                with act.Fori(0, U_QKV // 2) as i:
                    n = l * 12 + i
                    for s in range(2):
                        unit_full(l * PAIRS + AT_QKV + i, s)
                        A(conv_in[s][:, 2:2 + SEQ], PS[:, s, :], ACT.Copy).then_inc(conv_loaded[s], 1)
                        act.wait_ge(conv_step[s], n * 5 + 5)
                        A(conv_act[s][:], conv_acc[s][:], ACT.Silu).then_inc(conv_silu[s], 1)
                        act.wait_ge(tok_ready[s], n + 1)
                        A(raw[:, bass.ds(i * 2 + s, 1), :, :].rearrange("p a c t -> p (a c t)"), PS[:, 2 + s, :],
                          ACT.Copy).then_inc(tok_stored[s], 1)
                act.wait_ge(gate_dve, l * 19 + 1)
                A(rn[:], rn[:], ACT.Sqrt).then_inc(gate_act, 1)
                act.wait_ge(gate_dve, l * 19 + 7)
                A(sm[3][:], sm[2][:], ACT.Exp).then_inc(gate_act, 1)
                act.wait_ge(gate_dve, l * 19 + 8)
                A(sm[5][:], sm[4][:], ACT.Ln).then_inc(gate_act, 1)
                A(sm[9][:], ba[:, :, 0:16], ACT.Sigmoid).then_inc(gate_act, 1)
                act.wait_ge(gate_dve, l * 19 + 16)
                A(tab[:, :, T_EG].rearrange("p h r c -> p h (r c)"),
                  tab[:, :, T_CUM].rearrange("p h r c -> p h (r c)"), ACT.Exp).then_inc(gate_act, 1)
                stage_end(act, l, 1)

                with act.Fori(0, HEADS) as h:
                    n = l * HEADS + h
                    act.wait_ge(qk_turned, n * 2 + 1)
                    A(qT[:].rearrange("p c t -> p (c t)"), PS[:, 0, :], ACT.Copy).then_inc(qT_ready, 1)
                    for r in range(2):
                        edge = P - 1 if r == 0 else 0
                        act.wait_ge(g_diff, n * 2 + r + 1)
                        A(egl[r][:], PS[:, 2 + r, :].rearrange("p (c t) -> p c t", c=CHUNKS)[:, :, edge], ACT.Exp)
                        A(DT[r][:], DT[r][:], ACT.Exp).then_inc(decay_done, 1)
                    for lev in range(1, 7):
                        for r in range(2):
                            act.wait_ge(w_mm[r], n * 6 + lev)
                            A(W[r][:].rearrange("p c t -> p (c t)"), PS[:, 3 * r, :], ACT.Copy).then_inc(w_ready[r], 1)
                    for step in range(CHUNKS):
                        if step > 0:
                            for r in range(2):
                                c = step if r == 0 else CHUNKS - 1 - step
                                act.wait_ge(tr_mm[r], n * 4 + step + 1)
                                A(O1[r][:], PS[:, 2 + r, 0:P], ACT.Copy,
                                  scale=ht[:, T_EG, r, c:c + 1]).then_inc(o1_ready[r], 1)
                        for r in range(2):
                            c = step if r == 0 else CHUNKS - 1 - step
                            act.wait_ge(tr_mm[r], n * 4 + step + 1)
                            if step == 0:
                                act.wait_ge(bdl_done, n * 2 + r + 1)
                            A(VN[r][:], PS[:, 4 + r, 0:P], ACT.Copy,
                              scale=ht[:, T_BETA, r, c:c + 1]).then_inc(vn_ready[r], 1)
                            if step < CHUNKS - 1:
                                A(VS[r][:], PS[:, 4 + r, 0:P], ACT.Copy,
                                  scale=bdl[r][:, c:c + 1]).then_inc(vs_ready[r], 1)
                act.wait_ge(rno_dve, l * 3 + 1)
                A(rno[:], rno[:], ACT.Sqrt).then_inc(rno_act, 1)
                stage_end(act, l, 2)

                with act.Fori(0, HEADS // 2) as i:
                    for s in range(2):
                        n = l * 4 + i
                        unit_full(l * PAIRS + AT_Z + i, s)
                        A(zs[s][:], PS[:, s, :], ACT.Silu).then_inc(z_silu[s], 1)
                        act.wait_ge(oz_ready[s], n + 2)
                        A(ozh[:, bass.ds(i * 2 + s, 1), :].rearrange("p a t -> p (a t)"), oz[s][:],
                          ACT.Copy).then_inc(oz_hi[s], 1)
                stage_end(act, l, 3)

                with act.Fori(0, SWC // 512) as b:
                    unit_full(l * PAIRS + AT_SW + b * 2 + 1, 1)
                    for c in (0, 1):
                        A(sw[:, c, bass.ds(b * 512, 512)], PS[:, c, :], ACT.Copy).then_inc(sw_act, 1)
                stage_end(act, l, 4)
                with act.Fori(0, GROUPS) as g:
                    n = l * GROUPS + g
                    for q in (0, 1):
                        act.wait_ge(qg_turned, n * 5 + q + 1)
                        A(qgT[:, q, :], PS[0:HD, q, :], ACT.Copy).then_inc(qgT_act, 1)
                    for b in range(CHUNKS):
                        lo, hi = max(b - 1, 0), min(b + 2, CHUNKS)
                        width = (hi - lo) * P
                        act.wait_ge(max_neg, n * 4 + b + 1)
                        if b > 0:
                            act.wait_ge(p_turned, n * 4 + b)
                            act.wait_ge(den_sum, n * 4 + b)
                        for q in range(GQ):
                            A(pr[:, q, 0:width], PS[:, q, 0:width], ACT.Exp, bias=mn[:, q:q + 1], scale=ATT_SCALE,
                              accum_out=den[:, q:q + 1]).then_inc(probs, 1)
                        act.wait_ge(sink_off, n * 4 + b + 1)
                        A(es[:], es[:], ACT.Exp).then_inc(sink_exp, 1)
                        act.wait_ge(p_turned, n * 4 + b + 1)
                        A(pT[:, 0, :], PS[:, 4, :], ACT.Copy).then_inc(pT_act, 1)
                store_hi(osw_t, l * 8, swh, osw_hi)
                stage_end(act, l, 5)

                with act.Fori(0, KT // 2) as i:
                    for j in range(2):
                        n = (l * 4 + i) * 2 + j
                        pair = l * PAIRS + AT_MERGE + i * 4 + j * 2
                        act.wait_ge(mg_sum, n + 1)
                        unit_full(pair, 0)
                        A(gA[j][:], PS[:, 4 * j, :], ACT.Sigmoid).then_inc(gate_sig, 1)
                        unit_full(pair + 1, 0)
                        A(gB[j][:], PS[:, 4 * j + 2, :], ACT.Sigmoid).then_inc(gate_sig, 1)
                stage_end(act, l, 6)

                act.dma_start(ln_g[:], ln_rows[l, 0, :].partition_broadcast(P)).then_inc(ln_loaded, 16)
                act.dma_start(ln_b[:], ln_rows[l, 1, :].partition_broadcast(P)).then_inc(ln_loaded, 16)

                def store_yT(n, dst):
                    act.wait_ge(y_mm, l * 2 + n + 1)
                    for k in range(0, KT, 2):
                        A(dst[:, k, :], PS[:, k, :], ACT.Copy).then_inc(yT_act, 1)

                def norm_sqrt(n):
                    act.wait_ge(ln_eps, l * 2 + n + 1)
                    A(ln_rs[:], ln_rs[:], ACT.Sqrt).then_inc(ln_sqrt, 1)
                store_yT(0, yT_a)
                norm_sqrt(0)
                stage_end(act, l, 7)
                store_hi(x_t, l * 16 + 8, xh, x_hi)
                stage_end(act, l, 8)

                with act.Fori(0, FT // 2) as i:
                    for j in range(2):
                        n = (l * 11 + i) * 2 + j
                        unit_full(l * PAIRS + AT_GU + i * 2 + j, 0)
                        A(sg[j][:], PS[:, 2 * j, :], ACT.Silu).then_inc(ff_silu, 1)
                        act.wait_ge(ff_h, n + 3)
                        A(hh[:, bass.ds(i * 2 + j, 1), :].rearrange("p a t -> p (a t)"), hf[j][:],
                          ACT.Copy).then_inc(ff_hi, 1)
                act.wait_ge(ff_lo, (l + 1) * FT)
                act.dma_start(ln_g[:], ln_rows[l, 2, :].partition_broadcast(P)).then_inc(ln_loaded, 16)
                act.dma_start(ln_b[:], ln_rows[l, 3, :].partition_broadcast(P)).then_inc(ln_loaded, 16)
                store_yT(1, yT_b)
                norm_sqrt(1)
                stage_end(act, l, 9)

        @block.vector
        def _(dve):
            TT = nc.vector.tensor_tensor
            TS = nc.vector.tensor_scalar
            STT = nc.vector.scalar_tensor_tensor

            def store_lo(hi_done, base_count, hi, lo, done):
                for k in range(KT):
                    dve.wait_ge(hi_done, base_count + k + 1)
                    TT(lo[:, k, :], PS[:, k, :], hi[:, k, :].bitcast(F32), ALU.subtract).then_inc(done, 1)

            dve.wait_ge(small_loaded, 16 * SMALL)
            nc.vector.tensor_copy(id_bf[:], ident).then_inc(ready_bf, 1)
            for r in range(2):
                TS(neg_bf[r][:], tri[r], 1.0, NEG_BIG, ALU.subtract, ALU.mult).then_inc(ready_bf, 1)
            nc.vector.memset(ln_rs[:], 0.0).then_inc(ready_bf, 1)
            dve.sem_inc(sw_dve, 1)
            for s in range(2):
                dve.sem_inc(oz_ready[s], 1)
                dve.sem_inc(on_used[s], 1)
                dve.sem_inc(mg_mul, 2)
                dve.sem_inc(ff_h, 1)
            dve.sem_inc(mg_sum, 2)
            dve.sem_inc(sumsq_done, 1)
            dve.wait_ge(ready_bf, 5)
            with dve.Fori(0, DEPTH) as l:
                store_lo(x_hi, l * 16, xh, xl, x_lo)
                for s in range(2):
                    nc.vector.memset(conv_in[s][:, 0:2], 0.0)
                    nc.vector.memset(conv_in[s][:, SEQ + 2:SEQ + 4], 0.0)
                dve.wait_ge(ba_loaded, l * 16 + 16)
                nc.vector.tensor_copy(bah[:], ba_raw[:]).then_inc(ba_hi, 1)
                dve.wait_ge(ba_hi, l + 1)
                TT(bal[:], ba_raw[:], bah[:].bitcast(F32), ALU.subtract).then_inc(ba_lo, 1)
                stage_end(dve, l, 0)

                with dve.Fori(0, U_QKV // 2) as i:
                    n = l * 12 + i
                    for s in range(2):
                        tile = l * U_QKV + i * 2 + s
                        dve.wait_ge(conv_loaded[s], n + 1)
                        for j in range(CONV):
                            w = cw[:, bass.ds(tile, 1), j:j + 1].rearrange("p a b -> p (a b)")
                            if j == 0:
                                TS(conv_acc[s][:], conv_in[s][:, 0:SEQ], w, None, ALU.mult).then_inc(conv_step[s], 1)
                            else:
                                dve.wait_ge(conv_step[s], n * 5 + j)
                                STT(conv_acc[s][:], conv_in[s][:, j:j + SEQ], w, conv_acc[s][:], ALU.mult,
                                    ALU.add).then_inc(conv_step[s], 1)
                for s in range(2):
                    dve.wait_ge(tok_stored[s], l * 12 + 12)
                settle(dve)
                with dve.Fori(0, 2 * HEADS) as u:
                    t = raw[:, bass.ds(u, 1), :, :].rearrange("p a c t -> p (a c) t")
                    dve.wait_ge(sumsq_done, l * 16 + u + 1)
                    TT(sq[:], t, t, ALU.mult).then_inc(sq_done, 1)
                    dve.wait_ge(sq_done, l * 16 + u + 1)
                    nc.vector.tensor_reduce(rn[:, bass.ds(u, 1), :].rearrange("p a c -> p (a c)"), sq[:], AX_X,
                                            ALU.add).then_inc(sumsq_done, 1)
                dve.wait_ge(sumsq_done, l * 16 + 17)

                g0 = l * 19

                def link(ins, n):
                    ins.then_inc(gate_dve, 1)
                    dve.wait_ge(gate_dve, g0 + n)
                link(TS(rn[:], rn[:], RMS_EPS, None, ALU.add), 1)
                dve.wait_ge(gate_act, l * 5 + 1)
                link(nc.vector.reciprocal(rn[:], rn[:]), 2)
                link(TS(rn[:, 0:HEADS, :], rn[:, 0:HEADS, :], float(P) ** -0.5, None, ALU.mult), 3)
                dve.wait_ge(ba_mm, l + 1)
                link(nc.vector.tensor_copy(ba[:].rearrange("p c n -> p (c n)"), PS[:, 4, 0:128]), 4)
                bias = dtb[:, bass.ds(l * 16, 16)].unsqueeze(1).broadcast_to([P, CHUNKS, 16])
                ea = exp_a[:, bass.ds(l * 16, 16)].unsqueeze(1).broadcast_to([P, CHUNKS, 16])
                link(TT(sm[0][:], ba[:, :, 16:32], bias, ALU.add), 5)
                link(TS(sm[1][:], sm[0][:], -1.0, None, ALU.mult), 6)
                link(TT(sm[2][:], sm[0][:], sm[1][:], ALU.min), 7)
                dve.wait_ge(gate_act, l * 5 + 2)
                link(TS(sm[4][:], sm[3][:], 1.0, None, ALU.add), 8)
                link(STT(sm[6][:], sm[4][:], 1.0, sm[3][:], ALU.subtract, ALU.subtract), 9)
                dve.wait_ge(gate_act, l * 5 + 3)
                link(nc.vector.reciprocal(sm[7][:], sm[4][:]), 10)
                link(TT(sm[7][:], sm[6][:], sm[7][:], ALU.mult), 11)
                link(TT(sm[5][:], sm[5][:], sm[7][:], ALU.subtract), 12)
                nc.vector.scalar_tensor_tensor(sm[1][:], sm[0][:], 0.0, sm[5][:], ALU.max,
                                               ALU.add).then_inc(gate_pre, 1)
                dve.wait_ge(gate_pre, l + 1)
                link(TT(sm[8][:], sm[1][:], ea, ALU.mult), 13)
                for r in range(2):
                    ins = TS(tab[:, :, T_G, r, :].rearrange("p h c -> p c h"), sm[8][:, :, r * 8:(r + 1) * 8], -1.0,
                             None, ALU.mult)
                link(ins, 14)
                dve.wait_ge(cum_mm, l + 1)
                for r in range(2):
                    ins = TS(tab[:, :, T_CUM, r, :].rearrange("p h c -> p c h"),
                             PS[:, 5, r * 32:(r + 1) * 32].rearrange("p (c h) -> p c h", c=CHUNKS), -1.0, None,
                             ALU.mult)
                    link(ins, 15 + r)
                dve.wait_ge(gate_act, l * 5 + 4)
                for kind, sign in ((T_BETA, 1.0), (T_NEG_BETA, -1.0)):
                    for r in range(2):
                        ins = TS(tab[:, :, kind, r, :].rearrange("p h c -> p c h"), sm[9][:, :, r * 8:(r + 1) * 8],
                                 sign, None, ALU.mult)
                    link(ins, 17 + (kind == T_NEG_BETA))
                dve.wait_ge(gate_act, l * 5 + 5)
                link(TS(tab[:, :, T_NEG_EG].rearrange("p h r c -> p h (r c)"),
                        tab[:, :, T_EG].rearrange("p h r c -> p h (r c)"), -1.0, None, ALU.mult), 19)
                stage_end(dve, l, 1)

                with dve.Fori(0, HEADS) as h:
                    n = l * HEADS + h
                    nc.vector.tensor_copy(ht[:].rearrange("p k r c -> p (k r c)"),
                                          tab[:, bass.ds(h, 1)].rearrange("p a k r c -> p (a k r c)")).then_inc(head_cols, 1)
                    for u, dst in ((0, qn), (HEADS, kn)):
                        src = raw[:, bass.ds(h + u, 1), :, :].rearrange("p a c t -> p (a c) t")
                        TT(dst[:], src, cols(rn[:, bass.ds(h + u, 1), :].rearrange("p a c -> p (a c)")),
                           ALU.mult).then_inc(qk_normed, 1)
                    dve.wait_ge(head_cols, n + 1)
                    for r in range(2):
                        TT(W[r][:], rows(tri[r]), cols(ht[:, T_G, r, :]), ALU.mult).then_inc(g_tri, 1)
                    dve.wait_ge(qk_turned, n * 2 + 2)
                    nc.vector.tensor_copy(kT[:].rearrange("p c t -> p (c t)"), PS[:, 1, :]).then_inc(kT_ready, 1)
                    for r in range(2):
                        dve.wait_ge(g_rows, n * 2 + r + 1)
                        TT(DT[r][:], PS[:, 2 + r, :].rearrange("p (c t) -> p c t", c=CHUNKS),
                           cols(ht[:, T_CUM, r, :]), ALU.subtract).then_inc(g_diff, 1)
                    for r in range(2):
                        nc.vector.tensor_copy(X[r][:], rows(ident)).then_inc(x_ident, 1)
                        nc.vector.tensor_copy(Y[r][:], rows(ident)).then_inc(y_ident, 1)
                    for r in range(2):
                        edge = P - 1 if r == 0 else 0
                        dve.wait_ge(decay_done, n * 2 + r + 1)
                        TT(bdl[r][:], DT[r][:, :, edge], ht[:, T_BETA, r, :], ALU.mult).then_inc(bdl_done, 1)
                        TT(W[r][:], DT[r][:], cols(ht[:, T_NEG_BETA, r, :]), ALU.mult).then_inc(beta_decay, 1)
                        dve.wait_ge(beta_decay, n * 2 + r + 1)
                        dve.wait_ge(kk_done, n + 1)
                        TT(NLT[r][:], W[r][:], PS[:, 4, :].rearrange("p (c t) -> p c t", c=CHUNKS),
                           ALU.mult).then_inc(nlt_done, 1)
                    dve.wait_ge(kq_done, n + 1)
                    for r in range(2):
                        TT(QKT[r][:], DT[r][:], PS[:, 5, :].rearrange("p (c t) -> p c t", c=CHUNKS),
                           ALU.mult).then_inc(qkt_done, 1)

                    def keep(dst, mask, src):
                        settle(dve)
                        return nc.vector.copy_predicated(dst[:], rows(mask.bitcast(I32)), src)

                    def bank(b):
                        return PS[:, b, :].rearrange("p (c t) -> p c t", c=CHUNKS)
                    for r in range(2):
                        dve.wait_ge(nl_done, n * 2 + r + 1)
                        dve.wait_ge(x_ident, n * 2 + r + 1)
                        keep(X[r], x_mask[r][0], bank(2 + r)).then_inc(x_upd[r], 1)
                        dve.wait_ge(y_ident, n * 2 + r + 1)
                        dve.wait_ge(nlt_done, n * 2 + r + 1)
                        keep(Y[r], y_mask[r][0], NLT[r][:]).then_inc(y_upd[r], 1)
                    for lev in range(1, 7):
                        for r in range(2):
                            if lev < 6:
                                dve.wait_ge(p_mm[r], n * 5 + lev)
                                dve.wait_ge(x_upd[r], n * 6 + lev)
                                keep(X[r], x_mask[r][lev], bank(3 * r + 1)).then_inc(x_upd[r], 1)
                            dve.wait_ge(q_mm[r], n * 6 + lev)
                            dve.wait_ge(y_upd[r], n * 7 + lev)
                            keep(Y[r], y_mask[r][lev], bank(3 * r + 2)).then_inc(y_upd[r], 1)
                    for step in range(CHUNKS):
                        for r in range(2):
                            c = step if r == 0 else CHUNKS - 1 - step
                            v = raw[:, bass.ds(h + 2 * HEADS, 1), c, :].rearrange("p a t -> p (a t)")
                            if step == 0:
                                nc.vector.tensor_copy(R[r][:], v).then_inc(r_ready[r], 1)
                            else:
                                dve.wait_ge(ks_mm[r], n * 3 + step)
                                STT(R[r][:], PS[:, r, 0:P], ht[:, T_NEG_EG, r, c:c + 1], v, ALU.mult,
                                    ALU.add).then_inc(r_ready[r], 1)
                        for r in range(2):
                            c = step if r == 0 else CHUNKS - 1 - step
                            dve.wait_ge(o_mm[r], n * 4 + step + 1)
                            if step < CHUNKS - 1:
                                dve.wait_ge(st_mm[r], n * 3 + step + 1)
                                if step == 0:
                                    nc.vector.tensor_copy(S[r][:], PS[:, 6 + r, P:2 * P]).then_inc(s_ready[r], 1)
                                else:
                                    dve.wait_ge(s_ready[r], n * 3 + step)
                                    STT(S[r][:], S[r][:], egl[r][:, c:c + 1], PS[:, 6 + r, P:2 * P], ALU.mult,
                                        ALU.add).then_inc(s_ready[r], 1)
                            if step == 0:
                                nc.vector.tensor_copy(OD[r][:, c, :], PS[:, 6 + r, 0:P]).then_inc(o_out[r], 1)
                            else:
                                dve.wait_ge(o1_ready[r], n * 3 + step)
                                TT(OD[r][:, c, :], PS[:, 6 + r, 0:P], O1[r][:], ALU.add).then_inc(o_out[r], 1)
                    for r in range(2):
                        dve.wait_ge(o_out[r], n * 4 + 4)
                    od = o_dn[:, bass.ds(h, 1), :, :].rearrange("p a c t -> p (a c) t")
                    TT(od, OD[0][:], OD[1][:], ALU.add).then_inc(o_sum, 1)
                    dve.wait_ge(o_sum, n + 1)
                    TT(OD[0][:], od, od, ALU.mult).then_inc(o_sq, 1)
                    dve.wait_ge(o_sq, n + 1)
                    nc.vector.tensor_reduce(rno[:, bass.ds(h, 1), :].rearrange("p a c -> p (a c)"), OD[0][:], AX_X,
                                            ALU.add).then_inc(o_ss, 1)
                dve.wait_ge(o_ss, (l + 1) * HEADS)
                TS(rno[:], rno[:], 1.0 / P, RMS_EPS, ALU.mult, ALU.add).then_inc(rno_dve, 1)
                dve.wait_ge(rno_act, l + 1)
                nc.vector.reciprocal(rno[:], rno[:]).then_inc(rno_dve, 1)
                dve.wait_ge(rno_dve, l * 3 + 2)
                dve.sem_inc(rno_dve, 1)
                stage_end(dve, l, 2)

                with dve.Fori(0, HEADS // 2) as i:
                    for s in range(2):
                        n = l * 4 + i
                        src = o_dn[:, bass.ds(i * 2 + s, 1), :, :].rearrange("p a c t -> p (a c) t")
                        dve.wait_ge(on_used[s], n + 1)
                        TT(on[s][:], src, cols(rno[:, bass.ds(i * 2 + s, 1), :].rearrange("p a c -> p (a c)")),
                           ALU.mult).then_inc(on_ready[s], 1)
                        dve.wait_ge(on_turned[s], n + 1)
                        dve.wait_ge(z_silu[s], n + 1)
                        dve.sem_inc(on_used[s], 1)
                        STT(oz[s][:], PS[:, 2 + s, :], dn_w[:, bass.ds(l, 1)], zs[s][:], ALU.mult,
                            ALU.mult).then_inc(oz_ready[s], 1)
                        dve.wait_ge(oz_hi[s], n + 1)
                        hi = ozh[:, bass.ds(i * 2 + s, 1), :].rearrange("p a t -> p (a t)")
                        lo = ozl[:, bass.ds(i * 2 + s, 1), :].rearrange("p a t -> p (a t)")
                        TT(lo, oz[s][:], hi.bitcast(F32), ALU.subtract).then_inc(oz_lo[s], 1)
                        dve.wait_ge(oz_lo[s], n + 1)
                stage_end(dve, l, 3)

                with dve.Fori(0, SWC // 512) as b:
                    dve.wait_ge(unit_done[1], l * PAIRS + AT_SW + b * 2 + 3)
                    for c in (2, 3):
                        nc.vector.tensor_copy(sw[:, c, bass.ds(b * 512, 512)], PS[:, c, :]).then_inc(sw_dve, 1)
                stage_end(dve, l, 4)
                cos4 = cst[:, C_COS:C_COS + CHUNKS * 32].rearrange("p (c k) -> p c k", c=CHUNKS).unsqueeze(2)
                sin4 = cst[:, C_SIN:C_SIN + CHUNKS * 32].rearrange("p (c k) -> p c k", c=CHUNKS).unsqueeze(2)
                with dve.Fori(0, GROUPS) as g:
                    n = l * GROUPS + g
                    step = 0
                    for first, nh, dst in ((g * (GQ * HD), GQ, qg), (g * HD + D, 1, kg)):
                        src = sw[:, :, bass.ds(first, nh * HD)].rearrange("p c (q k) -> p c q k", q=nh)
                        a, b = src[:, :, :, 0:32], src[:, :, :, 32:64]
                        cos = cos4.broadcast_to([P, CHUNKS, nh, 32])
                        sin = sin4.broadcast_to([P, CHUNKS, nh, 32])
                        for half, (u, v, op) in enumerate(((a, b, ALU.subtract), (b, a, ALU.add))):
                            if step:
                                dve.wait_ge(rope_half, n * 4 + step)
                            TT(r1[:, :, 0:nh, :], u, cos, ALU.mult).then_inc(rope_mul, 1)
                            TT(r2[:, :, 0:nh, :], v, sin, ALU.mult).then_inc(rope_mul, 1)
                            dve.wait_ge(rope_mul, n * 8 + step * 2 + 2)
                            TT(dst[:, :, :, half * 32:half * 32 + 32], r1[:, :, 0:nh, :], r2[:, :, 0:nh, :],
                               op).then_inc(rope_half, 1)
                            step += 1
                    for q in (2, 3):
                        dve.wait_ge(qg_turned, n * 5 + q + 1)
                        nc.vector.tensor_copy(qgT[:, q, :], PS[0:HD, q, :]).then_inc(qgT_dve, 1)
                    dve.wait_ge(qg_turned, n * 5 + 5)
                    nc.vector.tensor_copy(kgT[:], PS[0:HD, 4, :]).then_inc(qgT_dve, 1)
                    snk_g = snk[:, bass.ds(l * 16 + g * GQ, GQ)]

                    def stats(b):
                        lo, hi = max(b - 1, 0), min(b + 2, CHUNKS)
                        m = n * 4 + b + 1
                        dve.wait_ge(scores, m)
                        nc.vector.tensor_reduce(mx[:], PS[:, 0:GQ, 0:(hi - lo) * P], AX_X, ALU.max).then_inc(max_raw, 1)
                        dve.wait_ge(max_raw, m)
                        STT(mx[:], mx[:], ATT_SCALE, snk_g, ALU.mult, ALU.max).then_inc(max_sink, 1)
                        dve.wait_ge(max_sink, m)
                        TS(mn[:], mx[:], -1.0, None, ALU.mult).then_inc(max_neg, 1)
                        TT(es[:], snk_g, mx[:], ALU.subtract).then_inc(sink_off, 1)
                    stats(0)
                    for b in range(CHUNKS):
                        lo, hi = max(b - 1, 0), min(b + 2, CHUNKS)
                        m = n * 4 + b + 1
                        dve.wait_ge(p_turned, m)
                        for j in range(1, hi - lo):
                            ins = nc.vector.tensor_copy(pT[:, j, :], PS[:, 4 + j, :])
                        ins.then_inc(pT_dve, 1)
                        dve.wait_ge(probs, m * 4)
                        dve.wait_ge(sink_exp, m)
                        TT(den[:], den[:], es[:], ALU.add).then_inc(den_sum, 1)
                        dve.wait_ge(den_sum, m)
                        nc.vector.reciprocal(rd[:], den[:]).then_inc(den_inv, 1)
                        dve.wait_ge(den_inv, m)
                        dve.wait_ge(pv_mm, m)
                        TT(o_sw[:, b, bass.ds(g * GQ * HD, GQ * HD)].rearrange("p (q k) -> p q k", q=GQ),
                           PS[:, 7, 0:GQ * HD].rearrange("p (q k) -> p q k", q=GQ), cols(rd[:], HD),
                           ALU.mult).then_inc(o_scaled, 1)
                        if b < CHUNKS - 1:
                            stats(b + 1)
                store_lo(osw_hi, l * 8, swh, swl, osw_lo)
                stage_end(dve, l, 5)

                with dve.Fori(0, KT // 2) as i:
                    for j in range(2):
                        n = (l * 4 + i) * 2 + j
                        pair = l * PAIRS + AT_MERGE + i * 4 + j * 2
                        tile = i * 2 + j
                        dve.wait_ge(gate_sig, n * 2 + 1)
                        dve.wait_ge(unit_done[1], pair + 2)
                        TT(mA[:], gA[j][:], PS[:, 4 * j + 1, :], ALU.mult).then_inc(mg_mul, 1)
                        dve.wait_ge(gate_sig, n * 2 + 2)
                        dve.wait_ge(unit_done[1], pair + 3)
                        TT(mB[:], gB[j][:], PS[:, 4 * j + 3, :], ALU.mult).then_inc(mg_mul, 1)
                        dve.wait_ge(mg_mul, n * 2 + 6)
                        TT(mS[:], mA[:], mB[:], ALU.add).then_inc(mg_sum, 1)
                        dve.wait_ge(mg_sum, n + 3)
                        hi = mgh[:, bass.ds(tile, 1), :].rearrange("p a t -> p (a t)")
                        lo = mgl[:, bass.ds(tile, 1), :].rearrange("p a t -> p (a t)")
                        nc.vector.tensor_copy(hi, mS[:]).then_inc(mg_hi, 1)
                        dve.wait_ge(mg_hi, n + 1)
                        TT(lo, mS[:], hi.bitcast(F32), ALU.subtract).then_inc(mg_lo, 1)
                        dve.wait_ge(mg_lo, n + 1)
                stage_end(dve, l, 6)

                def store_yT(n, dst):
                    dve.wait_ge(y_mm, l * 2 + n + 1)
                    for k in range(1, KT, 2):
                        nc.vector.tensor_copy(dst[:, k, :], PS[:, k, :]).then_inc(yT_dve, 1)

                def norm(n):
                    m = l * 2 + n
                    for c in range(CHUNKS):
                        dve.wait_ge(y_turned, m * 4 + c + 1)
                        STT(x[:, c, :].rearrange("p (b t) -> p b t", b=2), x[:, c, :].rearrange("p (b t) -> p b t", b=2),
                            ALPHA, PS[:, 2 * c:2 * c + 2, :], ALU.mult, ALU.add).then_inc(res_done, 1)
                    for c in range(CHUNKS):
                        dve.wait_ge(res_done, m * 4 + c + 1)
                        for half in range(2):
                            nc.vector.bn_stats(ln_st[:, c, half * 6:half * 6 + 6],
                                               x[:, c, half * 512:(half + 1) * 512]).then_inc(ln_stat, 1)
                    for c in range(CHUNKS):
                        dve.wait_ge(ln_stat, m * 8 + c * 2 + 2)
                        settle(dve)
                        nc.vector.bn_aggr(ln_mv[:, c, :], ln_st[:, c, :]).then_inc(ln_aggr, 1)
                    dve.wait_ge(ln_aggr, m * 4 + 4)
                    TS(ln_rs[:].rearrange("p c o -> p (c o)"), ln_mv[:, :, 1], LN_EPS, None, ALU.add).then_inc(ln_eps, 1)
                    dve.wait_ge(ln_sqrt, m + 1)
                    nc.vector.reciprocal(ln_rs[:], ln_rs[:]).then_inc(ln_inv, 1)
                    dve.wait_ge(ln_inv, m + 1)
                    dve.wait_ge(ln_loaded, m * 32 + 32)
                    for c in range(CHUNKS):
                        TS(x[:, c, :], x[:, c, :], ln_mv[:, c, 0:1], ln_rs[:, c, :], ALU.subtract,
                           ALU.mult).then_inc(ln_norm, 1)
                    for c in range(CHUNKS):
                        dve.wait_ge(ln_norm, m * 4 + c + 1)
                        TT(x[:, c, :], x[:, c, :], ln_g[:], ALU.mult).then_inc(ln_gain, 1)
                    for c in range(CHUNKS):
                        dve.wait_ge(ln_gain, m * 4 + c + 1)
                        TT(x[:, c, :], x[:, c, :], ln_b[:], ALU.add).then_inc(ln_out, 1)
                store_yT(0, yT_a)
                norm(0)
                stage_end(dve, l, 7)
                store_lo(x_hi, l * 16 + 8, xh, xl, x_lo)
                stage_end(dve, l, 8)

                with dve.Fori(0, FT // 2) as i:
                    for j in range(2):
                        n = (l * 11 + i) * 2 + j
                        dve.wait_ge(ff_silu, n + 1)
                        dve.wait_ge(unit_done[1], l * PAIRS + AT_GU + i * 2 + j + 2)
                        TT(hf[j][:], sg[j][:], PS[:, 2 * j + 1, :], ALU.mult).then_inc(ff_h, 1)
                        dve.wait_ge(ff_hi, n + 1)
                        hi = hh[:, bass.ds(i * 2 + j, 1), :].rearrange("p a t -> p (a t)")
                        lo = hl[:, bass.ds(i * 2 + j, 1), :].rearrange("p a t -> p (a t)")
                        TT(lo, hf[j][:], hi.bitcast(F32), ALU.subtract).then_inc(ff_lo, 1)
                dve.wait_ge(ff_lo, (l + 1) * FT)
                store_yT(1, yT_b)
                norm(1)
                stage_end(dve, l, 9)


def constants():
    i = np.arange(P)
    tiles = [np.eye(P), i[:, None] <= i[None, :], i[:, None] >= i[None, :], np.ones((P, P))]
    lows = [((i[:, None] // (2 * s)) == (i[None, :] // (2 * s))) & ((i[:, None] // s) % 2 == 1)
            & ((i[None, :] // s) % 2 == 0) for s in LEVELS]
    tiles += lows + [m.T for m in lows]
    half = HD // 2
    inv_freq = np.float32(10000.0) ** (-np.arange(half, dtype=np.float32) / np.float32(half))
    ang = np.arange(SEQ, dtype=np.float32)[:, None] * inv_freq[None, :]
    for table in (np.cos(ang), np.sin(ang)):
        tiles.append(table.reshape(CHUNKS, P, half).transpose(1, 0, 2).reshape(P, CHUNKS * half))
    return np.concatenate([np.asarray(t, np.float32) for t in tiles], axis=1)


def feature_tiles(w):
    n = w.shape[1] // P
    return w.reshape(KT, P, n, P).transpose(2, 1, 0, 3).reshape(n, P, KT * P)


def kernel(x, w_in, conv_w, a_log, dt_bias, dn_norm_w, sinks, w_branch_a, w_branch_b, w_out,
           ln1_g, ln1_b, w_gate_up, w_down, ln2_g, ln2_b):
    import concourse.bacc as bacc
    from concourse.bass_utils import run_bass_kernel_spmd

    w_in, w_gate_up, w_down, w_out = (np.asarray(a) for a in (w_in, w_gate_up, w_down, w_out))
    w_branch_a, w_branch_b = np.asarray(w_branch_a), np.asarray(w_branch_b)
    units = []
    for l in range(DEPTH):
        qkv, z, ba_cols, sw_cols, gates = np.split(w_in[l], [3072, 4096, 4128, 5664], axis=1)
        units.append(feature_tiles(qkv))
        units.append(feature_tiles(z))
        units.append(sw_cols.reshape(KT // 2, 2, P, SWC // 512, 512).transpose(3, 0, 2, 1, 4).reshape(-1, P, 1024))
        gate_tiles = feature_tiles(gates)
        units.append(np.stack([gate_tiles[:KT], feature_tiles(w_branch_a[l]), gate_tiles[KT:],
                               feature_tiles(w_branch_b[l])], axis=1).reshape(-1, P, 1024))
        units.append(w_out[l].reshape(KT, P, 1024))
        gu = feature_tiles(w_gate_up[l])
        units.append(np.stack([gu[:FT], gu[FT:]], axis=1).reshape(-1, P, 1024))
        units.append(w_down[l].reshape(FT, P, 1024))
    stream = np.concatenate(units).reshape(DEPTH * PAIRS, 2, P, 1024)

    def row(a):
        return np.ascontiguousarray(np.asarray(a).reshape(-1))
    arrays = {
        "x_in": np.asarray(x).reshape(CHUNKS, P, D).transpose(1, 0, 2),
        "stream": stream,
        "w_ba": w_in[:, :, 4096:4128].reshape(DEPTH, KT, P, 32).transpose(0, 2, 1, 3),
        "conv_w": np.asarray(conv_w).reshape(DEPTH, CONV, U_QKV, P).transpose(3, 0, 2, 1).reshape(P, DEPTH * U_QKV, CONV),
        "a_log": row(a_log),
        "dt_bias": row(dt_bias),
        "dn_norm": np.asarray(dn_norm_w).transpose(1, 0),
        "sinks": row(sinks),
        "ln_rows": np.stack([np.asarray(a) for a in (ln1_g, ln1_b, ln2_g, ln2_b)], axis=1),
        "consts": constants(),
    }
    arrays = {k: np.ascontiguousarray(v) for k, v in arrays.items()}
    nc = bacc.Bacc("TRN2", target_bir_lowering=False, num_devices=1)
    args = [nc.dram_tensor(k, v.shape, mybir.dt.from_np(v.dtype), kind="ExternalInput").ap() for k, v in arrays.items()]
    out = nc.dram_tensor("out", (P, CHUNKS, D), F32, kind="ExternalOutput").ap()
    trunk(nc, *args, out)
    result = run_bass_kernel_spmd(nc, [arrays], core_ids=[0]).results[0]["out"]
    return result.transpose(1, 0, 2).reshape(1, SEQ, D)
```

```python
from contextlib import ExitStack

import numpy as np

import concourse.bass as bass
from concourse import mybir

F32 = mybir.dt.float32
F32R = mybir.dt.float32r
BF16 = mybir.dt.bfloat16
F16 = mybir.dt.float16
I32 = mybir.dt.int32
ALU = mybir.AluOpType
ACT = mybir.ActivationFunctionType
AX_X = mybir.AxisListType.X

P = 128
SEQ = 512
D = 1024
DEPTH = 2
CHUNKS = SEQ // P
KT = D // P
HEADS = 8
CONV = 5
GROUPS = 4
HD = 64
GQ = 4
SWC = 1536
FF = 2816
FT = FF // P
ALPHA = (2.0 * DEPTH) ** 0.25
LN_EPS = 1e-5
RMS_EPS = 1e-6
ATT_SCALE = HD ** -0.5
NEG_BIG = 1.0e30
E_SCALE = 1024.0
LEVELS = (1, 2, 4, 8, 16, 32, 64)

U_QKV = 3 * HEADS
U_DELTA = 2 * HEADS
U_SW = SWC // 512 * (KT // 2)
U_ATT = HEADS
U_MERGE = 2 * KT
U_OUT = KT
U_GU = 2 * FT
U_DOWN = FT
UNITS = U_QKV + U_DELTA + U_SW + U_ATT + U_MERGE + U_OUT + U_GU + U_DOWN
PAIRS = UNITS // 2
AT_QKV = 0
AT_DELTA = AT_QKV + U_QKV // 2
AT_SW = AT_DELTA + U_DELTA // 2
AT_ATT = AT_SW + U_SW // 2
AT_MERGE = AT_ATT + U_ATT // 2
AT_OUT = AT_MERGE + U_MERGE // 2
AT_GU = AT_OUT + U_OUT // 2
AT_DOWN = AT_GU + U_GU // 2

C_ID = 0
C_TRIF = P
C_TRIB = 2 * P
C_ONES = 3 * P
C_LOW = 4 * P
C_UP = C_LOW + len(LEVELS) * P
C_MINUS = C_UP + len(LEVELS) * P
C_COS = C_MINUS + P
C_SIN = C_COS + CHUNKS * HD // 2
C_ALL = C_SIN + CHUNKS * HD // 2

T_G, T_CUM, T_EG, T_NEG_EG, T_BETA, T_NEG_BETA = range(6)

BARRIERS = 10
TURN_BANK = (0, 1, 2, 4)
SMALL = 7


def trunk(nc, x_in, stream, w_ba, conv_w, a_log, dt_bias, dn_norm, sinks, ln_rows, consts, out):
    with ExitStack() as ctx:
        base = [nc.sbuf_base + (-nc.sbuf_base) % 64]

        def place(name, shape, dt, at=None):
            size = int(np.prod(shape[1:])) * (2 if dt in (BF16, F16) else 4)
            if at is None:
                at = base[0]
                base[0] += size + (-size) % 32
            return nc.alloc_sbuf_tensor_at(name, shape, dt, offset=at)

        def sem(name):
            return ctx.enter_context(nc.semaphore(name))

        PS = ctx.enter_context(nc.psum_tensor("PS", [P, 8, 512], F32))

        x = place("x", [P, CHUNKS, D], F32)
        xh = place("xh", [P, KT, SEQ], F32R)
        xl = place("xl", [P, KT, SEQ], F32R)
        w_raw = [place(f"w_raw{s}", [P, 1024], F32) for s in range(2)]
        wh = [place(f"wh{s}", [P, 1024], F32R) for s in range(2)]
        wl = [place(f"wl{s}", [P, 1024], F32R) for s in range(2)]
        cst = place("cst", [P, C_ALL], F32)
        id_bf = place("id_bf", [P, P], BF16)
        id_16 = place("id_16", [P, P], F16)
        neg_bf = [place(f"neg_bf{r}", [P, P], BF16) for r in range(2)]
        cw = place("cw", [P, DEPTH * U_QKV, CONV], F32)
        dn_w = place("dn_w", [P, DEPTH], F32)
        exp_a = place("exp_a", [P, DEPTH * 16], F32)
        dtb = place("dtb", [P, DEPTH * 16], F32)
        snk = place("snk", [P, DEPTH * 16], F32)
        tab = place("tab", [P, HEADS, 6, 2, CHUNKS], F32)
        rn = place("rn", [P, 2 * HEADS, CHUNKS], F32)
        rno = place("rno", [P, HEADS, CHUNKS], F32)
        ln_st = place("ln_st", [P, CHUNKS, 12], F32)
        ln_mv = place("ln_mv", [P, CHUNKS, 2], F32)
        ln_rs = place("ln_rs", [P, CHUNKS, 1], F32)
        big = base[0]
        KB = 1024

        raw = place("raw", [P, U_QKV, CHUNKS, P], F32, big)
        o_dn = place("o_dn", [P, HEADS, CHUNKS, P], F32, big + 48 * KB)
        conv_in = [place(f"conv_in{s}", [P, SEQ + CONV - 1], F32, big + 64 * KB + s * 2112) for s in range(2)]
        conv_acc = [place(f"conv_acc{s}", [P, SEQ], F32, big + 69 * KB + s * 2 * KB) for s in range(2)]
        conv_act = [place(f"conv_act{s}", [P, SEQ], F32, big + 73 * KB + s * 2 * KB) for s in range(2)]
        sq = place("sq", [P, CHUNKS, P], F32, big + 77 * KB)
        ba_raw = place("ba_raw", [P, KT, 32], F32, big + 80 * KB)
        bah = place("bah", [P, KT, 32], F32R, big + 81 * KB)
        bal = place("bal", [P, KT, 32], F32R, big + 82 * KB)
        ba = place("ba", [P, CHUNKS, 32], F32, big + 83 * KB)
        sm = [place(f"sm{n}", [P, CHUNKS, 16], F32, big + 84 * KB + 256 * n) for n in range(10)]

        work = [big + 64 * KB]

        def head_buf(name, shape, dt=F32):
            t = place(name, shape, dt, work[0])
            work[0] += -(-int(np.prod(shape[1:])) * (2 if dt == F16 else 4) // 32) * 32
            return t
        blk = [P, CHUNKS, P]
        qn, kn, qT, kT = (head_buf(n, blk) for n in ("qn", "kn", "qT", "kT"))
        DT = [head_buf(f"DT{r}", blk) for r in range(2)]
        NAT = [head_buf(f"NAT{r}", blk) for r in range(2)]
        QKT = [head_buf(f"QKT{r}", blk) for r in range(2)]
        OD, YF, TMP = DT, NAT, QKT
        NAh = [head_buf(f"NAh{r}", blk, F16) for r in range(2)]
        NAl = [head_buf(f"NAl{r}", blk, F16) for r in range(2)]
        X = [head_buf(f"X{r}", blk, F16) for r in range(2)]
        Y = [head_buf(f"Y{r}", blk, F16) for r in range(2)]
        V = [head_buf(f"V{r}", blk, F16) for r in range(2)]
        S = [head_buf(f"S{r}", [P, P]) for r in range(2)]
        R = [head_buf(f"R{r}", [P, P]) for r in range(2)]
        VN = [head_buf(f"VN{r}", [P, P]) for r in range(2)]
        VS = [head_buf(f"VS{r}", [P, P]) for r in range(2)]
        O1 = [head_buf(f"O1{r}", [P, P]) for r in range(2)]
        ht = head_buf("ht", [P, 6, 2, CHUNKS])
        egl = [head_buf(f"egl{r}", [P, CHUNKS]) for r in range(2)]
        bdl = [head_buf(f"bdl{r}", [P, CHUNKS]) for r in range(2)]
        assert work[0] <= big + 112 * KB

        ozh = place("ozh", [P, KT, SEQ], F32R, big + 64 * KB)
        ozl = place("ozl", [P, KT, SEQ], F32R, big + 80 * KB)
        on = [place(f"on{s}", blk, F32, big + (32 + s * 2) * KB) for s in range(2)]
        zs = [place(f"zs{s}", [P, SEQ], F32, big + (36 + s * 2) * KB) for s in range(2)]
        oz = [place(f"oz{s}", [P, SEQ], F32, big + (40 + s * 2) * KB) for s in range(2)]
        gate_a = raw[:, HEADS:2 * HEADS, :, :].rearrange("p u c t -> p u (c t)")

        gate_b = place("gate_b", [P, KT, SEQ], F32, big)
        o_sw = place("o_sw", [P, CHUNKS, D], F32, big + 32 * KB)
        kv = place("kv", [P, CHUNKS, 512], F32, big + 48 * KB)
        qgT = place("qgT", [HD, GQ, SEQ], F32, big + 56 * KB)
        kgT = place("kgT", [HD, SEQ], F32, big + 96 * KB)
        r1 = place("r1", [P, CHUNKS, GQ, HD // 2], F32, big + 98 * KB)
        r2 = place("r2", [P, CHUNKS, GQ, HD // 2], F32, big + 100 * KB)
        kg = place("kg", [P, CHUNKS, 1, HD], F32, big + 102 * KB)
        qg = place("qg", [P, CHUNKS, GQ, HD], F32, big + 104 * KB)
        pr = place("pr", [P, GQ, 3, P], F32, big + 98 * KB)
        pT = place("pT", [P, 3, 512], F32, big + 104 * KB)
        mx, mn, es, den, rd = (place(f"att_{n}", [P, GQ], F32, big + 110 * KB + 32 * n) for n in range(5))
        swh = place("swh", [P, KT, SEQ], F32R, big + 48 * KB)
        swl = place("swl", [P, KT, SEQ], F32R, big + 96 * KB)

        mgh = place("mgh", [P, KT, SEQ], F32R, big + 32 * KB)
        mgl = place("mgl", [P, KT, SEQ], F32R, big + 16 * KB)

        yT_a = place("yT_a", [P, KT, SEQ], F32, big + 64 * KB)
        yT_b = place("yT_b", [P, KT, SEQ], F32, big)
        ln_g = place("ln_g", [P, D], F32, big + 88 * KB)
        ln_b = place("ln_b", [P, D], F32, big + 92 * KB)
        hh = place("hh", [P, FT, SEQ], F32R, big)
        hl = place("hl", [P, FT, SEQ], F32R, big + 44 * KB)
        sg = [place(f"sg{s}", [P, SEQ], F32, big + (96 + 2 * s) * KB) for s in range(2)]
        hf = [place(f"hf{s}", [P, SEQ], F32, big + (100 + 2 * s) * KB) for s in range(2)]
        assert big + 112 * KB <= nc.sbuf_usable_end, (big + 112 * KB, nc.sbuf_usable_end)

        ident = cst[:, C_ID:C_ID + P]
        ones = cst[:, C_ONES:C_ONES + P]
        tri = [cst[:, C_TRIF:C_TRIF + P], cst[:, C_TRIB:C_TRIB + P]]
        low = [cst[:, C_LOW + n * P:C_LOW + (n + 1) * P] for n in range(len(LEVELS))]
        up = [cst[:, C_UP + n * P:C_UP + (n + 1) * P] for n in range(len(LEVELS))]
        x_mask = [low, up]
        y_mask = [up, low]
        minus_ident = cst[:, C_MINUS:C_MINUS + P]

        def rows(ap):
            return ap.unsqueeze(1).broadcast_to([P, CHUNKS, P])

        def cols(ap, n=P):
            return ap.unsqueeze(2).broadcast_to([P, ap.shape[1], n])

        small_loaded = sem("small_loaded")
        settled = sem("settled")
        loaded = [sem(f"loaded{s}") for s in range(2)]
        split_done = [sem(f"split_done{s}") for s in range(2)]
        unit_done = [sem(f"unit_done{s}") for s in range(2)]
        w_hi_done = [sem(f"w_hi_done{s}") for s in range(2)]
        gate_pre = sem("gate_pre")
        on_used = [sem(f"on_used{s}") for s in range(2)]
        stage_done = sem("stage_done")
        ready_bf = sem("ready_bf")
        x_t = sem("x_t")
        x_hi = sem("x_hi")
        x_lo = sem("x_lo")
        conv_loaded = [sem(f"conv_loaded{s}") for s in range(2)]
        conv_step = [sem(f"conv_step{s}") for s in range(2)]
        conv_silu = [sem(f"conv_silu{s}") for s in range(2)]
        tok_ready = [sem(f"tok_ready{s}") for s in range(2)]
        tok_stored = [sem(f"tok_stored{s}") for s in range(2)]
        sq_done = sem("sq_done")
        sumsq_done = sem("sumsq_done")
        ba_loaded = sem("ba_loaded")
        ba_hi = sem("ba_hi")
        ba_lo = sem("ba_lo")
        ba_mm = sem("ba_mm")
        cum_mm = sem("cum_mm")
        gate_dve = sem("gate_dve")
        gate_act = sem("gate_act")
        head_cols = sem("head_cols")
        qk_normed = sem("qk_normed")
        qk_turned = sem("qk_turned")
        qT_ready = sem("qT_ready")
        kT_ready = sem("kT_ready")
        g_tri = sem("g_tri")
        g_rows = sem("g_rows")
        g_diff = sem("g_diff")
        decay_done = sem("decay_done")
        kk_done = sem("kk_done")
        kq_done = sem("kq_done")
        beta_decay = sem("beta_decay")
        bdl_done = sem("bdl_done")
        nat_raw = sem("nat_raw")
        nat_done = sem("nat_done")
        na_hi = sem("na_hi")
        na_lo = sem("na_lo")
        e_mm = [sem(f"e_mm{r}") for r in range(2)]
        e_ready = [sem(f"e_ready{r}") for r in range(2)]
        y_fix = [sem(f"y_fix{r}") for r in range(2)]
        y_done = [sem(f"y_done{r}") for r in range(2)]
        extra_out = [sem(f"extra_out{s}") for s in range(2)]
        qkt_done = sem("qkt_done")
        na_turned = sem("na_turned")
        x_upd = [sem(f"x_upd{r}") for r in range(2)]
        y_upd = [sem(f"y_upd{r}") for r in range(2)]
        v_mm = [sem(f"v_mm{r}") for r in range(2)]
        v_ready = [sem(f"v_ready{r}") for r in range(2)]
        xv_mm = [sem(f"xv_mm{r}") for r in range(2)]
        vx_mm = [sem(f"vx_mm{r}") for r in range(2)]
        ks_mm = [sem(f"ks_mm{r}") for r in range(2)]
        r_ready = [sem(f"r_ready{r}") for r in range(2)]
        tr_mm = [sem(f"tr_mm{r}") for r in range(2)]
        o1_ready = [sem(f"o1_ready{r}") for r in range(2)]
        vn_ready = [sem(f"vn_ready{r}") for r in range(2)]
        vs_ready = [sem(f"vs_ready{r}") for r in range(2)]
        o_mm = [sem(f"o_mm{r}") for r in range(2)]
        st_mm = [sem(f"st_mm{r}") for r in range(2)]
        o_out = [sem(f"o_out{r}") for r in range(2)]
        s_ready = [sem(f"s_ready{r}") for r in range(2)]
        o_sum = sem("o_sum")
        o_sq = sem("o_sq")
        o_ss = sem("o_ss")
        rno_dve = sem("rno_dve")
        rno_act = sem("rno_act")
        on_ready = [sem(f"on_ready{s}") for s in range(2)]
        on_turned = [sem(f"on_turned{s}") for s in range(2)]
        z_silu = [sem(f"z_silu{s}") for s in range(2)]
        oz_ready = [sem(f"oz_ready{s}") for s in range(2)]
        gate_b_out = sem("gate_b_out")
        oz_hi = [sem(f"oz_hi{s}") for s in range(2)]
        oz_lo = [sem(f"oz_lo{s}") for s in range(2)]
        sw_act = sem("sw_act")
        sw_dve = sem("sw_dve")
        rope_mul = sem("rope_mul")
        rope_half = sem("rope_half")
        qg_turned = sem("qg_turned")
        qgT_act = sem("qgT_act")
        qgT_dve = sem("qgT_dve")
        scores = sem("scores")
        stats_step = sem("stats_step")
        probs = sem("probs")
        den_step = sem("den_step")
        ident_set = sem("ident_set")
        sink_exp = sem("sink_exp")
        p_turned = sem("p_turned")
        pT_act = sem("pT_act")
        pT_dve = sem("pT_dve")
        pv_mm = sem("pv_mm")
        o_scaled = sem("o_scaled")
        osw_t = sem("osw_t")
        osw_hi = sem("osw_hi")
        osw_lo = sem("osw_lo")
        gate_sig = sem("gate_sig")
        mg_mul = sem("mg_mul")
        mg_sum = sem("mg_sum")
        mg_hi = sem("mg_hi")
        mg_lo = sem("mg_lo")
        ln_loaded = sem("ln_loaded")
        y_mm = sem("y_mm")
        yT_act = sem("yT_act")
        yT_dve = sem("yT_dve")
        y_turned = sem("y_turned")
        ln_dve = sem("ln_dve")
        ln_sqrt = sem("ln_sqrt")
        ff_silu = sem("ff_silu")
        ff_h = sem("ff_h")
        ff_hi = sem("ff_hi")
        ff_lo = sem("ff_lo")
        stored = sem("stored")

        def settle(eng):
            eng.sem_inc(settled, 1)

        def stage_end(eng, l, n):
            settle(eng)
            eng.drain().then_inc(stage_done, 1)
            eng.wait_ge(stage_done, (l * BARRIERS + n) * 3 + 3)
            settle(eng)

        block = ctx.enter_context(nc.Block())

        @block.sync
        def _(sp):
            for dst, src in ((x[:], x_in), (cst[:], consts), (cw[:], conv_w), (dn_w[:], dn_norm),
                             (exp_a[:], a_log.partition_broadcast(P)), (dtb[:], dt_bias.partition_broadcast(P)),
                             (snk[:], sinks.partition_broadcast(P))):
                sp.dma_start(dst, src).then_inc(small_loaded, 16)
            with sp.Fori(0, DEPTH * PAIRS) as p:
                for s in range(2):
                    sp.wait_ge(split_done[s], p + 1)
                    sp.dma_start(w_raw[s][:], stream[p, s, :, :]).then_inc(loaded[s], 16)
            sp.wait_ge(stage_done, DEPTH * BARRIERS * 3)
            sp.dma_start(out, x[:]).then_inc(stored, 16)
            sp.wait_ge(stored, 16)

        @block.gpsimd
        def _(pool):
            for s in range(2):
                pool.sem_inc(split_done[s], 1)
            with pool.Fori(0, DEPTH * PAIRS) as p:
                for s in range(2):
                    pool.wait_ge(loaded[s], p * 16 + 16)
                    pool.wait_ge(unit_done[s], p + 1)
                    settle(pool)
                    nc.gpsimd.tensor_scalar(wh[s][:], w_raw[s][:], 1.0, 1.0, ALU.mult, ALU.mult).then_inc(w_hi_done[s], 1)
                    pool.wait_ge(w_hi_done[s], p + 1)
                    nc.gpsimd.tensor_tensor(wl[s][:], w_raw[s][:], wh[s][:].bitcast(F32),
                                            ALU.subtract).then_inc(split_done[s], 1)

        @block.tensor
        def _(pe):
            mm = nc.tensor.matmul

            def unit_ready(pair, s):
                pe.wait_ge(split_done[s], pair + 2)

            def product(o, ah, al, bh, bl, first, last):
                mm(o, ah, bh, start=first, stop=False)
                mm(o, al, bh, start=False, stop=False)
                return mm(o, ah, bl, start=False, stop=last)

            def feature_unit(s, bank, bh, bl):
                for k in range(KT):
                    c = slice(k * P, (k + 1) * P)
                    ins = product(PS[:, bank, :], wh[s][:, c], wl[s][:, c], bh[:, k, :], bl[:, k, :],
                                  k == 0, k == KT - 1)
                ins.then_inc(unit_done[s], 1)

            def turn_to_features(l_count, src, turned, lo_done):
                for k in range(KT):
                    for c in range(CHUNKS):
                        ins = nc.tensor.transpose(PS[:, k, c * P:(c + 1) * P], src[:, c, k * P:(k + 1) * P], ident)
                    ins.then_inc(turned, 1)

            def down_units(l, first_pair, npairs, bh, bl):
                def pair_of(i, first, last):
                    for s in range(2):
                        unit_ready(l * PAIRS + first_pair + i, s)
                        k = i * 2 + s
                        for d in range(KT):
                            c = slice(d * P, (d + 1) * P)
                            ins = product(PS[:, d, :], wh[s][:, c], wl[s][:, c],
                                          bh[:, bass.ds(k, 1), :].rearrange("p a t -> p (a t)"),
                                          bl[:, bass.ds(k, 1), :].rearrange("p a t -> p (a t)"),
                                          first and s == 0, last and s == 1)
                        ins.then_inc(unit_done[s], 1)
                pair_of(0, True, False)
                with pe.Fori(1, npairs - 1) as i:
                    pair_of(i, False, False)
                pair_of(npairs - 1, False, True)

            def turn_back(l, src, n):
                pe.wait_ge(yT_act, (l * 2 + n) * 4 + 4)
                pe.wait_ge(yT_dve, (l * 2 + n) * 4 + 4)
                for c in range(CHUNKS):
                    for half in range(2):
                        for j in range(4):
                            ins = nc.tensor.transpose(PS[:, c * 2 + half, j * P:(j + 1) * P],
                                                      src[:, half * 4 + j, c * P:(c + 1) * P], ident)
                    ins.then_inc(y_turned, 1)

            pe.sem_inc(unit_done[0], 1)
            pe.sem_inc(unit_done[1], 1)
            pe.wait_ge(small_loaded, 16 * SMALL)
            pe.wait_ge(ready_bf, 6)
            with pe.Fori(0, DEPTH) as l:
                turn_to_features(l, x, x_t, None)
                stage_end(pe, l, 0)

                def qkv_unit(i, s):
                    unit_ready(l * PAIRS + AT_QKV + i, s)
                    feature_unit(s, s, xh, xl)

                def qkv_turn(i, s):
                    pe.wait_ge(conv_silu[s], l * 12 + i + 1)
                    for c in range(CHUNKS):
                        ins = nc.tensor.transpose(PS[:, 2 + s, c * P:(c + 1) * P],
                                                  conv_act[s][:, c * P:(c + 1) * P], ident)
                    ins.then_inc(tok_ready[s], 1)
                qkv_unit(0, 0)
                with pe.Fori(0, U_QKV // 2 - 1) as i:
                    qkv_unit(i, 1)
                    qkv_turn(i, 0)
                    qkv_unit(i + 1, 0)
                    qkv_turn(i, 1)
                last = U_QKV // 2 - 1
                qkv_unit(last, 1)
                qkv_turn(last, 0)
                qkv_turn(last, 1)

                pe.wait_ge(ba_lo, l + 1)
                for c in range(CHUNKS):
                    t = slice(c * P, (c + 1) * P)
                    for k in range(KT):
                        ins = product(PS[:, 4, c * 32:(c + 1) * 32], xh[:, k, t], xl[:, k, t],
                                      bah[:, k, :], bal[:, k, :], k == 0, k == KT - 1)
                ins.then_inc(ba_mm, 1)
                pe.wait_ge(gate_dve, l * 19 + 13)
                for r in range(2):
                    ins = mm(PS[:, 5, r * 32:(r + 1) * 32].rearrange("p (c h) -> p c h", c=CHUNKS), tri[r],
                             sm[8][:, :, r * 8:(r + 1) * 8], start=True, stop=True)
                ins.then_inc(cum_mm, 1)
                stage_end(pe, l, 1)

                def extra(n, h, j):
                    s, k = divmod(j, KT)
                    if k == 0:
                        unit_ready(l * PAIRS + AT_DELTA + h, s)
                        pe.wait_ge(extra_out[s], n + 1)
                    c = slice(k * P, (k + 1) * P)
                    ins = product(PS[:, 6 + s, :], wh[s][:, c], wl[s][:, c], xh[:, k, :], xl[:, k, :],
                                  k == 0, k == KT - 1)
                    if k == KT - 1:
                        ins.then_inc(unit_done[s], 1)

                with pe.Fori(0, HEADS) as h:
                    n = l * HEADS + h
                    pe.wait_ge(qk_normed, n * 2 + 1)
                    for c in range(CHUNKS):
                        ins = nc.tensor.transpose(PS[:, 0, c * P:(c + 1) * P], qn[:, c, :], ident)
                    ins.then_inc(qk_turned, 1)
                    pe.wait_ge(qk_normed, n * 2 + 2)
                    for c in range(CHUNKS):
                        ins = nc.tensor.transpose(PS[:, 1, c * P:(c + 1) * P], kn[:, c, :], ident)
                    ins.then_inc(qk_turned, 1)
                    for j in range(3):
                        extra(n, h, j)
                    for r in range(2):
                        pe.wait_ge(g_tri, n * 2 + r + 1)
                        mm(PS[:, 2 + r, :], ones, TMP[r][:].rearrange("p c t -> p (c t)"), start=True, stop=False)
                        mm(PS[:, 2 + r, :].rearrange("p (c t) -> p c t", c=CHUNKS), id_bf[:], rows(neg_bf[r][:]),
                           start=False, stop=True).then_inc(g_rows, 1)
                    pe.wait_ge(kT_ready, n + 1)
                    pe.wait_ge(qT_ready, n + 1)
                    for c in range(CHUNKS):
                        ins = mm(PS[:, 0, c * P:(c + 1) * P], kT[:, c, :], kT[:, c, :], start=True, stop=True)
                    ins.then_inc(kk_done, 1)
                    for c in range(CHUNKS):
                        ins = mm(PS[:, 1, c * P:(c + 1) * P], kT[:, c, :], qT[:, c, :], start=True, stop=True)
                    ins.then_inc(kq_done, 1)
                    for j in range(3, 6):
                        extra(n, h, j)
                    for r in range(2):
                        pe.wait_ge(nat_done, n * 2 + r + 1)
                        for c in range(CHUNKS):
                            ins = nc.tensor.transpose(PS[:, 4 + r, c * P:(c + 1) * P], NAT[r][:, c, :], ident)
                        ins.then_inc(na_turned, 1)
                    for lev in range(1, 7):
                        for r in range(2):
                            if lev == 1:
                                pe.wait_ge(na_hi, n * 2 + r + 1)
                                pe.wait_ge(nat_done, n * 2 + 2)
                            pe.wait_ge(y_upd[r], n * 7 + lev)
                            for c in range(CHUNKS):
                                ins = mm(PS[:, 3 * r, c * P:(c + 1) * P], NAh[r][:, c, :], Y[r][:, c, :],
                                         start=True, stop=True)
                            ins.then_inc(v_mm[r], 1)
                        extra(n, h, 5 + lev)
                        for r in range(2):
                            if lev == 1:
                                pe.wait_ge(qkt_done, n * 2 + 2)
                                pe.wait_ge(na_lo, n * 2 + 1 + r)
                            pe.wait_ge(v_ready[r], n * 6 + lev)
                            pe.wait_ge(x_upd[r], n * 7 + lev)
                            for c in range(CHUNKS):
                                ins = mm(PS[:, 3 * r + 1, c * P:(c + 1) * P], X[r][:, c, :], V[r][:, c, :],
                                         start=True, stop=True)
                            ins.then_inc(xv_mm[r], 1)
                            for c in range(CHUNKS):
                                ins = mm(PS[:, 3 * r + 2, c * P:(c + 1) * P], V[r][:, c, :], X[r][:, c, :],
                                         start=True, stop=True)
                            ins.then_inc(vx_mm[r], 1)
                    for r in range(2):
                        pe.wait_ge(y_upd[r], n * 7 + 7)
                        for c in range(CHUNKS):
                            o = PS[:, 3 * r, c * P:(c + 1) * P]
                            mm(o, id_16[:], id_16[:], start=True, stop=False)
                            mm(o, NAh[r][:, c, :], Y[r][:, c, :], start=False, stop=False)
                            ins = mm(o, NAl[r][:, c, :], Y[r][:, c, :], start=False, stop=True)
                        ins.then_inc(e_mm[r], 1)
                    extra(n, h, 12)
                    extra(n, h, 13)
                    for r in range(2):
                        pe.wait_ge(e_ready[r], n + 1)
                        pe.wait_ge(x_upd[r], n * 7 + 7)
                        for c in range(CHUNKS):
                            ins = mm(PS[:, 3 * r + 1, c * P:(c + 1) * P], X[r][:, c, :], V[r][:, c, :],
                                     start=True, stop=True)
                        ins.then_inc(y_fix[r], 1)
                    extra(n, h, 14)
                    for step in range(CHUNKS):
                        for r in range(2):
                            c = step if r == 0 else CHUNKS - 1 - step
                            if step == 0:
                                pe.wait_ge(y_done[0], n + 1)
                                pe.wait_ge(y_done[1], n + 1)
                            else:
                                pe.wait_ge(s_ready[r], n * 3 + step)
                                mm(PS[:, r, 0:P], kT[:, c, :], S[r][:], start=True, stop=True).then_inc(ks_mm[r], 1)
                                pe.wait_ge(o_out[r], n * 4 + step)
                                mm(PS[:, 2 + r, 0:P], qT[:, c, :], S[r][:], start=True, stop=True)
                        if step == 1:
                            extra(n, h, 15)
                        for r in range(2):
                            c = step if r == 0 else CHUNKS - 1 - step
                            pe.wait_ge(r_ready[r], n * 4 + step + 1)
                            mm(PS[:, 4 + r, 0:P], YF[r][:, c, :], R[r][:], start=True, stop=True).then_inc(tr_mm[r], 1)
                        for r in range(2):
                            c = step if r == 0 else CHUNKS - 1 - step
                            if step < CHUNKS - 1:
                                pe.wait_ge(vs_ready[r], n * 3 + step + 1)
                                mm(PS[:, r, P:2 * P], kn[:, c, :], VS[r][:], start=True,
                                   stop=True).then_inc(st_mm[r], 1)
                            pe.wait_ge(vn_ready[r], n * 4 + step + 1)
                            mm(PS[:, 2 + r, P:2 * P], QKT[r][:, c, :], VN[r][:], start=True,
                               stop=True).then_inc(o_mm[r], 1)
                    for r in range(2):
                        pe.wait_ge(o_out[r], n * 4 + 4)
                stage_end(pe, l, 2)

                with pe.Fori(0, HEADS // 2) as i:
                    for s in range(2):
                        pe.wait_ge(oz_ready[s], l * 4 + i + 1)
                        pe.wait_ge(on_ready[s], l * 4 + i + 1)
                        for c in range(CHUNKS):
                            ins = nc.tensor.transpose(PS[:, 2 + s, c * P:(c + 1) * P], on[s][:, c, :], ident)
                        ins.then_inc(on_turned[s], 1)
                stage_end(pe, l, 3)

                with pe.Fori(0, SWC // 512) as b:
                    pe.wait_ge(sw_act, (l * 3 + b) * 2 + 1)
                    pe.wait_ge(sw_dve, (l * 3 + b) * 2 + 1)
                    for u in range(KT // 2):
                        s = u % 2
                        unit_ready(l * PAIRS + AT_SW + b * 2 + u // 2, s)
                        for j in range(2):
                            k = u * 2 + j
                            for c in range(CHUNKS):
                                t = slice(c * P, (c + 1) * P)
                                w = slice(j * 512, (j + 1) * 512)
                                ins = product(PS[:, c, :], xh[:, k, t], xl[:, k, t], wh[s][:, w], wl[s][:, w],
                                              k == 0, k == KT - 1)
                        ins.then_inc(unit_done[s], 1)
                stage_end(pe, l, 4)

                with pe.Fori(0, GROUPS) as g:
                    n = l * GROUPS + g
                    pe.wait_ge(rope_half, n * 4 + 4)
                    settle(pe)
                    for q in range(GQ):
                        for c in range(CHUNKS):
                            ins = nc.tensor.transpose(PS[0:HD, TURN_BANK[q], c * P:(c + 1) * P], qg[:, c, q, :], ident)
                        ins.then_inc(qg_turned, 1)
                    for c in range(CHUNKS):
                        ins = nc.tensor.transpose(PS[0:HD, 5, c * P:(c + 1) * P], kg[:, c, 0, :], ident)
                    ins.then_inc(qg_turned, 1)

                    def extra_gate(j):
                        s, k = divmod(j, KT)
                        if k == 0:
                            unit_ready(l * PAIRS + AT_ATT + g, s)
                            pe.wait_ge(gate_b_out, n * 2 + s + 1)
                        c = slice(k * P, (k + 1) * P)
                        ins = product(PS[:, 3, :], wh[s][:, c], wl[s][:, c], xh[:, k, :], xl[:, k, :],
                                      k == 0, k == KT - 1)
                        if k == KT - 1:
                            ins.then_inc(unit_done[s], 1)

                    def score(b):
                        lo, hi = max(b - 1, 0), min(b + 2, CHUNKS)
                        if b == 0:
                            pe.wait_ge(qgT_act, n * 2 + 2)
                            pe.wait_ge(qgT_dve, n * 3 + 3)
                        else:
                            pe.wait_ge(probs, n * 16 + b * 4)
                        for j in range(hi - lo):
                            masked = lo + j != b
                            for q in range(GQ):
                                ins = mm(PS[:, j, q * P:(q + 1) * P], qgT[:, q, b * P:(b + 1) * P],
                                         kgT[:, (lo + j) * P:(lo + j + 1) * P], start=q == 0, stop=not masked,
                                         skip_group_check=True)
                            if masked:
                                mask = neg_bf[0 if lo + j < b else 1]
                                ins = mm(PS[:, j, :].rearrange("p (q t) -> p q t", q=GQ), id_bf[:], rows(mask[:]),
                                         start=False, stop=True, skip_group_check=True)
                        ins.then_inc(scores, 1)
                    score(0)
                    for b in range(CHUNKS):
                        lo, hi = max(b - 1, 0), min(b + 2, CHUNKS)
                        extra_gate(4 * b)
                        extra_gate(4 * b + 1)
                        pe.wait_ge(probs, n * 16 + b * 4 + 4)
                        for j in range(hi - lo):
                            for q in range(GQ):
                                ins = nc.tensor.transpose(PS[:, 4 + j, q * P:(q + 1) * P], pr[:, q, j, :], ident)
                        ins.then_inc(p_turned, 1)
                        extra_gate(4 * b + 2)
                        extra_gate(4 * b + 3)
                        if b < CHUNKS - 1:
                            score(b + 1)
                        pe.wait_ge(pT_act, n * 4 + b + 1)
                        pe.wait_ge(pT_dve, n * 4 + b + 1)
                        if b > 0:
                            pe.wait_ge(o_scaled, n * 4 + b)
                        for q in range(GQ):
                            for j in range(hi - lo):
                                v = kv[:, lo + j, bass.ds(256 + g * HD, HD)]
                                ins = mm(PS[:, 7, q * HD:(q + 1) * HD], pT[:, j, q * P:(q + 1) * P], v,
                                         start=j == 0, stop=j == hi - lo - 1)
                        ins.then_inc(pv_mm, 1)
                    pe.wait_ge(o_scaled, n * 4 + 4)
                    settle(pe)
                pe.wait_ge(gate_b_out, (l + 1) * KT + 1)
                turn_to_features(l, o_sw, osw_t, None)
                stage_end(pe, l, 5)

                with pe.Fori(0, KT // 2) as i:
                    for j in range(2):
                        pe.wait_ge(mg_mul, (l * 4 + i) * 4 + 2 * j + 2)
                        pair = l * PAIRS + AT_MERGE + i * 2 + j
                        unit_ready(pair, 0)
                        feature_unit(0, 2 * j, ozh, ozl)
                        unit_ready(pair, 1)
                        feature_unit(1, 2 * j + 1, swh, swl)
                stage_end(pe, l, 6)

                down_units(l, AT_OUT, U_OUT // 2, mgh, mgl)
                pe.drain().then_inc(y_mm, 1)
                turn_back(l, yT_a, 0)
                stage_end(pe, l, 7)

                turn_to_features(l, x, x_t, None)
                stage_end(pe, l, 8)

                with pe.Fori(0, FT // 2) as i:
                    for j in range(2):
                        pair = l * PAIRS + AT_GU + i * 2 + j
                        pe.wait_ge(ff_h, (l * 11 + i) * 2 + j + 1)
                        for s in range(2):
                            unit_ready(pair, s)
                            feature_unit(s, 2 * j + s, xh, xl)
                pe.wait_ge(ff_lo, (l + 1) * FT)
                settle(pe)
                down_units(l, AT_DOWN, U_DOWN // 2, hh, hl)
                pe.drain().then_inc(y_mm, 1)
                turn_back(l, yT_b, 1)
                stage_end(pe, l, 9)

        @block.scalar
        def _(act):
            A = nc.scalar.activation

            def unit_full(pair, s):
                act.wait_ge(unit_done[s], pair + 2)

            def store_hi(turned, base_count, hi, done):
                for k in range(KT):
                    act.wait_ge(turned, base_count + k + 1)
                    A(hi[:, k, :], PS[:, k, :], ACT.Copy).then_inc(done, 1)

            act.wait_ge(small_loaded, 16 * SMALL)
            A(exp_a[:], exp_a[:], ACT.Exp).then_inc(ready_bf, 1)
            act.sem_inc(sw_act, 1)
            act.sem_inc(gate_b_out, 1)
            for s in range(2):
                act.sem_inc(extra_out[s], 1)
            with act.Fori(0, DEPTH) as l:
                act.dma_start(ba_raw[:], w_ba[l, :, :, :]).then_inc(ba_loaded, 16)
                store_hi(x_t, l * 16, xh, x_hi)
                stage_end(act, l, 0)

                with act.Fori(0, U_QKV // 2) as i:
                    n = l * 12 + i
                    for s in range(2):
                        unit_full(l * PAIRS + AT_QKV + i, s)
                        A(conv_in[s][:, 2:2 + SEQ], PS[:, s, :], ACT.Copy).then_inc(conv_loaded[s], 1)
                        act.wait_ge(conv_step[s], n * 5 + 5)
                        A(conv_act[s][:], conv_acc[s][:], ACT.Silu).then_inc(conv_silu[s], 1)
                        act.wait_ge(tok_ready[s], n + 1)
                        A(raw[:, bass.ds(i * 2 + s, 1), :, :].rearrange("p a c t -> p (a c t)"), PS[:, 2 + s, :],
                          ACT.Copy).then_inc(tok_stored[s], 1)
                act.wait_ge(gate_dve, l * 19 + 1)
                A(rn[:], rn[:], ACT.Sqrt).then_inc(gate_act, 1)
                act.wait_ge(gate_dve, l * 19 + 7)
                A(sm[3][:], sm[2][:], ACT.Exp).then_inc(gate_act, 1)
                act.wait_ge(gate_dve, l * 19 + 8)
                A(sm[5][:], sm[4][:], ACT.Ln).then_inc(gate_act, 1)
                A(sm[9][:], ba[:, :, 0:16], ACT.Sigmoid).then_inc(gate_act, 1)
                act.wait_ge(gate_dve, l * 19 + 16)
                A(tab[:, :, T_EG].rearrange("p h r c -> p h (r c)"),
                  tab[:, :, T_CUM].rearrange("p h r c -> p h (r c)"), ACT.Exp).then_inc(gate_act, 1)
                stage_end(act, l, 1)

                with act.Fori(0, HEADS) as h:
                    n = l * HEADS + h
                    act.wait_ge(qk_turned, n * 2 + 1)
                    A(qT[:].rearrange("p c t -> p (c t)"), PS[:, 0, :], ACT.Copy).then_inc(qT_ready, 1)
                    for r in range(2):
                        edge = P - 1 if r == 0 else 0
                        act.wait_ge(g_diff, n * 2 + r + 1)
                        A(egl[r][:], PS[:, 2 + r, :].rearrange("p (c t) -> p c t", c=CHUNKS)[:, :, edge], ACT.Exp)
                        A(DT[r][:], DT[r][:], ACT.Exp).then_inc(decay_done, 1)
                    for r in range(2):
                        act.wait_ge(na_turned, n * 2 + r + 1)
                        A(NAh[r][:].rearrange("p c t -> p (c t)"), PS[:, 4 + r, :], ACT.Copy).then_inc(na_hi, 1)
                    for lev in range(1, 7):
                        for r in range(2):
                            act.wait_ge(v_mm[r], n * 6 + lev)
                            A(V[r][:].rearrange("p c t -> p (c t)"), PS[:, 3 * r, :], ACT.Copy).then_inc(v_ready[r], 1)
                        if lev == 4:
                            unit_full(l * PAIRS + AT_DELTA + h, 0)
                            A(raw[:, bass.ds(h, 1), :, :].rearrange("p a c t -> p (a c t)"), PS[:, 6, :],
                              ACT.Copy).then_inc(extra_out[0], 1)
                    for r in range(2):
                        act.wait_ge(e_mm[r], n + 1)
                        act.wait_ge(vx_mm[r], n * 6 + 6)
                        A(V[r][:].rearrange("p c t -> p (c t)"), PS[:, 3 * r, :], ACT.Copy,
                          scale=E_SCALE).then_inc(e_ready[r], 1)
                    for step in range(CHUNKS):
                        if step > 0:
                            for r in range(2):
                                c = step if r == 0 else CHUNKS - 1 - step
                                act.wait_ge(tr_mm[r], n * 4 + step + 1)
                                A(O1[r][:], PS[:, 2 + r, 0:P], ACT.Copy,
                                  scale=ht[:, T_EG, r, c:c + 1]).then_inc(o1_ready[r], 1)
                        for r in range(2):
                            c = step if r == 0 else CHUNKS - 1 - step
                            act.wait_ge(tr_mm[r], n * 4 + step + 1)
                            if step == 0:
                                act.wait_ge(bdl_done, n * 2 + r + 1)
                            if step < CHUNKS - 1:
                                A(VS[r][:], PS[:, 4 + r, 0:P], ACT.Copy,
                                  scale=bdl[r][:, c:c + 1]).then_inc(vs_ready[r], 1)
                            A(VN[r][:], PS[:, 4 + r, 0:P], ACT.Copy,
                              scale=ht[:, T_BETA, r, c:c + 1]).then_inc(vn_ready[r], 1)
                        if step == 1:
                            unit_full(l * PAIRS + AT_DELTA + h, 1)
                            A(raw[:, bass.ds(h + HEADS, 1), :, :].rearrange("p a c t -> p (a c t)"), PS[:, 7, :],
                              ACT.Copy).then_inc(extra_out[1], 1)
                act.wait_ge(rno_dve, l * 3 + 1)
                A(rno[:], rno[:], ACT.Sqrt).then_inc(rno_act, 1)
                stage_end(act, l, 2)

                with act.Fori(0, HEADS // 2) as i:
                    for s in range(2):
                        n = l * 4 + i
                        act.wait_ge(oz_ready[s], n + 1)
                        A(zs[s][:], raw[:, bass.ds(i * 2 + s, 1), :, :].rearrange("p a c t -> p (a c t)"),
                          ACT.Silu).then_inc(z_silu[s], 1)
                        act.wait_ge(oz_ready[s], n + 2)
                        A(ozh[:, bass.ds(i * 2 + s, 1), :].rearrange("p a t -> p (a t)"), oz[s][:],
                          ACT.Copy).then_inc(oz_hi[s], 1)
                stage_end(act, l, 3)

                with act.Fori(0, 2) as b:
                    unit_full(l * PAIRS + AT_SW + b * 2 + 1, 1)
                    for c in (0, 1):
                        A(o_sw[:, c, bass.ds(b * 512, 512)], PS[:, c, :], ACT.Copy).then_inc(sw_act, 1)
                unit_full(l * PAIRS + AT_SW + 5, 1)
                for c in (0, 1):
                    A(kv[:, c, :], PS[:, c, :], ACT.Copy).then_inc(sw_act, 1)
                stage_end(act, l, 4)
                with act.Fori(0, GROUPS) as g:
                    n = l * GROUPS + g

                    def gate_out(s):
                        unit_full(l * PAIRS + AT_ATT + g, s)
                        A(gate_b[:, bass.ds(g * 2 + s, 1), :].rearrange("p a t -> p (a t)"), PS[:, 3, :],
                          ACT.Copy).then_inc(gate_b_out, 1)
                    for q in (0, 1):
                        act.wait_ge(qg_turned, n * 5 + q + 1)
                        A(qgT[:, q, :], PS[0:HD, q, :], ACT.Copy).then_inc(qgT_act, 1)
                    for b in range(CHUNKS):
                        nb = min(b + 2, CHUNKS) - max(b - 1, 0)
                        if b == 2:
                            gate_out(0)
                        act.wait_ge(stats_step, n * 16 + b * 4 + 3)
                        if b > 0:
                            act.wait_ge(p_turned, n * 4 + b)
                            act.wait_ge(den_step, n * 8 + b * 2)
                        for q in range(GQ):
                            A(pr[:, q, 0:nb, :], PS[:, 0:nb, q * P:(q + 1) * P], ACT.Exp, bias=mn[:, q:q + 1],
                              scale=ATT_SCALE, accum_out=den[:, q:q + 1]).then_inc(probs, 1)
                        act.wait_ge(stats_step, n * 16 + b * 4 + 4)
                        A(es[:], es[:], ACT.Exp).then_inc(sink_exp, 1)
                        act.wait_ge(p_turned, n * 4 + b + 1)
                        A(pT[:, 0, :], PS[:, 4, :], ACT.Copy).then_inc(pT_act, 1)
                    gate_out(1)
                store_hi(osw_t, l * 8, swh, osw_hi)
                stage_end(act, l, 5)

                with act.Fori(0, KT) as j:
                    for gate in (gate_a, gate_b):
                        g = gate[:, bass.ds(j, 1), :].rearrange("p a t -> p (a t)")
                        A(g, g, ACT.Sigmoid).then_inc(gate_sig, 1)
                stage_end(act, l, 6)

                act.dma_start(ln_g[:], ln_rows[l, 0, :].partition_broadcast(P)).then_inc(ln_loaded, 16)
                act.dma_start(ln_b[:], ln_rows[l, 1, :].partition_broadcast(P)).then_inc(ln_loaded, 16)

                def store_yT(n, dst):
                    act.wait_ge(y_mm, l * 2 + n + 1)
                    for k in range(0, KT, 2):
                        A(dst[:, k, :], PS[:, k, :], ACT.Copy).then_inc(yT_act, 1)

                def norm_sqrt(n):
                    act.wait_ge(ln_dve, (l * 2 + n) * 30 + 17)
                    A(ln_rs[:], ln_rs[:], ACT.Sqrt).then_inc(ln_sqrt, 1)
                store_yT(0, yT_a)
                norm_sqrt(0)
                stage_end(act, l, 7)
                store_hi(x_t, l * 16 + 8, xh, x_hi)
                stage_end(act, l, 8)

                with act.Fori(0, FT // 2) as i:
                    for j in range(2):
                        n = (l * 11 + i) * 2 + j
                        unit_full(l * PAIRS + AT_GU + i * 2 + j, 0)
                        A(sg[j][:], PS[:, 2 * j, :], ACT.Silu).then_inc(ff_silu, 1)
                        act.wait_ge(ff_h, n + 3)
                        A(hh[:, bass.ds(i * 2 + j, 1), :].rearrange("p a t -> p (a t)"), hf[j][:],
                          ACT.Copy).then_inc(ff_hi, 1)
                act.wait_ge(ff_lo, (l + 1) * FT)
                act.dma_start(ln_g[:], ln_rows[l, 2, :].partition_broadcast(P)).then_inc(ln_loaded, 16)
                act.dma_start(ln_b[:], ln_rows[l, 3, :].partition_broadcast(P)).then_inc(ln_loaded, 16)
                store_yT(1, yT_b)
                norm_sqrt(1)
                stage_end(act, l, 9)

        @block.vector
        def _(dve):
            TT = nc.vector.tensor_tensor
            TS = nc.vector.tensor_scalar
            STT = nc.vector.scalar_tensor_tensor

            def store_lo(hi_done, base_count, hi, lo, done):
                for k in range(KT):
                    dve.wait_ge(hi_done, base_count + k + 1)
                    TT(lo[:, k, :], PS[:, k, :], hi[:, k, :].bitcast(F32), ALU.subtract).then_inc(done, 1)

            dve.wait_ge(small_loaded, 16 * SMALL)
            nc.vector.tensor_copy(id_bf[:], ident).then_inc(ready_bf, 1)
            nc.vector.tensor_copy(id_16[:], ident).then_inc(ready_bf, 1)
            for r in range(2):
                TS(neg_bf[r][:], tri[r], 1.0, NEG_BIG, ALU.subtract, ALU.mult).then_inc(ready_bf, 1)
            nc.vector.memset(ln_rs[:], 0.0).then_inc(ready_bf, 1)
            dve.sem_inc(sw_dve, 1)
            for s in range(2):
                dve.sem_inc(oz_ready[s], 1)
                dve.sem_inc(on_used[s], 1)
                dve.sem_inc(mg_mul, 2)
                dve.sem_inc(ff_h, 1)
            dve.sem_inc(sumsq_done, 1)
            dve.wait_ge(ready_bf, 6)
            with dve.Fori(0, DEPTH) as l:
                store_lo(x_hi, l * 16, xh, xl, x_lo)
                for s in range(2):
                    nc.vector.memset(conv_in[s][:, 0:2], 0.0)
                    nc.vector.memset(conv_in[s][:, SEQ + 2:SEQ + 4], 0.0)
                dve.wait_ge(ba_loaded, l * 16 + 16)
                nc.vector.tensor_copy(bah[:], ba_raw[:]).then_inc(ba_hi, 1)
                dve.wait_ge(ba_hi, l + 1)
                TT(bal[:], ba_raw[:], bah[:].bitcast(F32), ALU.subtract).then_inc(ba_lo, 1)
                stage_end(dve, l, 0)

                with dve.Fori(0, U_QKV // 2) as i:
                    n = l * 12 + i
                    for s in range(2):
                        tile = l * U_QKV + i * 2 + s
                        dve.wait_ge(conv_loaded[s], n + 1)
                        for j in range(CONV):
                            w = cw[:, bass.ds(tile, 1), j:j + 1].rearrange("p a b -> p (a b)")
                            if j == 0:
                                TS(conv_acc[s][:], conv_in[s][:, 0:SEQ], w, None, ALU.mult).then_inc(conv_step[s], 1)
                            else:
                                dve.wait_ge(conv_step[s], n * 5 + j)
                                STT(conv_acc[s][:], conv_in[s][:, j:j + SEQ], w, conv_acc[s][:], ALU.mult,
                                    ALU.add).then_inc(conv_step[s], 1)
                for s in range(2):
                    dve.wait_ge(tok_stored[s], l * 12 + 12)
                settle(dve)
                with dve.Fori(0, 2 * HEADS) as u:
                    t = raw[:, bass.ds(u, 1), :, :].rearrange("p a c t -> p (a c) t")
                    dve.wait_ge(sumsq_done, l * 16 + u + 1)
                    TT(sq[:], t, t, ALU.mult).then_inc(sq_done, 1)
                    dve.wait_ge(sq_done, l * 16 + u + 1)
                    nc.vector.tensor_reduce(rn[:, bass.ds(u, 1), :].rearrange("p a c -> p (a c)"), sq[:], AX_X,
                                            ALU.add).then_inc(sumsq_done, 1)
                dve.wait_ge(sumsq_done, l * 16 + 17)

                g0 = l * 19

                def link(ins, n):
                    ins.then_inc(gate_dve, 1)
                    dve.wait_ge(gate_dve, g0 + n)
                link(TS(rn[:], rn[:], RMS_EPS, None, ALU.add), 1)
                dve.wait_ge(gate_act, l * 5 + 1)
                link(nc.vector.reciprocal(rn[:], rn[:]), 2)
                link(TS(rn[:, 0:HEADS, :], rn[:, 0:HEADS, :], float(P) ** -0.5, None, ALU.mult), 3)
                dve.wait_ge(ba_mm, l + 1)
                link(nc.vector.tensor_copy(ba[:].rearrange("p c n -> p (c n)"), PS[:, 4, 0:128]), 4)
                bias = dtb[:, bass.ds(l * 16, 16)].unsqueeze(1).broadcast_to([P, CHUNKS, 16])
                ea = exp_a[:, bass.ds(l * 16, 16)].unsqueeze(1).broadcast_to([P, CHUNKS, 16])
                link(TT(sm[0][:], ba[:, :, 16:32], bias, ALU.add), 5)
                link(TS(sm[1][:], sm[0][:], -1.0, None, ALU.mult), 6)
                link(TT(sm[2][:], sm[0][:], sm[1][:], ALU.min), 7)
                dve.wait_ge(gate_act, l * 5 + 2)
                link(TS(sm[4][:], sm[3][:], 1.0, None, ALU.add), 8)
                link(STT(sm[6][:], sm[4][:], 1.0, sm[3][:], ALU.subtract, ALU.subtract), 9)
                dve.wait_ge(gate_act, l * 5 + 3)
                link(nc.vector.reciprocal(sm[7][:], sm[4][:]), 10)
                link(TT(sm[7][:], sm[6][:], sm[7][:], ALU.mult), 11)
                link(TT(sm[5][:], sm[5][:], sm[7][:], ALU.subtract), 12)
                nc.vector.scalar_tensor_tensor(sm[1][:], sm[0][:], 0.0, sm[5][:], ALU.max,
                                               ALU.add).then_inc(gate_pre, 1)
                dve.wait_ge(gate_pre, l + 1)
                link(TT(sm[8][:], sm[1][:], ea, ALU.mult), 13)
                for r in range(2):
                    ins = TS(tab[:, :, T_G, r, :].rearrange("p h c -> p c h"), sm[8][:, :, r * 8:(r + 1) * 8], -1.0,
                             None, ALU.mult)
                link(ins, 14)
                dve.wait_ge(cum_mm, l + 1)
                for r in range(2):
                    ins = TS(tab[:, :, T_CUM, r, :].rearrange("p h c -> p c h"),
                             PS[:, 5, r * 32:(r + 1) * 32].rearrange("p (c h) -> p c h", c=CHUNKS), -1.0, None,
                             ALU.mult)
                    link(ins, 15 + r)
                dve.wait_ge(gate_act, l * 5 + 4)
                for kind, sign in ((T_BETA, 1.0), (T_NEG_BETA, -1.0)):
                    for r in range(2):
                        ins = TS(tab[:, :, kind, r, :].rearrange("p h c -> p c h"), sm[9][:, :, r * 8:(r + 1) * 8],
                                 sign, None, ALU.mult)
                    link(ins, 17 + (kind == T_NEG_BETA))
                dve.wait_ge(gate_act, l * 5 + 5)
                link(TS(tab[:, :, T_NEG_EG].rearrange("p h r c -> p h (r c)"),
                        tab[:, :, T_EG].rearrange("p h r c -> p h (r c)"), -1.0, None, ALU.mult), 19)
                stage_end(dve, l, 1)

                with dve.Fori(0, HEADS) as h:
                    n = l * HEADS + h
                    nc.vector.tensor_copy(ht[:].rearrange("p k r c -> p (k r c)"),
                                          tab[:, bass.ds(h, 1)].rearrange("p a k r c -> p (a k r c)")).then_inc(head_cols, 1)
                    for u, dst in ((0, qn), (HEADS, kn)):
                        src = raw[:, bass.ds(h + u, 1), :, :].rearrange("p a c t -> p (a c) t")
                        TT(dst[:], src, cols(rn[:, bass.ds(h + u, 1), :].rearrange("p a c -> p (a c)")),
                           ALU.mult).then_inc(qk_normed, 1)
                    dve.wait_ge(head_cols, n + 1)
                    for r in range(2):
                        TT(TMP[r][:], rows(tri[r]), cols(ht[:, T_G, r, :]), ALU.mult).then_inc(g_tri, 1)
                    dve.wait_ge(qk_turned, n * 2 + 2)
                    nc.vector.tensor_copy(kT[:].rearrange("p c t -> p (c t)"), PS[:, 1, :]).then_inc(kT_ready, 1)
                    for r in range(2):
                        dve.wait_ge(g_rows, n * 2 + r + 1)
                        TT(DT[r][:], PS[:, 2 + r, :].rearrange("p (c t) -> p c t", c=CHUNKS),
                           cols(ht[:, T_CUM, r, :]), ALU.subtract).then_inc(g_diff, 1)
                    def keep(dst, mask, src):
                        settle(dve)
                        return nc.vector.copy_predicated(dst[:], rows(mask.bitcast(I32)), src)

                    def bank(b):
                        return PS[:, b, :].rearrange("p (c t) -> p c t", c=CHUNKS)
                    for r in range(2):
                        nc.vector.tensor_copy(X[r][:], rows(ident)).then_inc(ident_set, 1)
                        nc.vector.tensor_copy(Y[r][:], rows(ident)).then_inc(ident_set, 1)
                    for r in range(2):
                        edge = P - 1 if r == 0 else 0
                        dve.wait_ge(decay_done, n * 2 + r + 1)
                        TT(TMP[r][:], DT[r][:], cols(ht[:, T_NEG_BETA, r, :]), ALU.mult).then_inc(beta_decay, 1)
                        dve.wait_ge(beta_decay, n * 2 + r + 1)
                        dve.wait_ge(kk_done, n + 1)
                        TT(NAT[r][:], TMP[r][:], bank(0), ALU.mult).then_inc(nat_raw, 1)
                        dve.wait_ge(nat_raw, n * 2 + r + 1)
                        keep(NAT[r], ident, rows(minus_ident)).then_inc(nat_done, 1)
                    for r in range(2):
                        dve.wait_ge(ident_set, n * 4 + 2 * r + 2)
                        dve.wait_ge(nat_done, n * 2 + r + 1)
                        keep(Y[r], y_mask[r][0], NAT[r][:]).then_inc(y_upd[r], 1)
                    dve.wait_ge(kq_done, n + 1)
                    for r in range(2):
                        TT(QKT[r][:], DT[r][:], bank(1), ALU.mult).then_inc(qkt_done, 1)
                    for r in range(2):
                        edge = P - 1 if r == 0 else 0
                        dve.wait_ge(na_hi, n * 2 + r + 1)
                        dve.wait_ge(ident_set, n * 4 + 2 * r + 1)
                        keep(X[r], x_mask[r][0], NAh[r][:]).then_inc(x_upd[r], 1)
                        TT(NAl[r][:], bank(4 + r), NAh[r][:], ALU.subtract).then_inc(na_lo, 1)
                        TT(bdl[r][:], DT[r][:, :, edge], ht[:, T_BETA, r, :], ALU.mult).then_inc(bdl_done, 1)
                    for lev in range(1, 7):
                        for r in range(2):
                            dve.wait_ge(xv_mm[r], n * 6 + lev)
                            dve.wait_ge(y_upd[r], n * 7 + lev)
                            keep(Y[r], y_mask[r][lev], bank(3 * r + 1)).then_inc(y_upd[r], 1)
                            dve.wait_ge(vx_mm[r], n * 6 + lev)
                            dve.wait_ge(x_upd[r], n * 7 + lev)
                            keep(X[r], x_mask[r][lev], bank(3 * r + 2)).then_inc(x_upd[r], 1)
                    for r in range(2):
                        dve.wait_ge(y_fix[r], n + 1)
                        dve.wait_ge(y_upd[r], n * 7 + 7)
                        STT(YF[r][:], bank(3 * r + 1), 1.0 / E_SCALE, Y[r][:], ALU.mult,
                            ALU.add).then_inc(y_done[r], 1)
                    for step in range(CHUNKS):
                        for r in range(2):
                            c = step if r == 0 else CHUNKS - 1 - step
                            v = raw[:, bass.ds(h + 2 * HEADS, 1), c, :].rearrange("p a t -> p (a t)")
                            if step == 0:
                                nc.vector.tensor_copy(R[r][:], v).then_inc(r_ready[r], 1)
                            else:
                                dve.wait_ge(ks_mm[r], n * 3 + step)
                                STT(R[r][:], PS[:, r, 0:P], ht[:, T_NEG_EG, r, c:c + 1], v, ALU.mult,
                                    ALU.add).then_inc(r_ready[r], 1)
                        for r in range(2):
                            c = step if r == 0 else CHUNKS - 1 - step
                            if step < CHUNKS - 1:
                                dve.wait_ge(st_mm[r], n * 3 + step + 1)
                                if step == 0:
                                    nc.vector.tensor_copy(S[r][:], PS[:, r, P:2 * P]).then_inc(s_ready[r], 1)
                                else:
                                    dve.wait_ge(s_ready[r], n * 3 + step)
                                    STT(S[r][:], S[r][:], egl[r][:, c:c + 1], PS[:, r, P:2 * P], ALU.mult,
                                        ALU.add).then_inc(s_ready[r], 1)
                            dve.wait_ge(o_mm[r], n * 4 + step + 1)
                            if step == 0:
                                nc.vector.tensor_copy(OD[r][:, c, :], PS[:, 2 + r, P:2 * P]).then_inc(o_out[r], 1)
                            else:
                                dve.wait_ge(o1_ready[r], n * 3 + step)
                                TT(OD[r][:, c, :], PS[:, 2 + r, P:2 * P], O1[r][:], ALU.add).then_inc(o_out[r], 1)
                    for r in range(2):
                        dve.wait_ge(o_out[r], n * 4 + 4)
                    od = o_dn[:, bass.ds(h, 1), :, :].rearrange("p a c t -> p (a c) t")
                    TT(od, OD[0][:], OD[1][:], ALU.add).then_inc(o_sum, 1)
                    dve.wait_ge(o_sum, n + 1)
                    TT(OD[0][:], od, od, ALU.mult).then_inc(o_sq, 1)
                    dve.wait_ge(o_sq, n + 1)
                    nc.vector.tensor_reduce(rno[:, bass.ds(h, 1), :].rearrange("p a c -> p (a c)"), OD[0][:], AX_X,
                                            ALU.add).then_inc(o_ss, 1)
                dve.wait_ge(o_ss, (l + 1) * HEADS)
                TS(rno[:], rno[:], 1.0 / P, RMS_EPS, ALU.mult, ALU.add).then_inc(rno_dve, 1)
                dve.wait_ge(rno_act, l + 1)
                nc.vector.reciprocal(rno[:], rno[:]).then_inc(rno_dve, 1)
                dve.wait_ge(rno_dve, l * 3 + 2)
                dve.sem_inc(rno_dve, 1)
                stage_end(dve, l, 2)

                with dve.Fori(0, HEADS // 2) as i:
                    for s in range(2):
                        n = l * 4 + i
                        src = o_dn[:, bass.ds(i * 2 + s, 1), :, :].rearrange("p a c t -> p (a c) t")
                        dve.wait_ge(on_used[s], n + 1)
                        TT(on[s][:], src, cols(rno[:, bass.ds(i * 2 + s, 1), :].rearrange("p a c -> p (a c)")),
                           ALU.mult).then_inc(on_ready[s], 1)
                        dve.wait_ge(on_turned[s], n + 1)
                        dve.wait_ge(z_silu[s], n + 1)
                        dve.sem_inc(on_used[s], 1)
                        STT(oz[s][:], PS[:, 2 + s, :], dn_w[:, bass.ds(l, 1)], zs[s][:], ALU.mult,
                            ALU.mult).then_inc(oz_ready[s], 1)
                        dve.wait_ge(oz_hi[s], n + 1)
                        hi = ozh[:, bass.ds(i * 2 + s, 1), :].rearrange("p a t -> p (a t)")
                        lo = ozl[:, bass.ds(i * 2 + s, 1), :].rearrange("p a t -> p (a t)")
                        TT(lo, oz[s][:], hi.bitcast(F32), ALU.subtract).then_inc(oz_lo[s], 1)
                        dve.wait_ge(oz_lo[s], n + 1)
                stage_end(dve, l, 3)

                with dve.Fori(0, 2) as b:
                    dve.wait_ge(unit_done[1], l * PAIRS + AT_SW + b * 2 + 3)
                    for c in (2, 3):
                        nc.vector.tensor_copy(o_sw[:, c, bass.ds(b * 512, 512)], PS[:, c, :]).then_inc(sw_dve, 1)
                dve.wait_ge(unit_done[1], l * PAIRS + AT_SW + 7)
                for c in (2, 3):
                    nc.vector.tensor_copy(kv[:, c, :], PS[:, c, :]).then_inc(sw_dve, 1)
                stage_end(dve, l, 4)
                cos4 = cst[:, C_COS:C_COS + CHUNKS * 32].rearrange("p (c k) -> p c k", c=CHUNKS).unsqueeze(2)
                sin4 = cst[:, C_SIN:C_SIN + CHUNKS * 32].rearrange("p (c k) -> p c k", c=CHUNKS).unsqueeze(2)
                with dve.Fori(0, GROUPS) as g:
                    n = l * GROUPS + g
                    step = 0
                    for tok, first, nh, dst in ((o_sw, g * (GQ * HD), GQ, qg), (kv, g * HD, 1, kg)):
                        src = tok[:, :, bass.ds(first, nh * HD)].rearrange("p c (q k) -> p c q k", q=nh)
                        a, b = src[:, :, :, 0:32], src[:, :, :, 32:64]
                        cos = cos4.broadcast_to([P, CHUNKS, nh, 32])
                        sin = sin4.broadcast_to([P, CHUNKS, nh, 32])
                        for half, (u, v, op) in enumerate(((a, b, ALU.subtract), (b, a, ALU.add))):
                            if step:
                                dve.wait_ge(rope_half, n * 4 + step)
                            TT(r1[:, :, 0:nh, :], u, cos, ALU.mult).then_inc(rope_mul, 1)
                            TT(r2[:, :, 0:nh, :], v, sin, ALU.mult).then_inc(rope_mul, 1)
                            dve.wait_ge(rope_mul, n * 8 + step * 2 + 2)
                            TT(dst[:, :, :, half * 32:half * 32 + 32], r1[:, :, 0:nh, :], r2[:, :, 0:nh, :],
                               op).then_inc(rope_half, 1)
                            step += 1
                    for q in (2, 3):
                        dve.wait_ge(qg_turned, n * 5 + q + 1)
                        nc.vector.tensor_copy(qgT[:, q, :], PS[0:HD, TURN_BANK[q], :]).then_inc(qgT_dve, 1)
                    dve.wait_ge(qg_turned, n * 5 + 5)
                    nc.vector.tensor_copy(kgT[:], PS[0:HD, 5, :]).then_inc(qgT_dve, 1)
                    snk_g = snk[:, bass.ds(l * 16 + g * GQ, GQ)]

                    def stats(b):
                        lo, hi = max(b - 1, 0), min(b + 2, CHUNKS)
                        m = n * 4 + b + 1
                        dve.wait_ge(scores, m)
                        nc.vector.tensor_reduce(mx[:], PS[:, 0:hi - lo, :].rearrange("p j (q t) -> p q j t", q=GQ),
                                                mybir.AxisListType.XY, ALU.max).then_inc(stats_step, 1)
                        dve.wait_ge(stats_step, m * 4 - 3)
                        STT(mx[:], mx[:], ATT_SCALE, snk_g, ALU.mult, ALU.max).then_inc(stats_step, 1)
                        dve.wait_ge(stats_step, m * 4 - 2)
                        TS(mn[:], mx[:], -1.0, None, ALU.mult).then_inc(stats_step, 1)
                        TT(es[:], snk_g, mx[:], ALU.subtract).then_inc(stats_step, 1)
                    stats(0)
                    for b in range(CHUNKS):
                        lo, hi = max(b - 1, 0), min(b + 2, CHUNKS)
                        m = n * 4 + b + 1
                        dve.wait_ge(p_turned, m)
                        for j in range(1, hi - lo):
                            ins = nc.vector.tensor_copy(pT[:, j, :], PS[:, 4 + j, :])
                        ins.then_inc(pT_dve, 1)
                        dve.wait_ge(probs, m * 4)
                        dve.wait_ge(sink_exp, m)
                        TT(den[:], den[:], es[:], ALU.add).then_inc(den_step, 1)
                        dve.wait_ge(den_step, m * 2 - 1)
                        nc.vector.reciprocal(rd[:], den[:]).then_inc(den_step, 1)
                        dve.wait_ge(den_step, m * 2)
                        dve.wait_ge(pv_mm, m)
                        TT(o_sw[:, b, bass.ds(g * GQ * HD, GQ * HD)].rearrange("p (q k) -> p q k", q=GQ),
                           PS[:, 7, 0:GQ * HD].rearrange("p (q k) -> p q k", q=GQ), cols(rd[:], HD),
                           ALU.mult).then_inc(o_scaled, 1)
                        if b < CHUNKS - 1:
                            stats(b + 1)
                store_lo(osw_hi, l * 8, swh, swl, osw_lo)
                stage_end(dve, l, 5)

                with dve.Fori(0, KT // 2) as i:
                    for j in range(2):
                        n = (l * 4 + i) * 2 + j
                        pair = l * PAIRS + AT_MERGE + i * 2 + j
                        tile = i * 2 + j
                        ga, gb, hi, lo = (t[:, bass.ds(tile, 1), :].rearrange("p a t -> p (a t)")
                                          for t in (gate_a, gate_b, mgh, mgl))
                        dve.wait_ge(gate_sig, n * 2 + 2)
                        dve.wait_ge(unit_done[0], pair + 2)
                        TT(ga, ga, PS[:, 2 * j, :], ALU.mult).then_inc(mg_mul, 1)
                        dve.wait_ge(unit_done[1], pair + 2)
                        TT(gb, gb, PS[:, 2 * j + 1, :], ALU.mult).then_inc(mg_mul, 1)
                        dve.wait_ge(mg_mul, n * 2 + 6)
                        TT(gb, ga, gb, ALU.add).then_inc(mg_sum, 1)
                        dve.wait_ge(mg_sum, n + 1)
                        nc.vector.tensor_copy(hi, gb).then_inc(mg_hi, 1)
                        dve.wait_ge(mg_hi, n + 1)
                        TT(lo, gb, hi.bitcast(F32), ALU.subtract).then_inc(mg_lo, 1)
                        dve.wait_ge(mg_lo, n + 1)
                stage_end(dve, l, 6)

                def store_yT(n, dst):
                    dve.wait_ge(y_mm, l * 2 + n + 1)
                    for k in range(1, KT, 2):
                        nc.vector.tensor_copy(dst[:, k, :], PS[:, k, :]).then_inc(yT_dve, 1)

                def norm(n):
                    m = l * 2 + n
                    for c in range(CHUNKS):
                        dve.wait_ge(y_turned, m * 4 + c + 1)
                        STT(x[:, c, :].rearrange("p (b t) -> p b t", b=2), x[:, c, :].rearrange("p (b t) -> p b t", b=2),
                            ALPHA, PS[:, 2 * c:2 * c + 2, :], ALU.mult, ALU.add).then_inc(ln_dve, 1)
                    for c in range(CHUNKS):
                        dve.wait_ge(ln_dve, m * 30 + c + 1)
                        for half in range(2):
                            nc.vector.bn_stats(ln_st[:, c, half * 6:half * 6 + 6],
                                               x[:, c, half * 512:(half + 1) * 512]).then_inc(ln_dve, 1)
                    for c in range(CHUNKS):
                        dve.wait_ge(ln_dve, m * 30 + 4 + c * 2 + 2)
                        settle(dve)
                        nc.vector.bn_aggr(ln_mv[:, c, :], ln_st[:, c, :]).then_inc(ln_dve, 1)
                    dve.wait_ge(ln_dve, m * 30 + 16)
                    TS(ln_rs[:].rearrange("p c o -> p (c o)"), ln_mv[:, :, 1], LN_EPS, None, ALU.add).then_inc(ln_dve, 1)
                    dve.wait_ge(ln_sqrt, m + 1)
                    nc.vector.reciprocal(ln_rs[:], ln_rs[:]).then_inc(ln_dve, 1)
                    dve.wait_ge(ln_dve, m * 30 + 18)
                    dve.wait_ge(ln_loaded, m * 32 + 32)
                    for c in range(CHUNKS):
                        TS(x[:, c, :], x[:, c, :], ln_mv[:, c, 0:1], ln_rs[:, c, :], ALU.subtract,
                           ALU.mult).then_inc(ln_dve, 1)
                    for c in range(CHUNKS):
                        dve.wait_ge(ln_dve, m * 30 + 18 + c + 1)
                        TT(x[:, c, :], x[:, c, :], ln_g[:], ALU.mult).then_inc(ln_dve, 1)
                    for c in range(CHUNKS):
                        dve.wait_ge(ln_dve, m * 30 + 22 + c + 1)
                        TT(x[:, c, :], x[:, c, :], ln_b[:], ALU.add).then_inc(ln_dve, 1)
                store_yT(0, yT_a)
                norm(0)
                stage_end(dve, l, 7)
                store_lo(x_hi, l * 16 + 8, xh, xl, x_lo)
                stage_end(dve, l, 8)

                with dve.Fori(0, FT // 2) as i:
                    for j in range(2):
                        n = (l * 11 + i) * 2 + j
                        dve.wait_ge(ff_silu, n + 1)
                        dve.wait_ge(unit_done[1], l * PAIRS + AT_GU + i * 2 + j + 2)
                        TT(hf[j][:], sg[j][:], PS[:, 2 * j + 1, :], ALU.mult).then_inc(ff_h, 1)
                        dve.wait_ge(ff_hi, n + 1)
                        hi = hh[:, bass.ds(i * 2 + j, 1), :].rearrange("p a t -> p (a t)")
                        lo = hl[:, bass.ds(i * 2 + j, 1), :].rearrange("p a t -> p (a t)")
                        TT(lo, hf[j][:], hi.bitcast(F32), ALU.subtract).then_inc(ff_lo, 1)
                dve.wait_ge(ff_lo, (l + 1) * FT)
                store_yT(1, yT_b)
                norm(1)
                stage_end(dve, l, 9)


def constants():
    i = np.arange(P)
    tiles = [np.eye(P), i[:, None] <= i[None, :], i[:, None] >= i[None, :], np.ones((P, P))]
    lows = [((i[:, None] // (2 * s)) == (i[None, :] // (2 * s))) & ((i[:, None] // s) % 2 == 1)
            & ((i[None, :] // s) % 2 == 0) for s in LEVELS]
    tiles += lows + [m.T for m in lows] + [-np.eye(P)]
    half = HD // 2
    inv_freq = np.float32(10000.0) ** (-np.arange(half, dtype=np.float32) / np.float32(half))
    ang = np.arange(SEQ, dtype=np.float32)[:, None] * inv_freq[None, :]
    for table in (np.cos(ang), np.sin(ang)):
        tiles.append(table.reshape(CHUNKS, P, half).transpose(1, 0, 2).reshape(P, CHUNKS * half))
    return np.concatenate([np.asarray(t, np.float32) for t in tiles], axis=1)


def feature_tiles(w):
    n = w.shape[1] // P
    return w.reshape(KT, P, n, P).transpose(2, 1, 0, 3).reshape(n, P, KT * P)


def kernel(x, w_in, conv_w, a_log, dt_bias, dn_norm_w, sinks, w_branch_a, w_branch_b, w_out,
           ln1_g, ln1_b, w_gate_up, w_down, ln2_g, ln2_b):
    import concourse.bacc as bacc
    from concourse.bass_utils import run_bass_kernel_spmd

    w_in, w_gate_up, w_down, w_out = (np.asarray(a) for a in (w_in, w_gate_up, w_down, w_out))
    w_branch_a, w_branch_b = np.asarray(w_branch_a), np.asarray(w_branch_b)
    units = []
    for l in range(DEPTH):
        qkv, z, ba_cols, sw_cols, gates = np.split(w_in[l], [3072, 4096, 4128, 5664], axis=1)
        units.append(feature_tiles(qkv))
        gate_tiles = feature_tiles(gates)
        units.append(np.stack([feature_tiles(z), gate_tiles[:KT]], axis=1).reshape(-1, P, 1024))
        units.append(sw_cols.reshape(KT // 2, 2, P, SWC // 512, 512).transpose(3, 0, 2, 1, 4).reshape(-1, P, 1024))
        units.append(gate_tiles[KT:])
        units.append(np.stack([feature_tiles(w_branch_a[l]), feature_tiles(w_branch_b[l])],
                              axis=1).reshape(-1, P, 1024))
        units.append(w_out[l].reshape(KT, P, 1024))
        gu = feature_tiles(w_gate_up[l])
        units.append(np.stack([gu[:FT], gu[FT:]], axis=1).reshape(-1, P, 1024))
        units.append(w_down[l].reshape(FT, P, 1024))
    stream = np.concatenate(units).reshape(DEPTH * PAIRS, 2, P, 1024)

    def row(a):
        return np.ascontiguousarray(np.asarray(a).reshape(-1))
    arrays = {
        "x_in": np.asarray(x).reshape(CHUNKS, P, D).transpose(1, 0, 2),
        "stream": stream,
        "w_ba": w_in[:, :, 4096:4128].reshape(DEPTH, KT, P, 32).transpose(0, 2, 1, 3),
        "conv_w": np.asarray(conv_w).reshape(DEPTH, CONV, U_QKV, P).transpose(3, 0, 2, 1).reshape(P, DEPTH * U_QKV, CONV),
        "a_log": row(a_log),
        "dt_bias": row(dt_bias),
        "dn_norm": np.asarray(dn_norm_w).transpose(1, 0),
        "sinks": row(sinks),
        "ln_rows": np.stack([np.asarray(a) for a in (ln1_g, ln1_b, ln2_g, ln2_b)], axis=1),
        "consts": constants(),
    }
    arrays = {k: np.ascontiguousarray(v) for k, v in arrays.items()}
    nc = bacc.Bacc("TRN2", target_bir_lowering=False, num_devices=1)
    args = [nc.dram_tensor(k, v.shape, mybir.dt.from_np(v.dtype), kind="ExternalInput").ap() for k, v in arrays.items()]
    out = nc.dram_tensor("out", (P, CHUNKS, D), F32, kind="ExternalOutput").ap()
    trunk(nc, *args, out)
    result = run_bass_kernel_spmd(nc, [arrays], core_ids=[0]).results[0]["out"]
    return result.transpose(1, 0, 2).reshape(1, SEQ, D)
```

```python
from contextlib import ExitStack

import numpy as np

import concourse.bass as bass
from concourse import mybir

F32 = mybir.dt.float32
F32R = mybir.dt.float32r
BF16 = mybir.dt.bfloat16
F16 = mybir.dt.float16
I32 = mybir.dt.int32
ALU = mybir.AluOpType
ACT = mybir.ActivationFunctionType
AX_X = mybir.AxisListType.X

P = 128
SEQ = 512
D = 1024
DEPTH = 2
CHUNKS = SEQ // P
KT = D // P
HEADS = 8
CONV = 5
GROUPS = 4
HD = 64
GQ = 4
SWC = 1536
FF = 2816
FT = FF // P
ALPHA = (2.0 * DEPTH) ** 0.25
LN_EPS = 1e-5
RMS_EPS = 1e-6
ATT_SCALE = HD ** -0.5
NEG_BIG = 1.0e30
E_SCALE = 1024.0
LEVELS = (1, 2, 4, 8, 16, 32, 64)

U_QKV = 3 * HEADS
U_DELTA = 2 * HEADS
U_SW = SWC // 512 * (KT // 2)
U_ATT = HEADS
U_MERGE = 2 * KT
U_OUT = KT
U_GU = 2 * FT
U_DOWN = FT
UNITS = U_QKV + U_DELTA + U_SW + U_ATT + U_MERGE + U_OUT + U_GU + U_DOWN
PAIRS = UNITS // 2
AT_QKV = 0
AT_DELTA = AT_QKV + U_QKV // 2
AT_SW = AT_DELTA + U_DELTA // 2
AT_ATT = AT_SW + U_SW // 2
AT_MERGE = AT_ATT + U_ATT // 2
AT_OUT = AT_MERGE + U_MERGE // 2
AT_GU = AT_OUT + U_OUT // 2
AT_DOWN = AT_GU + U_GU // 2

C_ID = 0
C_TRIF = P
C_TRIB = 2 * P
C_ONES = 3 * P
C_LOW = 4 * P
C_UP = C_LOW + len(LEVELS) * P
C_COS = C_UP + len(LEVELS) * P
C_SIN = C_COS + CHUNKS * HD // 2
C_ALL = C_SIN + CHUNKS * HD // 2

T_G, T_NEG_CUM, T_EG, T_NEG_EG, T_BETA, T_NEG_BETA = range(6)

BARRIERS = 7
LN_STEPS = 36
LN_VARIANCE = (10, 16, 22, 24)
LN_NORMED = (14, 20, 26, 28)
SMALL = 8


def trunk(nc, x_in, stream, w_ba, conv_w, a_log, dt_bias, dn_norm, sinks, ln_rows, ln_cols, consts, out):
    with ExitStack() as ctx:
        base = [nc.sbuf_base + (-nc.sbuf_base) % 64]

        def place(name, shape, dt, at=None):
            size = int(np.prod(shape[1:])) * (2 if dt in (BF16, F16) else 4)
            if at is None:
                at = base[0]
                base[0] += size + (-size) % 32
            return nc.alloc_sbuf_tensor_at(name, shape, dt, offset=at)

        def sem(name):
            return ctx.enter_context(nc.semaphore(name))

        PS = ctx.enter_context(nc.psum_tensor("PS", [P, 8, 512], F32))

        x = place("x", [P, CHUNKS, D], F32)
        xh = place("xh", [P, KT, SEQ], F32R)
        xl = place("xl", [P, KT, SEQ], F32R)
        w_raw = [place(f"w_raw{s}", [P, 1024], F32) for s in range(2)]
        wh = [place(f"wh{s}", [P, 1024], F32R) for s in range(2)]
        wl = [place(f"wl{s}", [P, 1024], F32R) for s in range(2)]
        cst = place("cst", [P, C_ALL], F32)
        id_bf = place("id_bf", [P, P], BF16)
        id_16 = place("id_16", [P, P], F16)
        minus_two = place("minus_two", [P, P], F16)
        neg_bf = [place(f"neg_bf{r}", [P, P], BF16) for r in range(2)]
        cw = place("cw", [P, DEPTH * U_QKV, CONV], F32)
        dn_w = place("dn_w", [P, DEPTH], F32)
        ln_c = place("ln_c", [P, DEPTH * 2, 2, KT], F32)
        exp_a = place("exp_a", [P, DEPTH * 16], F32)
        dtb = place("dtb", [P, DEPTH * 16], F32)
        snk = place("snk", [P, DEPTH * 16], F32)
        tab = place("tab", [P, HEADS, 6, 2, CHUNKS], F32)
        rn = place("rn", [P, 2 * HEADS, CHUNKS], F32)
        rno = place("rno", [P, HEADS, CHUNKS], F32)
        ln_st = place("ln_st", [P, CHUNKS, 12], F32)
        ln_mv = place("ln_mv", [P, CHUNKS, 2], F32)
        ln_rs = place("ln_rs", [P, CHUNKS, 1], F32)
        big = base[0]
        KB = 1024

        raw = place("raw", [P, U_QKV, CHUNKS, P], F32, big)
        o_dn = place("o_dn", [P, HEADS, CHUNKS, P], F32, big + 48 * KB)
        conv_in = [place(f"conv_in{s}", [P, SEQ + CONV - 1], F32, big + 64 * KB + s * 2112) for s in range(2)]
        conv_acc = [place(f"conv_acc{s}", [P, SEQ], F32, big + 69 * KB + s * 2 * KB) for s in range(2)]
        conv_act = [place(f"conv_act{s}", [P, SEQ], F32, big + 73 * KB + s * 2 * KB) for s in range(2)]
        sq = place("sq", [P, CHUNKS, P], F32, big + 77 * KB)
        ba_raw = place("ba_raw", [P, KT, 32], F32, big + 90 * KB)
        bah = place("bah", [P, KT, 32], F32R, big + 91 * KB)
        bal = place("bal", [P, KT, 32], F32R, big + 92 * KB)
        ba = place("ba", [P, CHUNKS, 32], F32, big + 83 * KB)
        baT = place("baT", [32, SEQ], F32, big + 87 * KB)
        sm = [place(f"sm{n}", [P, CHUNKS, 16], F32, big + 84 * KB + 256 * n) for n in range(10)]

        work = [big + 64 * KB]

        def head_buf(name, shape, dt=F32):
            t = place(name, shape, dt, work[0])
            work[0] += -(-int(np.prod(shape[1:])) * (2 if dt == F16 else 4) // 32) * 32
            return t
        blk = [P, CHUNKS, P]
        qn = head_buf("qn", blk)
        kn, qT, kT = ([head_buf(f"{name}{s}", blk) for s in range(2)] for name in ("kn", "qT", "kT"))
        QKT = [[head_buf(f"QKT{s}{r}", blk) for r in range(2)] for s in range(2)]
        DT = [head_buf(f"DT{r}", blk) for r in range(2)]
        YF = [head_buf(f"YF{r}", blk) for r in range(2)]
        NAh = [head_buf(f"NAh{r}", blk, F16) for r in range(2)]
        NAT, NAl, V, TMP, X, Y = ([], [], [], [], [], [])
        for r in range(2):
            at = work[0]
            NAl.append(head_buf(f"NAl{r}", blk, F16))
            V.append(head_buf(f"V{r}", blk, F16))
            NAT.append(place(f"NAT{r}", blk, F32, at))
            at = work[0]
            X.append(head_buf(f"X{r}", blk, F16))
            Y.append(head_buf(f"Y{r}", blk, F16))
            TMP.append(place(f"TMP{r}", blk, F32, at))
        S = [[head_buf(f"S{r}{odd}", [P, P]) for odd in range(2)] for r in range(2)]
        R = [head_buf(f"R{r}", [P, P]) for r in range(2)]
        VN = [head_buf(f"VN{r}", [P, P]) for r in range(2)]
        VS = [head_buf(f"VS{r}", [P, P]) for r in range(2)]
        O1 = [head_buf(f"O1{r}", [P, P]) for r in range(2)]
        OT = [head_buf(f"OT{r}", [P, P]) for r in range(2)]
        ht = [head_buf(f"ht{s}", [P, 6, 2, CHUNKS]) for s in range(2)]
        egl = [[head_buf(f"egl{s}{r}", [P, CHUNKS]) for r in range(2)] for s in range(2)]
        bdl = [[head_buf(f"bdl{s}{r}", [P, CHUNKS]) for r in range(2)] for s in range(2)]
        assert work[0] <= big + 112 * KB

        ozh = place("ozh", [P, KT, SEQ], F32R, big + 64 * KB)
        ozl = place("ozl", [P, KT, SEQ], F32R, big + 80 * KB)
        on = [place(f"on{s}", blk, F32, big + (96 + s * 2) * KB) for s in range(2)]
        zs = [place(f"zs{s}", [P, SEQ], F32, big + (100 + s * 2) * KB) for s in range(2)]
        oz = [place(f"oz{s}", [P, SEQ], F32, big + (104 + s * 2) * KB) for s in range(2)]
        gate_a = raw[:, HEADS:2 * HEADS, :, :].rearrange("p u c t -> p u (c t)")

        gate_b = place("gate_b", [P, KT, SEQ], F32, big)
        o_sw = place("o_sw", [P, CHUNKS, D], F32, big + 32 * KB)
        kv = place("kv", [P, CHUNKS, 512], F32, big + 48 * KB)
        rope = [[place(f"rope{s}{n}", [P, CHUNKS, 2, HD // 2], F32, big + (112 + s * 4 + n) * KB) for n in range(4)]
                for s in range(2)]
        qg = place("qg", [P, CHUNKS, GQ * HD], F32, big + 112 * KB)
        kg = place("kg", [P, CHUNKS, 2, HD], F32, big + 116 * KB)
        qgT = place("qgT", [P, GQ // 2, SEQ], F32, big + 56 * KB)
        kgT = place("kgT", [P, 2, SEQ], F32, big + 60 * KB)
        pr = place("pr", [P, GQ, 3, P], F32, big + 98 * KB)
        pT = place("pT", [P, 3, 512], F32, big + 104 * KB)
        mx, mn, es, den, rd = (place(f"att_{n}", [P, GQ], F32, big + 110 * KB + 32 * n) for n in range(5))
        swh = place("swh", [P, KT, SEQ], F32R, big + 48 * KB)
        swl = place("swl", [P, KT, SEQ], F32R, big + 96 * KB)

        mgh = place("mgh", [P, KT, SEQ], F32R, big + 32 * KB)
        mgl = place("mgl", [P, KT, SEQ], F32R, big + 16 * KB)

        yT_a = place("yT_a", [P, KT, SEQ], F32, big + 64 * KB)
        yT_b = place("yT_b", [P, KT, SEQ], F32, big)
        ln_g = place("ln_g", [P, D], F32, big + 112 * KB)
        ln_b = place("ln_b", [P, D], F32, big + 116 * KB)
        xf = [place(f"xf{s}", [P, SEQ], F32, big + (104 + 2 * s) * KB) for s in range(3)]
        hh = place("hh", [P, FT, SEQ], F32R, big)
        hl = place("hl", [P, FT, SEQ], F32R, big + 44 * KB)
        sg = [place(f"sg{s}", [P, SEQ], F32, big + (96 + 2 * s) * KB) for s in range(2)]
        hf = [place(f"hf{s}", [P, SEQ], F32, big + (100 + 2 * s) * KB) for s in range(2)]
        assert big + 120 * KB <= nc.sbuf_usable_end, (big + 120 * KB, nc.sbuf_usable_end)

        ident = cst[:, C_ID:C_ID + P]
        ones = cst[:, C_ONES:C_ONES + P]
        tri = [cst[:, C_TRIF:C_TRIF + P], cst[:, C_TRIB:C_TRIB + P]]
        low = [cst[:, C_LOW + n * P:C_LOW + (n + 1) * P] for n in range(len(LEVELS))]
        up = [cst[:, C_UP + n * P:C_UP + (n + 1) * P] for n in range(len(LEVELS))]
        x_mask = [low, up]
        y_mask = [up, low]

        def rows(ap):
            return ap.unsqueeze(1).broadcast_to([P, CHUNKS, P])

        def cols(ap, n=P):
            return ap.unsqueeze(2).broadcast_to([P, ap.shape[1], n])

        BLOCK_LEVELS = (5, 6)

        def new_blocks(lev, upper):
            size = 1 << lev
            pairs = [(slice(at, at + size), slice(at + size, at + 2 * size)) for at in range(0, P, 2 * size)]
            return pairs if upper else [(b, a) for a, b in pairs]

        small_loaded = sem("small_loaded")
        settled = sem("settled")
        loaded = [sem(f"loaded{s}") for s in range(2)]
        split_done = [sem(f"split_done{s}") for s in range(2)]
        unit_done = [sem(f"unit_done{s}") for s in range(2)]
        w_hi_done = [sem(f"w_hi_done{s}") for s in range(2)]
        gate_pre = sem("gate_pre")
        on_used = [sem(f"on_used{s}") for s in range(2)]
        stage_done = sem("stage_done")
        ready_bf = sem("ready_bf")
        x_t = sem("x_t")
        x_hi = sem("x_hi")
        x_lo = sem("x_lo")
        conv_loaded = [sem(f"conv_loaded{s}") for s in range(2)]
        conv_step = [sem(f"conv_step{s}") for s in range(2)]
        conv_silu = [sem(f"conv_silu{s}") for s in range(2)]
        tok_ready = [sem(f"tok_ready{s}") for s in range(2)]
        tok_stored = sem("tok_stored")
        xf_act = sem("xf_act")
        xf_dve = sem("xf_dve")
        ba_loaded = sem("ba_loaded")
        ba_hi = sem("ba_hi")
        ba_lo = sem("ba_lo")
        ba_mm = sem("ba_mm")
        baT_ready = sem("baT_ready")
        cum_mm = sem("cum_mm")
        gate_dve = sem("gate_dve")
        gate_act = sem("gate_act")
        head_cols = sem("head_cols")
        qk_normed = sem("qk_normed")
        qk_turned = sem("qk_turned")
        qT_ready = sem("qT_ready")
        kT_ready = sem("kT_ready")
        g_tri = sem("g_tri")
        g_rows = sem("g_rows")
        decay_done = sem("decay_done")
        kk_done = sem("kk_done")
        kq_done = sem("kq_done")
        beta_decay = sem("beta_decay")
        bdl_done = sem("bdl_done")
        nat_raw = sem("nat_raw")
        nat_done = sem("nat_done")
        na_hi = sem("na_hi")
        na_lo = sem("na_lo")
        e_mm = [sem(f"e_mm{r}") for r in range(2)]
        e_ready = [sem(f"e_ready{r}") for r in range(2)]
        y_fix = [sem(f"y_fix{r}") for r in range(2)]
        y_done = [sem(f"y_done{r}") for r in range(2)]
        extra_out = [sem(f"extra_out{s}") for s in range(2)]
        qkt_done = sem("qkt_done")
        na_turned = sem("na_turned")
        x_upd = [sem(f"x_upd{r}") for r in range(2)]
        y_upd = [sem(f"y_upd{r}") for r in range(2)]
        v_mm = [sem(f"v_mm{r}") for r in range(2)]
        v_ready = [sem(f"v_ready{r}") for r in range(2)]
        xv_mm = [sem(f"xv_mm{r}") for r in range(2)]
        vx_mm = [sem(f"vx_mm{r}") for r in range(2)]
        ks_mm = [sem(f"ks_mm{r}") for r in range(2)]
        r_ready = [sem(f"r_ready{r}") for r in range(2)]
        tr_mm = [sem(f"tr_mm{r}") for r in range(2)]
        o1_ready = [sem(f"o1_ready{r}") for r in range(2)]
        vn_ready = [sem(f"vn_ready{r}") for r in range(2)]
        vs_ready = [sem(f"vs_ready{r}") for r in range(2)]
        o_mm = [sem(f"o_mm{r}") for r in range(2)]
        st_mm = [sem(f"st_mm{r}") for r in range(2)]
        o_out = [sem(f"o_out{r}") for r in range(2)]
        s_ready = [sem(f"s_ready{r}") for r in range(2)]
        o_sum = sem("o_sum")
        o_ss = sem("o_ss")
        rno_dve = sem("rno_dve")
        rno_act = sem("rno_act")
        on_ready = [sem(f"on_ready{s}") for s in range(2)]
        on_turned = [sem(f"on_turned{s}") for s in range(2)]
        z_silu = [sem(f"z_silu{s}") for s in range(2)]
        oz_ready = [sem(f"oz_ready{s}") for s in range(2)]
        gate_b_out = sem("gate_b_out")
        oz_hi = [sem(f"oz_hi{s}") for s in range(2)]
        oz_lo = [sem(f"oz_lo{s}") for s in range(2)]
        sw_act = sem("sw_act")
        sw_dve = sem("sw_dve")
        rope_mul = sem("rope_mul")
        rope_half = sem("rope_half")
        qg_copied = sem("qg_copied")
        qg_turned = sem("qg_turned")
        qgT_act = sem("qgT_act")
        qgT_dve = sem("qgT_dve")
        scores = sem("scores")
        stats_step = sem("stats_step")
        probs = sem("probs")
        den_step = sem("den_step")
        qs_mm = [sem(f"qs_mm{r}") for r in range(2)]
        sink_exp = sem("sink_exp")
        p_turned = sem("p_turned")
        pT_act = sem("pT_act")
        pT_dve = sem("pT_dve")
        pv_mm = sem("pv_mm")
        o_scaled = sem("o_scaled")
        osw_t = sem("osw_t")
        osw_hi = sem("osw_hi")
        osw_lo = sem("osw_lo")
        gate_sig = sem("gate_sig")
        mg_mul = sem("mg_mul")
        mg_sum = sem("mg_sum")
        mg_hi = sem("mg_hi")
        mg_lo = sem("mg_lo")
        ln_loaded = sem("ln_loaded")
        y_mm = sem("y_mm")
        yT_act = sem("yT_act")
        yT_dve = sem("yT_dve")
        y_turned = sem("y_turned")
        ln_dve = sem("ln_dve")
        ln_sqrt = sem("ln_sqrt")
        ff_silu = sem("ff_silu")
        ff_h = sem("ff_h")
        ff_hi = sem("ff_hi")
        ff_lo = sem("ff_lo")
        stored = sem("stored")

        def settle(eng):
            eng.sem_inc(settled, 1)

        def stage_end(eng, l, n):
            settle(eng)
            eng.drain().then_inc(stage_done, 1)
            eng.wait_ge(stage_done, (l * BARRIERS + n) * 3 + 3)
            settle(eng)

        block = ctx.enter_context(nc.Block())

        @block.sync
        def _(sp):
            for dst, src in ((x[:], x_in), (cst[:], consts), (cw[:], conv_w), (dn_w[:], dn_norm), (ln_c[:], ln_cols),
                             (exp_a[:], a_log.partition_broadcast(P)), (dtb[:], dt_bias.partition_broadcast(P)),
                             (snk[:], sinks.partition_broadcast(P))):
                sp.dma_start(dst, src).then_inc(small_loaded, 16)
            with sp.Fori(0, DEPTH) as l:
                sp.dma_start(ba_raw[:], w_ba[l, :, :, :]).then_inc(ba_loaded, 16)
                with sp.Fori(0, PAIRS) as i:
                    for s in range(2):
                        sp.wait_ge(split_done[s], l * PAIRS + i + 1)
                        sp.dma_start(w_raw[s][:], stream[l, i, s, :, :]).then_inc(loaded[s], 16)
            for c in range(CHUNKS):
                sp.wait_ge(ln_dve, DEPTH * 2 * LN_STEPS - (CHUNKS - 1 - c))
                sp.dma_start(out[:, c, :], x[:, c, :]).then_inc(stored, 16)
            sp.wait_ge(stored, CHUNKS * 16)

        @block.gpsimd
        def _(pool):
            for s in range(2):
                pool.sem_inc(split_done[s], 1)
            with pool.Fori(0, DEPTH) as l:
                pool.wait_ge(ba_loaded, l * 16 + 16)
                settle(pool)
                flat = [t[:].rearrange("p k n -> p (k n)") for t in (ba_raw, bah, bal)]
                nc.gpsimd.tensor_scalar(flat[1], flat[0], 1.0, 1.0, ALU.mult, ALU.mult).then_inc(ba_hi, 1)
                pool.wait_ge(ba_hi, l + 1)
                nc.gpsimd.tensor_tensor(flat[2], flat[0], flat[1].bitcast(F32), ALU.subtract).then_inc(ba_lo, 1)
                with pool.Fori(0, PAIRS) as i:
                    p = l * PAIRS + i
                    for s in range(2):
                        pool.wait_ge(loaded[s], p * 16 + 16)
                        pool.wait_ge(unit_done[s], p + 1)
                        settle(pool)
                        nc.gpsimd.tensor_scalar(wh[s][:], w_raw[s][:], 1.0, 1.0, ALU.mult,
                                                ALU.mult).then_inc(w_hi_done[s], 1)
                        pool.wait_ge(w_hi_done[s], p + 1)
                        nc.gpsimd.tensor_tensor(wl[s][:], w_raw[s][:], wh[s][:].bitcast(F32),
                                                ALU.subtract).then_inc(split_done[s], 1)

        @block.tensor
        def _(pe):
            mm = nc.tensor.matmul

            def unit_ready(pair, s):
                pe.wait_ge(split_done[s], pair + 2)

            def product(o, ah, al, bh, bl, first, last):
                mm(o, ah, bh, start=first, stop=False)
                mm(o, al, bh, start=False, stop=False)
                return mm(o, ah, bl, start=False, stop=last)

            def feature_unit(s, bank, bh, bl, lo_count=None):
                for k in range(KT):
                    if lo_count is not None:
                        pe.wait_ge(x_lo, lo_count + k + 1)
                    c = slice(k * P, (k + 1) * P)
                    ins = product(PS[:, bank, :], wh[s][:, c], wl[s][:, c], bh[:, k, :], bl[:, k, :],
                                  k == 0, k == KT - 1)
                ins.then_inc(unit_done[s], 1)

            def turn_to_features(src, turned):
                for k in range(KT):
                    for c in range(CHUNKS):
                        ins = nc.tensor.transpose(PS[:, k, c * P:(c + 1) * P], src[:, c, k * P:(k + 1) * P], ident)
                    ins.then_inc(turned, 1)

            def down_units(l, first_pair, npairs, bh, bl):
                def pair_of(i, first, last):
                    for s in range(2):
                        unit_ready(l * PAIRS + first_pair + i, s)
                        k = i * 2 + s
                        for d in range(KT):
                            c = slice(d * P, (d + 1) * P)
                            ins = product(PS[:, d, :], wh[s][:, c], wl[s][:, c],
                                          bh[:, bass.ds(k, 1), :].rearrange("p a t -> p (a t)"),
                                          bl[:, bass.ds(k, 1), :].rearrange("p a t -> p (a t)"),
                                          first and s == 0, last and s == 1)
                        ins.then_inc(unit_done[s], 1)
                pair_of(0, True, False)
                with pe.Fori(1, npairs - 1) as i:
                    pair_of(i, False, False)
                pair_of(npairs - 1, False, True)

            def turn_back(l, src, n):
                for c in range(CHUNKS):
                    for half in range(2):
                        if c == 0:
                            pe.wait_ge(yT_act, (l * 2 + n) * 4 + 2 * half + 2)
                            pe.wait_ge(yT_dve, (l * 2 + n) * 4 + 2 * half + 2)
                        for j in range(4):
                            ins = nc.tensor.transpose(PS[:, c * 2 + half, j * P:(j + 1) * P],
                                                      src[:, half * 4 + j, c * P:(c + 1) * P], ident)
                    ins.then_inc(y_turned, 1)

            def turn_normed(l, n):
                for c in range(CHUNKS):
                    pe.wait_ge(ln_dve, (l * 2 + n) * LN_STEPS + LN_NORMED[c])
                    for k in range(KT):
                        ins = nc.tensor.transpose(PS[:, k, c * P:(c + 1) * P], x[:, c, k * P:(k + 1) * P], ident)
                        if c == CHUNKS - 1:
                            ins.then_inc(x_t, 1)

            pe.sem_inc(unit_done[0], 1)
            pe.sem_inc(unit_done[1], 1)
            pe.wait_ge(small_loaded, 16 * SMALL)
            pe.wait_ge(ready_bf, 7)
            turn_to_features(x, x_t)
            with pe.Fori(0, DEPTH) as l:
                pe.wait_ge(ba_lo, l + 1)
                for k in range(KT):
                    pe.wait_ge(x_lo, l * 16 + max(k + 1, 2))
                    ins = product(PS[0:32, 1, :], bah[:, k, :], bal[:, k, :], xh[:, k, :], xl[:, k, :],
                                  k == 0, k == KT - 1)
                ins.then_inc(ba_mm, 1)

                def qkv_unit(i, s):
                    unit_ready(l * PAIRS + AT_QKV + i, s)
                    feature_unit(s, s, xh, xl)

                def qkv_turn(i, s):
                    pe.wait_ge(conv_silu[s], l * 12 + i + 1)
                    for c in range(CHUNKS):
                        ins = nc.tensor.transpose(PS[:, 2 + s, c * P:(c + 1) * P],
                                                  conv_act[s][:, c * P:(c + 1) * P], ident)
                    ins.then_inc(tok_ready[s], 1)
                qkv_unit(0, 0)
                pe.wait_ge(baT_ready, l + 1)
                settle(pe)
                for c in range(CHUNKS):
                    ins = nc.tensor.transpose(PS[:, 5, c * 32:(c + 1) * 32], baT[:, c * P:(c + 1) * P],
                                              ident[0:32, 0:32])
                ins.then_inc(ba_mm, 1)
                qkv_unit(0, 1)
                pe.wait_ge(gate_dve, l * 19 + 10)
                for r in range(2):
                    ins = mm(PS[:, 4, r * 32:(r + 1) * 32].rearrange("p (c h) -> p c h", c=CHUNKS), tri[r],
                             sm[8][:, :, r * 8:(r + 1) * 8], start=True, stop=True)
                ins.then_inc(cum_mm, 1)
                with pe.Fori(1, U_QKV // 2) as i:
                    for s in range(2):
                        pe.wait_ge(conv_loaded[s], l * 12 + i)
                        qkv_unit(i, s)
                        qkv_turn(i - 1, s)
                for s in range(2):
                    qkv_turn(U_QKV // 2 - 1, s)
                stage_end(pe, l, 0)

                def extra(n, h, j):
                    s, k = divmod(j, KT)
                    if k == 0:
                        unit_ready(l * PAIRS + AT_DELTA + h, s)
                        pe.wait_ge(extra_out[s], n + 1)
                    c = slice(k * P, (k + 1) * P)
                    ins = product(PS[:, 6 + s, :], wh[s][:, c], wl[s][:, c], xh[:, k, :], xl[:, k, :],
                                  k == 0, k == KT - 1)
                    if k == KT - 1:
                        ins.then_inc(unit_done[s], 1)

                def front_turn(m, t):
                    for b, src in ((4, qn), (5, kn[t])):
                        pe.wait_ge(qk_normed, m * 2 + b - 3)
                        for c in range(CHUNKS):
                            ins = nc.tensor.transpose(PS[:, b, c * P:(c + 1) * P], src[:, c, :], ident)
                        ins.then_inc(qk_turned, 1)

                def front_rows(m, r):
                    pe.wait_ge(qT_ready, m + 1)
                    pe.wait_ge(kT_ready, m + 1)
                    pe.wait_ge(g_tri, m * 2 + r + 1)
                    mm(PS[:, 4 + r, :], ones, TMP[r][:].rearrange("p c t -> p (c t)"), start=True, stop=False)
                    mm(PS[:, 4 + r, :].rearrange("p (c t) -> p c t", c=CHUNKS), id_bf[:], rows(neg_bf[r][:]),
                       start=False, stop=True).then_inc(g_rows, 1)

                def front_products(m, t, b):
                    pe.wait_ge(decay_done, m * 2 + b - 3)
                    src, done = (kT[t], kk_done) if b == 4 else (qT[t], kq_done)
                    for c in range(CHUNKS):
                        ins = mm(PS[:, b, c * P:(c + 1) * P], kT[t][:, c, :], src[:, c, :], start=True, stop=True)
                    ins.then_inc(done, 1)

                def front_back(m, r):
                    pe.wait_ge(nat_done if r == 0 else qkt_done, m * 2 + 2)
                    for c in range(CHUNKS):
                        ins = nc.tensor.transpose(PS[:, 4 + r, c * P:(c + 1) * P], NAT[r][:, c, :], ident)
                    ins.then_inc(na_turned, 1)

                def head(h, s, more):
                    n = l * HEADS + h
                    for lev in range(1, 7):
                        for r in range(2):
                            if lev == 1:
                                pe.wait_ge(na_hi, n * 2 + r + 1)
                            pe.wait_ge(y_upd[r], n * 7 + lev)
                            for c in range(CHUNKS):
                                ins = mm(PS[:, 3 * r, c * P:(c + 1) * P], NAh[r][:, c, :], Y[r][:, c, :],
                                         start=True, stop=True)
                            ins.then_inc(v_mm[r], 1)
                        extra(n, h, lev - 1)
                        for r in range(2):
                            if lev == 1 and r == 1:
                                pe.wait_ge(na_lo, n * 2 + 2)
                            pe.wait_ge(v_ready[r], n * 6 + lev)
                            pe.wait_ge(x_upd[r], n * 7 + lev)
                            for c in range(CHUNKS):
                                ins = mm(PS[:, 3 * r + 1, c * P:(c + 1) * P], X[r][:, c, :], V[r][:, c, :],
                                         start=True, stop=True)
                            ins.then_inc(xv_mm[r], 1)
                            alone = lev in BLOCK_LEVELS
                            if not alone:
                                mm(PS[:, 3 * r + 2, :], id_16[:], X[r][:].rearrange("p c t -> p (c t)"), start=True,
                                   stop=False, skip_group_check=True)
                            for c in range(CHUNKS):
                                ins = mm(PS[:, 3 * r + 2, c * P:(c + 1) * P], V[r][:, c, :], X[r][:, c, :],
                                         start=alone, stop=True, skip_group_check=True)
                            ins.then_inc(vx_mm[r], 1)
                    for r in range(2):
                        pe.wait_ge(y_upd[r], n * 7 + 7)
                        mm(PS[:, 3 * r, :], minus_two[:], Y[r][:].rearrange("p c t -> p (c t)"), start=True,
                           stop=False, skip_group_check=True)
                        for c in range(CHUNKS):
                            o = PS[:, 3 * r, c * P:(c + 1) * P]
                            mm(o, id_16[:], id_16[:], start=False, stop=False, skip_group_check=True)
                            mm(o, NAh[r][:, c, :], Y[r][:, c, :], start=False, stop=False, skip_group_check=True)
                            ins = mm(o, NAl[r][:, c, :], Y[r][:, c, :], start=False, stop=True,
                                     skip_group_check=True)
                        ins.then_inc(e_mm[r], 1)
                    extra(n, h, 6)
                    if more:
                        pe.wait_ge(x_upd[1], n * 7 + 7)
                        front_turn(n + 1, 1 - s)
                    extra(n, h, 7)
                    for r in range(2):
                        pe.wait_ge(e_ready[r], n + 1)
                        pe.wait_ge(x_upd[r], n * 7 + 7)
                        for c in range(CHUNKS):
                            ins = mm(PS[:, 3 * r, c * P:(c + 1) * P], X[r][:, c, :], V[r][:, c, :],
                                     start=True, stop=True)
                        ins.then_inc(y_fix[r], 1)
                    for r in range(2):
                        pe.wait_ge(y_done[r], n + 1)
                    def within_chunk(step):
                        for r in range(2):
                            c = step if r == 0 else CHUNKS - 1 - step
                            pe.wait_ge(vn_ready[r], n * 4 + step + 1)
                            if step > 0:
                                pe.wait_ge(o1_ready[r], n * 3 + step)
                            mm(PS[:, 2 + r, P:2 * P], QKT[s][r][:, c, :], VN[r][:], start=True,
                               stop=True).then_inc(o_mm[r], 1)
                    for step in range(CHUNKS):
                        chunk = (step, CHUNKS - 1 - step)
                        if step > 0:
                            for r in range(2):
                                pe.wait_ge(s_ready[r], n * 3 + step)
                                mm(PS[:, r, 0:P], kT[s][:, chunk[r], :], S[r][(step - 1) % 2][:], start=True,
                                   stop=True).then_inc(ks_mm[r], 1)
                            within_chunk(step - 1)
                        for r in range(2):
                            if step == 0:
                                right = raw[:, bass.ds(h + 2 * HEADS, 1), chunk[r], :].rearrange("p a t -> p (a t)")
                            else:
                                pe.wait_ge(r_ready[r], n * 3 + step)
                                right = R[r][:]
                            mm(PS[:, r, 2 * P:3 * P], YF[r][:, chunk[r], :], right, start=True,
                               stop=True).then_inc(tr_mm[r], 1)
                        if step == 0 or not more:
                            extra(n, h, 8 + step)
                        elif step == 1:
                            front_rows(n + 1, 1)
                        elif step == 2:
                            front_products(n + 1, 1 - s, 4)
                        if step < CHUNKS - 1:
                            for r in range(2):
                                pe.wait_ge(vs_ready[r], n * 3 + step + 1)
                                mm(PS[:, r, P:2 * P], kn[s][:, chunk[r], :], VS[r][:], start=True,
                                   stop=True).then_inc(st_mm[r], 1)
                        if step > 0:
                            for r in range(2):
                                pe.wait_ge(o_out[r], n * 4 + step)
                                mm(PS[:, 2 + r, 0:P], qT[s][:, chunk[r], :], S[r][(step - 1) % 2][:], start=True,
                                   stop=True).then_inc(qs_mm[r], 1)
                        if more and step == 0:
                            front_rows(n + 1, 0)
                        if more and step == 2:
                            front_products(n + 1, 1 - s, 5)
                    if more:
                        for j in (9, 10, 11):
                            extra(n, h, j)
                    within_chunk(CHUNKS - 1)
                    extra(n, h, 12)
                    if more:
                        front_back(n + 1, 0)
                    extra(n, h, 13)
                    if more:
                        front_back(n + 1, 1)
                    extra(n, h, 14)
                    extra(n, h, 15)
                    for r in range(2):
                        pe.wait_ge(o_out[r], n * 4 + 4)
                    settle(pe)
                front_turn(l * HEADS, 0)
                for r in range(2):
                    front_rows(l * HEADS, r)
                for b in (4, 5):
                    front_products(l * HEADS, 0, b)
                front_back(l * HEADS, 0)
                front_back(l * HEADS, 1)
                with pe.Fori(0, HEADS // 2 - 1) as i:
                    head(i * 2, 0, True)
                    head(i * 2 + 1, 1, True)
                head(HEADS - 2, 0, True)
                head(HEADS - 1, 1, False)
                stage_end(pe, l, 1)

                def turn_output(i, s):
                    pe.wait_ge(oz_ready[s], l * 4 + i + 1)
                    pe.wait_ge(on_ready[s], l * 4 + i + 1)
                    for c in range(CHUNKS):
                        ins = nc.tensor.transpose(PS[:, 4 + s, c * P:(c + 1) * P], on[s][:, c, :], ident)
                    ins.then_inc(on_turned[s], 1)

                def window_columns(b, turn):
                    pe.wait_ge(sw_act, (l * 3 + b) * 2 + 1)
                    pe.wait_ge(sw_dve, (l * 3 + b) * 2 + 1)
                    for u in range(KT // 2):
                        s = u % 2
                        unit_ready(l * PAIRS + AT_SW + b * 2 + u // 2, s)
                        for j in range(2):
                            k = u * 2 + j
                            for c in range(CHUNKS):
                                t = slice(c * P, (c + 1) * P)
                                w = slice(j * 512, (j + 1) * 512)
                                ins = product(PS[:, c, :], xh[:, k, t], xl[:, k, t], wh[s][:, w], wl[s][:, w],
                                              k == 0, k == KT - 1)
                            if turn and j == 0:
                                turn_output(b * 2 + u // 2, s)
                        ins.then_inc(unit_done[s], 1)
                with pe.Fori(0, 2) as b:
                    window_columns(b, True)
                window_columns(2, False)
                stage_end(pe, l, 2)

                def turn_group(n):
                    pe.wait_ge(qg_copied, n * 3 + 3)
                    for j in range(GQ // 2):
                        for c in range(CHUNKS):
                            ins = nc.tensor.transpose(PS[:, j, c * P:(c + 1) * P], qg[:, c, j * P:(j + 1) * P], ident)
                        ins.then_inc(qg_turned, 1)
                    for c in range(CHUNKS):
                        ins = nc.tensor.transpose(PS[:, 2, c * P:(c + 1) * P],
                                                  kg[:, c, :, :].rearrange("p a k -> p (a k)"), ident)
                    ins.then_inc(qg_turned, 1)

                def score(b):
                    lo, hi = max(b - 1, 0), min(b + 2, CHUNKS)
                    for j in range(hi - lo):
                        masked = lo + j != b
                        for q in range(GQ):
                            ins = mm(PS[:, j, q * P:(q + 1) * P], qgT[:, q // 2, b * P:(b + 1) * P],
                                     kgT[:, q % 2, (lo + j) * P:(lo + j + 1) * P], start=q == 0, stop=not masked,
                                     skip_group_check=True)
                        if masked:
                            mask = neg_bf[0 if lo + j < b else 1]
                            ins = mm(PS[:, j, :].rearrange("p (q t) -> p q t", q=GQ), id_bf[:], rows(mask[:]),
                                     start=False, stop=True, skip_group_check=True)
                    ins.then_inc(scores, 1)

                def first_score(n):
                    pe.wait_ge(qgT_act, n * 2 + 2)
                    pe.wait_ge(qgT_dve, n * 2 + 2)
                    settle(pe)
                    score(0)

                def group(g, more):
                    n = l * GROUPS + g

                    def extra_gate(j):
                        s, k = divmod(j, KT)
                        if k == 0:
                            unit_ready(l * PAIRS + AT_ATT + g, s)
                            pe.wait_ge(gate_b_out, n * 2 + s + 1)
                        c = slice(k * P, (k + 1) * P)
                        ins = product(PS[:, 3, :], wh[s][:, c], wl[s][:, c], xh[:, k, :], xl[:, k, :],
                                      k == 0, k == KT - 1)
                        if k == KT - 1:
                            ins.then_inc(unit_done[s], 1)
                    for j in range(4):
                        extra_gate(j)
                    for b in range(CHUNKS):
                        lo, hi = max(b - 1, 0), min(b + 2, CHUNKS)
                        pe.wait_ge(probs, n * 16 + b * 4 + 4)
                        settle(pe)
                        if b < CHUNKS - 1:
                            score(b + 1)
                        elif more:
                            turn_group(n + 1)
                        for j in range(hi - lo):
                            for q in range(GQ):
                                ins = nc.tensor.transpose(PS[:, 4 + j, q * P:(q + 1) * P], pr[:, q, j, :], ident)
                        ins.then_inc(p_turned, 1)
                        extra_gate(4 + 2 * b)
                        extra_gate(5 + 2 * b)
                        pe.wait_ge(pT_act, n * 4 + b + 1)
                        pe.wait_ge(pT_dve, n * 4 + b + 1)
                        if b > 0:
                            pe.wait_ge(o_scaled, n * 4 + b)
                        for q in range(GQ):
                            for j in range(hi - lo):
                                v = kv[:, lo + j, bass.ds(256 + g * HD, HD)]
                                ins = mm(PS[:, 7, q * HD:(q + 1) * HD], pT[:, j, q * P:(q + 1) * P], v,
                                         start=j == 0, stop=j == hi - lo - 1)
                        ins.then_inc(pv_mm, 1)
                    for j in range(12, 16):
                        extra_gate(j)
                    if more:
                        first_score(n + 1)
                    pe.wait_ge(o_scaled, n * 4 + 4)
                    settle(pe)
                turn_group(l * GROUPS)
                first_score(l * GROUPS)
                with pe.Fori(0, GROUPS - 1) as g:
                    group(g, True)
                group(GROUPS - 1, False)
                pe.wait_ge(gate_b_out, (l + 1) * KT + 1)
                turn_to_features(o_sw, osw_t)
                stage_end(pe, l, 3)

                with pe.Fori(0, KT // 2) as i:
                    for j in range(2):
                        pe.wait_ge(mg_mul, (l * 4 + i) * 4 + 2 * j + 2)
                        pair = l * PAIRS + AT_MERGE + i * 2 + j
                        unit_ready(pair, 0)
                        feature_unit(0, 2 * j, ozh, ozl)
                        unit_ready(pair, 1)
                        feature_unit(1, 2 * j + 1, swh, swl)
                stage_end(pe, l, 4)

                down_units(l, AT_OUT, U_OUT // 2, mgh, mgl)
                pe.drain().then_inc(y_mm, 1)
                turn_back(l, yT_a, 0)
                stage_end(pe, l, 5)
                turn_normed(l, 0)

                with pe.Fori(0, FT // 2) as i:
                    for j in range(2):
                        pair = l * PAIRS + AT_GU + i * 2 + j
                        pe.wait_ge(ff_h, (l * 11 + i) * 2 + j + 1)
                        for s in range(2):
                            unit_ready(pair, s)
                            feature_unit(s, 2 * j + s, xh, xl, l * 16 + 8 if j == s == 0 else None)
                pe.wait_ge(ff_lo, (l + 1) * FT)
                settle(pe)
                down_units(l, AT_DOWN, U_DOWN // 2, hh, hl)
                pe.drain().then_inc(y_mm, 1)
                turn_back(l, yT_b, 1)
                stage_end(pe, l, 6)
                turn_normed(l, 1)

        @block.scalar
        def _(act):
            A = nc.scalar.activation

            def unit_full(pair, s):
                act.wait_ge(unit_done[s], pair + 2)

            def store_hi(turned, base_count, hi, done):
                for k in range(KT):
                    act.wait_ge(turned, base_count + k + 1)
                    nc.scalar.copy(hi[:, k, :], PS[:, k, :]).then_inc(done, 1)

            def store_normed(l, n):
                m = l * 2 + n

                def scaled(k):
                    act.wait_ge(x_t, m * 8 + 8 + k + 1)
                    act.wait_ge(x_lo, m * 8 + 8 + k - 2)
                    gain, offset = (ln_c[:, bass.ds(m, 1), j, k].rearrange("p a -> p a") for j in range(2))
                    A(xf[k % 3][:], PS[:, k, :], ACT.Identity, bias=offset, scale=gain).then_inc(xf_act, 1)

                def high_part(k):
                    act.wait_ge(xf_dve if k % 2 else xf_act, m * 4 + k // 2 + 1)
                    nc.scalar.copy(xh[:, k, :], xf[k % 3][:]).then_inc(x_hi, 1)
                scaled(0)
                scaled(2)
                high_part(0)
                high_part(1)
                high_part(2)
                scaled(4)
                high_part(3)
                scaled(6)
                for k in range(4, KT):
                    high_part(k)

            act.wait_ge(small_loaded, 16 * SMALL)
            A(exp_a[:], exp_a[:], ACT.Exp).then_inc(ready_bf, 1)
            act.sem_inc(sw_act, 1)
            act.sem_inc(gate_b_out, 1)
            act.sem_inc(tok_stored, 1)
            for s in range(2):
                act.sem_inc(extra_out[s], 1)
            store_hi(x_t, 0, xh, x_hi)
            with act.Fori(0, DEPTH) as l:
                act.wait_ge(ba_mm, l * 2 + 1)
                A(baT[:], PS[0:32, 1, :], ACT.Copy).then_inc(baT_ready, 1)
                act.wait_ge(gate_dve, l * 19 + 4)
                A(sm[3][:], sm[2][:], ACT.Exp).then_inc(gate_act, 1)
                act.wait_ge(gate_dve, l * 19 + 5)
                A(sm[5][:], sm[4][:], ACT.Ln).then_inc(gate_act, 1)
                A(sm[9][:], ba[:, :, 0:16], ACT.Sigmoid).then_inc(gate_act, 1)
                act.wait_ge(gate_dve, l * 19 + 13)
                A(tab[:, :, T_EG].rearrange("p h r c -> p h (r c)"),
                  tab[:, :, T_NEG_CUM].rearrange("p h r c -> p h (r c)"), ACT.Exp, scale=-1.0).then_inc(gate_act, 1)

                def conv_load(i, s):
                    unit_full(l * PAIRS + AT_QKV + i, s)
                    nc.scalar.copy(conv_in[s][:, 2:2 + SEQ], PS[:, s, :]).then_inc(conv_loaded[s], 1)

                def conv_activate(i, s):
                    act.wait_ge(conv_step[s], (l * 12 + i) * 5 + 5)
                    A(conv_act[s][:], conv_acc[s][:], ACT.Silu).then_inc(conv_silu[s], 1)

                def keep_tokens(i, s, squares):
                    act.wait_ge(tok_ready[s], l * 12 + i + 1)
                    if squares:
                        act.wait_ge(tok_stored, l * U_QKV + i * 2 + s + 1)
                        for c in range(CHUNKS):
                            A(sq[:, c, :], PS[:, 2 + s, c * P:(c + 1) * P], ACT.Square,
                              accum_out=rn[:, bass.ds(i * 2 + s, 1), c].rearrange("p a -> p a"))
                    nc.scalar.copy(raw[:, bass.ds(i * 2 + s, 1), :, :].rearrange("p a c t -> p (a c t)"),
                                   PS[:, 2 + s, :]).then_inc(tok_stored, 1)
                for s in range(2):
                    conv_load(0, s)
                    conv_activate(0, s)
                for first, end, squares in ((1, HEADS + 1, True), (HEADS + 1, U_QKV // 2, False)):
                    with act.Fori(first, end) as i:
                        for s in range(2):
                            conv_load(i, s)
                            keep_tokens(i - 1, s, squares)
                            conv_activate(i, s)
                for s in range(2):
                    keep_tokens(U_QKV // 2 - 1, s, False)
                act.wait_ge(gate_dve, l * 19 + 17)
                A(rn[:], rn[:], ACT.Sqrt).then_inc(gate_act, 1)
                stage_end(act, l, 0)

                copy = nc.scalar.copy

                def front_turned(m, t):
                    for b, dst, done in ((4, qT[t], qT_ready), (5, kT[t], kT_ready)):
                        act.wait_ge(qk_turned, m * 2 + b - 3)
                        copy(dst[:].rearrange("p c t -> p (c t)"), PS[:, b, :]).then_inc(done, 1)

                def front_decays(m, t):
                    for r in range(2):
                        edge = P - 1 if r == 0 else 0
                        act.wait_ge(g_rows, m * 2 + r + 1)
                        A(egl[t][r][:], PS[:, 4 + r, :].rearrange("p (c t) -> p c t", c=CHUNKS)[:, :, edge], ACT.Exp)
                        for c in range(CHUNKS):
                            ins = A(DT[r][:, c, :], PS[:, 4 + r, c * P:(c + 1) * P], ACT.Exp,
                                    bias=ht[t][:, T_NEG_CUM, r, c:c + 1])
                        ins.then_inc(decay_done, 1)

                def front_high(m):
                    for r in range(2):
                        act.wait_ge(na_turned, m * 2 + r + 1)
                        copy(NAh[r][:].rearrange("p c t -> p (c t)"), PS[:, 4 + r, :]).then_inc(na_hi, 1)

                def head(h, s, more):
                    n = l * HEADS + h
                    for lev in range(1, 7):
                        for r in range(2):
                            act.wait_ge(vx_mm[r], n * 6 + lev)
                            if lev in BLOCK_LEVELS:
                                new = PS[:, 3 * r + 2, :].rearrange("p (c t) -> p c t", c=CHUNKS)
                                for a, b in new_blocks(lev, r == 1):
                                    ins = copy(X[r][a, :, b], new[a, :, b])
                                ins.then_inc(x_upd[r], 1)
                            else:
                                copy(X[r][:].rearrange("p c t -> p (c t)"), PS[:, 3 * r + 2, :]).then_inc(x_upd[r], 1)
                    for r in range(2):
                        act.wait_ge(e_mm[r], n + 1)
                        A(V[r][:].rearrange("p c t -> p (c t)"), PS[:, 3 * r, :], ACT.Copy,
                          scale=E_SCALE).then_inc(e_ready[r], 1)
                    if more:
                        front_turned(n + 1, 1 - s)
                    for step in range(CHUNKS):
                        chunk = (step, CHUNKS - 1 - step)
                        for r in range(2):
                            c = chunk[r]
                            act.wait_ge(tr_mm[r], n * 4 + step + 1)
                            if step == 0:
                                act.wait_ge(bdl_done, n * 2 + r + 1)
                            A(VN[r][:], PS[:, r, 2 * P:3 * P], ACT.Copy,
                              scale=ht[s][:, T_BETA, r, c:c + 1]).then_inc(vn_ready[r], 1)
                            if step < CHUNKS - 1:
                                A(VS[r][:], PS[:, r, 2 * P:3 * P], ACT.Copy,
                                  scale=bdl[s][r][:, c:c + 1]).then_inc(vs_ready[r], 1)
                        if step > 0:
                            for r in range(2):
                                c = chunk[r]
                                act.wait_ge(qs_mm[r], n * 3 + step)
                                A(O1[r][:], PS[:, 2 + r, 0:P], ACT.Copy,
                                  scale=ht[s][:, T_EG, r, c:c + 1]).then_inc(o1_ready[r], 1)
                        if step == 1:
                            if more:
                                front_decays(n + 1, 1 - s)
                            unit_full(l * PAIRS + AT_DELTA + h, 0)
                            copy(raw[:, bass.ds(h, 1), :, :].rearrange("p a c t -> p (a c t)"),
                                 PS[:, 6, :]).then_inc(extra_out[0], 1)
                    if more:
                        front_high(n + 1)
                    unit_full(l * PAIRS + AT_DELTA + h, 1)
                    copy(raw[:, bass.ds(h + HEADS, 1), :, :].rearrange("p a c t -> p (a c t)"),
                         PS[:, 7, :]).then_inc(extra_out[1], 1)
                    act.wait_ge(o_sum, (n + 1) * 4)
                    for c in range(CHUNKS):
                        ins = A(raw[:, bass.ds(h + 2 * HEADS, 1), c, :].rearrange("p a t -> p (a t)"),
                                o_dn[:, bass.ds(h, 1), c, :].rearrange("p a t -> p (a t)"), ACT.Square,
                                accum_out=rno[:, bass.ds(h, 1), c].rearrange("p a -> p a"))
                    ins.then_inc(o_ss, 1)
                front_turned(l * HEADS, 0)
                front_decays(l * HEADS, 0)
                front_high(l * HEADS)
                with act.Fori(0, HEADS // 2 - 1) as i:
                    head(i * 2, 0, True)
                    head(i * 2 + 1, 1, True)
                head(HEADS - 2, 0, True)
                head(HEADS - 1, 1, False)
                stage_end(act, l, 1)
                act.wait_ge(rno_dve, l * 3 + 1)
                A(rno[:], rno[:], ACT.Sqrt).then_inc(rno_act, 1)

                def gated_output(i, s):
                    act.wait_ge(oz_ready[s], l * 4 + i + 1)
                    A(zs[s][:], raw[:, bass.ds(i * 2 + s, 1), :, :].rearrange("p a c t -> p (a c t)"),
                      ACT.Silu).then_inc(z_silu[s], 1)
                    act.wait_ge(oz_ready[s], l * 4 + i + 2)
                    copy(ozh[:, bass.ds(i * 2 + s, 1), :].rearrange("p a t -> p (a t)"),
                         oz[s][:]).then_inc(oz_hi[s], 1)
                with act.Fori(0, 2) as b:
                    for u in range(4):
                        gated_output(b * 2 + u // 2, u % 2)
                    unit_full(l * PAIRS + AT_SW + b * 2 + 1, 1)
                    for c in (0, 1):
                        copy(o_sw[:, c, bass.ds(b * 512, 512)], PS[:, c, :]).then_inc(sw_act, 1)
                unit_full(l * PAIRS + AT_SW + 5, 1)
                act.wait_ge(rope_mul, (l + 1) * 40)
                for c in range(CHUNKS):
                    ins = copy(kv[:, c, 256:512], PS[:, c, 256:512])
                ins.then_inc(sw_act, 2)
                stage_end(act, l, 2)

                def group_copy(g, n):
                    copy(qg[:], o_sw[:, :, bass.ds(g * (GQ * HD), GQ * HD)]).then_inc(qg_copied, 1)
                    for j in range(2):
                        copy(kg[:, :, j, :], kv[:, :, bass.ds(g * HD, HD)]).then_inc(qg_copied, 1)

                def group_turned(n):
                    for j in range(GQ // 2):
                        act.wait_ge(qg_turned, n * 3 + j + 1)
                        copy(qgT[:, j, :], PS[:, j, :]).then_inc(qgT_act, 1)

                def group(g, more):
                    n = l * GROUPS + g

                    def gate_out(s):
                        unit_full(l * PAIRS + AT_ATT + g, s)
                        copy(gate_b[:, bass.ds(g * 2 + s, 1), :].rearrange("p a t -> p (a t)"),
                             PS[:, 3, :]).then_inc(gate_b_out, 1)
                    for b in range(CHUNKS):
                        nb = min(b + 2, CHUNKS) - max(b - 1, 0)
                        act.wait_ge(stats_step, n * 16 + b * 4 + 3)
                        if b > 0:
                            act.wait_ge(p_turned, n * 4 + b)
                            act.wait_ge(den_step, n * 8 + b * 2)
                        for q in range(GQ):
                            A(pr[:, q, 0:nb, :], PS[:, 0:nb, q * P:(q + 1) * P], ACT.Exp, bias=mn[:, q:q + 1],
                              scale=ATT_SCALE, accum_out=den[:, q:q + 1]).then_inc(probs, 1)
                        act.wait_ge(stats_step, n * 16 + b * 4 + 4)
                        A(es[:], es[:], ACT.Exp).then_inc(sink_exp, 1)
                        act.wait_ge(p_turned, n * 4 + b + 1)
                        copy(pT[:, 0, :], PS[:, 4, :]).then_inc(pT_act, 1)
                        if b == 0 and more:
                            group_copy(g + 1, n + 1)
                        if b == 1:
                            gate_out(0)
                    if more:
                        group_turned(n + 1)
                    gate_out(1)
                group_copy(0, l * GROUPS)
                group_turned(l * GROUPS)
                with act.Fori(0, GROUPS - 1) as g:
                    group(g, True)
                group(GROUPS - 1, False)
                store_hi(osw_t, l * 8, swh, osw_hi)
                stage_end(act, l, 3)

                with act.Fori(0, KT) as j:
                    for gate in (gate_a, gate_b):
                        g = gate[:, bass.ds(j, 1), :].rearrange("p a t -> p (a t)")
                        A(g, g, ACT.Sigmoid).then_inc(gate_sig, 1)
                stage_end(act, l, 4)

                act.dma_start(ln_g[:], ln_rows[l, 0, :].partition_broadcast(P)).then_inc(ln_loaded, 16)
                act.dma_start(ln_b[:], ln_rows[l, 1, :].partition_broadcast(P)).then_inc(ln_loaded, 16)

                def store_yT(n, dst):
                    act.wait_ge(y_mm, l * 2 + n + 1)
                    for k in range(0, KT, 2):
                        copy(dst[:, k, :], PS[:, k, :]).then_inc(yT_act, 1)

                def norm_sqrt(n):
                    for c in range(CHUNKS):
                        act.wait_ge(ln_dve, (l * 2 + n) * LN_STEPS + LN_VARIANCE[c])
                        A(ln_rs[:, c, :], ln_rs[:, c, :], ACT.Sqrt).then_inc(ln_sqrt, 1)
                store_yT(0, yT_a)
                stage_end(act, l, 5)
                norm_sqrt(0)
                store_normed(l, 0)

                with act.Fori(0, FT // 2) as i:
                    for j in range(2):
                        n = (l * 11 + i) * 2 + j
                        unit_full(l * PAIRS + AT_GU + i * 2 + j, 0)
                        A(sg[j][:], PS[:, 2 * j, :], ACT.Silu).then_inc(ff_silu, 1)
                        act.wait_ge(ff_h, n + 3)
                        A(hh[:, bass.ds(i * 2 + j, 1), :].rearrange("p a t -> p (a t)"), hf[j][:],
                          ACT.Copy).then_inc(ff_hi, 1)
                act.wait_ge(ff_lo, (l + 1) * FT)
                act.dma_start(ln_g[:], ln_rows[l, 2, :].partition_broadcast(P)).then_inc(ln_loaded, 16)
                act.dma_start(ln_b[:], ln_rows[l, 3, :].partition_broadcast(P)).then_inc(ln_loaded, 16)
                store_yT(1, yT_b)
                stage_end(act, l, 6)
                norm_sqrt(1)
                store_normed(l, 1)

        @block.vector
        def _(dve):
            TT = nc.vector.tensor_tensor
            TS = nc.vector.tensor_scalar
            STT = nc.vector.scalar_tensor_tensor

            def store_lo(hi_done, base_count, hi, lo, done):
                for k in range(KT):
                    dve.wait_ge(hi_done, base_count + k + 1)
                    TT(lo[:, k, :], PS[:, k, :], hi[:, k, :].bitcast(F32), ALU.subtract).then_inc(done, 1)

            dve.wait_ge(small_loaded, 16 * SMALL)
            nc.vector.tensor_copy(id_bf[:], ident).then_inc(ready_bf, 1)
            nc.vector.tensor_copy(id_16[:], ident).then_inc(ready_bf, 1)
            TS(minus_two[:], ident, -2.0, None, ALU.mult).then_inc(ready_bf, 1)
            for r in range(2):
                TS(neg_bf[r][:], tri[r], 1.0, NEG_BIG, ALU.subtract, ALU.mult).then_inc(ready_bf, 1)
            nc.vector.memset(ln_rs[:], 0.0).then_inc(ready_bf, 1)
            dve.sem_inc(sw_dve, 1)
            dve.sem_inc(rope_half, 4)
            for s in range(2):
                dve.sem_inc(oz_ready[s], 1)
                dve.sem_inc(on_used[s], 1)
                dve.sem_inc(mg_mul, 2)
                dve.sem_inc(ff_h, 1)
            dve.wait_ge(ready_bf, 7)
            store_lo(x_hi, 0, xh, xl, x_lo)
            with dve.Fori(0, DEPTH) as l:
                for s in range(2):
                    nc.vector.memset(conv_in[s][:, 0:2], 0.0)
                    nc.vector.memset(conv_in[s][:, SEQ + 2:SEQ + 4], 0.0)
                g0 = l * 19

                def link(ins, n):
                    ins.then_inc(gate_dve, 1)
                    dve.wait_ge(gate_dve, g0 + n)
                dve.wait_ge(ba_mm, l * 2 + 2)
                link(nc.vector.tensor_copy(ba[:].rearrange("p c n -> p (c n)"), PS[:, 5, 0:128]), 1)
                bias = dtb[:, bass.ds(l * 16, 16)].unsqueeze(1).broadcast_to([P, CHUNKS, 16])
                ea = exp_a[:, bass.ds(l * 16, 16)].unsqueeze(1).broadcast_to([P, CHUNKS, 16])
                link(TT(sm[0][:], ba[:, :, 16:32], bias, ALU.add), 2)
                link(TS(sm[1][:], sm[0][:], -1.0, None, ALU.mult), 3)
                link(TT(sm[2][:], sm[0][:], sm[1][:], ALU.min), 4)
                dve.wait_ge(gate_act, l * 5 + 1)
                link(TS(sm[4][:], sm[3][:], 1.0, None, ALU.add), 5)
                link(STT(sm[6][:], sm[4][:], 1.0, sm[3][:], ALU.subtract, ALU.subtract), 6)
                dve.wait_ge(gate_act, l * 5 + 2)
                link(nc.vector.reciprocal(sm[7][:], sm[4][:]), 7)
                link(TT(sm[7][:], sm[6][:], sm[7][:], ALU.mult), 8)
                link(TT(sm[5][:], sm[5][:], sm[7][:], ALU.subtract), 9)
                nc.vector.scalar_tensor_tensor(sm[1][:], sm[0][:], 0.0, sm[5][:], ALU.max,
                                               ALU.add).then_inc(gate_pre, 1)
                dve.wait_ge(gate_pre, l + 1)
                link(TT(sm[8][:], sm[1][:], ea, ALU.mult), 10)
                for r in range(2):
                    ins = TS(tab[:, :, T_G, r, :].rearrange("p h c -> p c h"), sm[8][:, :, r * 8:(r + 1) * 8], -1.0,
                             None, ALU.mult)
                link(ins, 11)
                dve.wait_ge(cum_mm, l + 1)
                for r in range(2):
                    ins = TS(tab[:, :, T_NEG_CUM, r, :].rearrange("p h c -> p c h"),
                             PS[:, 4, r * 32:(r + 1) * 32].rearrange("p (c h) -> p c h", c=CHUNKS), 1.0, None,
                             ALU.mult)
                    link(ins, 12 + r)
                dve.wait_ge(gate_act, l * 5 + 3)
                for kind, sign in ((T_BETA, 1.0), (T_NEG_BETA, -1.0)):
                    for r in range(2):
                        ins = TS(tab[:, :, kind, r, :].rearrange("p h c -> p c h"), sm[9][:, :, r * 8:(r + 1) * 8],
                                 sign, None, ALU.mult)
                    link(ins, 14 + (kind == T_NEG_BETA))
                dve.wait_ge(gate_act, l * 5 + 4)
                link(TS(tab[:, :, T_NEG_EG].rearrange("p h r c -> p h (r c)"),
                        tab[:, :, T_EG].rearrange("p h r c -> p h (r c)"), -1.0, None, ALU.mult), 16)
                settle(dve)

                with dve.Fori(0, U_QKV // 2) as i:
                    n = l * 12 + i
                    for s in range(2):
                        tile = l * U_QKV + i * 2 + s
                        dve.wait_ge(conv_loaded[s], n + 1)
                        for j in range(CONV):
                            w = cw[:, bass.ds(tile, 1), j:j + 1].rearrange("p a b -> p (a b)")
                            if j == 0:
                                TS(conv_acc[s][:], conv_in[s][:, 0:SEQ], w, None, ALU.mult).then_inc(conv_step[s], 1)
                            else:
                                dve.wait_ge(conv_step[s], n * 5 + j)
                                STT(conv_acc[s][:], conv_in[s][:, j:j + SEQ], w, conv_acc[s][:], ALU.mult,
                                    ALU.add).then_inc(conv_step[s], 1)
                dve.wait_ge(tok_stored, l * U_QKV + 2 * HEADS + 1)
                link(TS(rn[:], rn[:], RMS_EPS, None, ALU.add), 17)
                dve.wait_ge(gate_act, l * 5 + 5)
                link(nc.vector.reciprocal(rn[:], rn[:]), 18)
                link(TS(rn[:, 0:HEADS, :], rn[:, 0:HEADS, :], float(P) ** -0.5, None, ALU.mult), 19)
                stage_end(dve, l, 0)

                def bank(b):
                    return PS[:, b, :].rearrange("p (c t) -> p c t", c=CHUNKS)

                def front_scale(h, m, t):
                    nc.vector.tensor_copy(ht[t][:].rearrange("p k r c -> p (k r c)"),
                                          tab[:, bass.ds(h, 1)].rearrange("p a k r c -> p (a k r c)")).then_inc(head_cols, 1)
                    for u, dst in ((0, qn), (HEADS, kn[t])):
                        src = raw[:, bass.ds(h + u, 1), :, :].rearrange("p a c t -> p (a c) t")
                        TT(dst[:], src, cols(rn[:, bass.ds(h + u, 1), :].rearrange("p a c -> p (a c)")),
                           ALU.mult).then_inc(qk_normed, 1)

                def front_tri(m, t):
                    dve.wait_ge(head_cols, m + 1)
                    for r in range(2):
                        TT(TMP[r][:], rows(tri[r]), cols(ht[t][:, T_G, r, :]), ALU.mult).then_inc(g_tri, 1)

                def front_nat(m, t, r):
                    dve.wait_ge(decay_done, m * 2 + r + 1)
                    TT(TMP[r][:], DT[r][:], cols(ht[t][:, T_NEG_BETA, r, :]), ALU.mult).then_inc(beta_decay, 1)
                    dve.wait_ge(beta_decay, m * 2 + r + 1)
                    dve.wait_ge(kk_done, m + 1)
                    TT(NAT[r][:], TMP[r][:], bank(4), ALU.mult).then_inc(nat_raw, 1)
                    dve.wait_ge(nat_raw, m * 2 + r + 1)
                    settle(dve)
                    nc.vector.copy_predicated(NAT[r][:], rows(ident.bitcast(I32)), rows(ident)).then_inc(nat_done, 1)


                def front_qk(m, t, r):
                    dve.wait_ge(kq_done, m + 1)
                    TT(QKT[t][r][:], DT[r][:], bank(5), ALU.mult).then_inc(qkt_done, 1)

                def front_start(m, t):
                    for r in range(2):
                        dve.wait_ge(nat_done, m * 2 + r + 1)
                        TT(Y[r][:], NAT[r][:], rows(y_mask[r][0]), ALU.mult).then_inc(y_upd[r], 1)
                    for r in range(2):
                        dve.wait_ge(na_hi, m * 2 + r + 1)
                        TT(X[r][:], NAh[r][:], rows(x_mask[r][0]), ALU.mult).then_inc(x_upd[r], 1)
                    for r in range(2):
                        edge = P - 1 if r == 0 else 0
                        TT(bdl[t][r][:], DT[r][:, :, edge], ht[t][:, T_BETA, r, :], ALU.mult).then_inc(bdl_done, 1)

                def head(h, s, more):
                    n = l * HEADS + h

                    def value(c):
                        return raw[:, bass.ds(h + 2 * HEADS, 1), c, :].rearrange("p a t -> p (a t)")

                    def output(step):
                        for r in range(2):
                            c = step if r == 0 else CHUNKS - 1 - step
                            o = o_dn[:, bass.ds(h, 1), c, :].rearrange("p a t -> p (a t)")
                            dve.wait_ge(o_mm[r], n * 4 + step + 1)
                            if step == 0:
                                nc.vector.tensor_copy(o, PS[:, 2 + r, P:2 * P]).then_inc(o_out[r], 1)
                                continue
                            dve.wait_ge(o1_ready[r], n * 3 + step)
                            if step > CHUNKS // 2:
                                dve.wait_ge(o_sum, n * 4 + r + 1)
                            TT(o if step < CHUNKS // 2 else OT[r][:], PS[:, 2 + r, P:2 * P], O1[r][:],
                               ALU.add).then_inc(o_out[r], 1)
                        if step >= CHUNKS // 2:
                            for r in range(2):
                                c = step if r == 0 else CHUNKS - 1 - step
                                o = o_dn[:, bass.ds(h, 1), c, :].rearrange("p a t -> p (a t)")
                                dve.wait_ge(o_out[r], n * 4 + step + 1)
                                TT(o, o, OT[r][:], ALU.add).then_inc(o_sum, 1)
                    for lev in range(1, 7):
                        for r in range(2):
                            dve.wait_ge(v_mm[r], n * 6 + lev)
                            if lev == 1:
                                dve.wait_ge(y_upd[r], n * 7 + 1)
                            TT(V[r][:], bank(3 * r), rows(y_mask[r][lev]), ALU.mult).then_inc(v_ready[r], 1)
                        if lev == 1:
                            for r in range(2):
                                dve.wait_ge(na_hi, n * 2 + r + 1)
                                TT(NAl[r][:], bank(4 + r), NAh[r][:], ALU.subtract).then_inc(na_lo, 1)
                        for r in range(2):
                            dve.wait_ge(xv_mm[r], n * 6 + lev)
                            if lev in BLOCK_LEVELS:
                                for a, b in new_blocks(lev, r == 0):
                                    ins = nc.vector.tensor_copy(Y[r][a, :, b], bank(3 * r + 1)[a, :, b])
                                ins.then_inc(y_upd[r], 1)
                            else:
                                TT(Y[r][:], bank(3 * r + 1), Y[r][:], ALU.add).then_inc(y_upd[r], 1)
                    if more:
                        front_scale(h + 1, n + 1, 1 - s)
                    for r in range(2):
                        dve.wait_ge(y_fix[r], n + 1)
                        STT(YF[r][:], bank(3 * r), 1.0 / E_SCALE, Y[r][:], ALU.mult, ALU.add).then_inc(y_done[r], 1)
                    for step in range(CHUNKS):
                        for r in range(2):
                            c = step if r == 0 else CHUNKS - 1 - step
                            if step > 0:
                                dve.wait_ge(ks_mm[r], n * 3 + step)
                                STT(R[r][:], PS[:, r, 0:P], ht[s][:, T_NEG_EG, r, c:c + 1], value(c), ALU.mult,
                                    ALU.add).then_inc(r_ready[r], 1)
                        if step > 0:
                            output(step - 1)
                        if more and step == 0:
                            for r in range(2):
                                dve.wait_ge(y_done[r], n + 1)
                            front_tri(n + 1, 1 - s)
                        if more and step >= 2:
                            if step == 3:
                                front_qk(n + 1, 1 - s, 0)
                            front_nat(n + 1, 1 - s, step - 2)
                        if step < CHUNKS - 1:
                            for r in range(2):
                                c = step if r == 0 else CHUNKS - 1 - step
                                dve.wait_ge(st_mm[r], n * 3 + step + 1)
                                if step == 0:
                                    nc.vector.tensor_copy(S[r][0][:], PS[:, r, P:2 * P]).then_inc(s_ready[r], 1)
                                else:
                                    dve.wait_ge(s_ready[r], n * 3 + step)
                                    STT(S[r][step % 2][:], S[r][(step - 1) % 2][:], egl[s][r][:, c:c + 1],
                                        PS[:, r, P:2 * P], ALU.mult,
                                        ALU.add).then_inc(s_ready[r], 1)
                    output(CHUNKS - 1)
                    if more:
                        front_qk(n + 1, 1 - s, 1)
                        front_start(n + 1, 1 - s)
                front_scale(0, l * HEADS, 0)
                front_tri(l * HEADS, 0)
                front_nat(l * HEADS, 0, 0)
                front_nat(l * HEADS, 0, 1)
                for r in range(2):
                    front_qk(l * HEADS, 0, r)
                front_start(l * HEADS, 0)
                with dve.Fori(0, HEADS // 2 - 1) as i:
                    head(i * 2, 0, True)
                    head(i * 2 + 1, 1, True)
                head(HEADS - 2, 0, True)
                head(HEADS - 1, 1, False)
                stage_end(dve, l, 1)
                dve.wait_ge(o_ss, (l + 1) * HEADS)
                TS(rno[:], rno[:], 1.0 / P, RMS_EPS, ALU.mult, ALU.add).then_inc(rno_dve, 1)
                dve.wait_ge(rno_act, l + 1)
                nc.vector.reciprocal(rno[:], rno[:]).then_inc(rno_dve, 1)
                dve.wait_ge(rno_dve, l * 3 + 2)
                dve.sem_inc(rno_dve, 1)

                def gated_output(i, s):
                    n = l * 4 + i
                    src = o_dn[:, bass.ds(i * 2 + s, 1), :, :].rearrange("p a c t -> p (a c) t")
                    dve.wait_ge(on_used[s], n + 1)
                    TT(on[s][:], src, cols(rno[:, bass.ds(i * 2 + s, 1), :].rearrange("p a c -> p (a c)")),
                       ALU.mult).then_inc(on_ready[s], 1)
                    dve.wait_ge(on_turned[s], n + 1)
                    dve.wait_ge(z_silu[s], n + 1)
                    dve.sem_inc(on_used[s], 1)
                    STT(oz[s][:], PS[:, 4 + s, :], dn_w[:, bass.ds(l, 1)], zs[s][:], ALU.mult,
                        ALU.mult).then_inc(oz_ready[s], 1)
                    dve.wait_ge(oz_hi[s], n + 1)
                    hi = ozh[:, bass.ds(i * 2 + s, 1), :].rearrange("p a t -> p (a t)")
                    lo = ozl[:, bass.ds(i * 2 + s, 1), :].rearrange("p a t -> p (a t)")
                    TT(lo, oz[s][:], hi.bitcast(F32), ALU.subtract).then_inc(oz_lo[s], 1)
                    dve.wait_ge(oz_lo[s], n + 1)
                with dve.Fori(0, 2) as b:
                    for u in range(4):
                        gated_output(b * 2 + u // 2, u % 2)
                    dve.wait_ge(unit_done[1], l * PAIRS + AT_SW + b * 2 + 3)
                    for c in (2, 3):
                        nc.vector.tensor_copy(o_sw[:, c, bass.ds(b * 512, 512)], PS[:, c, :]).then_inc(sw_dve, 1)

                cos2 = cst[:, C_COS:C_COS + CHUNKS * 32].rearrange("p (c k) -> p c k", c=CHUNKS).unsqueeze(2).broadcast_to([P, CHUNKS, 2, 32])
                sin2 = cst[:, C_SIN:C_SIN + CHUNKS * 32].rearrange("p (c k) -> p c k", c=CHUNKS).unsqueeze(2).broadcast_to([P, CHUNKS, 2, 32])

                def rotate(src, dst, s, m):
                    src, dst = (t.rearrange("p c (q k) -> p c q k", q=2) for t in (src, dst))
                    a, b = src[:, :, :, 0:32], src[:, :, :, 32:64]
                    t = rope[s]
                    dve.wait_ge(rope_half, m * 2 + 2)
                    for part, u, table in ((t[0], a, cos2), (t[1], b, sin2), (t[2], b, cos2), (t[3], a, sin2)):
                        TT(part[:], u, table, ALU.mult).then_inc(rope_mul, 1)
                    dve.wait_ge(rope_mul, m * 4 + 4)
                    TT(dst[:, :, :, 0:32], t[0][:], t[1][:], ALU.subtract).then_inc(rope_half, 1)
                    TT(dst[:, :, :, 32:64], t[2][:], t[3][:], ALU.add).then_inc(rope_half, 1)
                dve.wait_ge(sw_act, (l * 3 + 2) * 2 + 1)
                settle(dve)
                with dve.Fori(0, 4) as j:
                    for s in range(2):
                        pair = o_sw[:, :, bass.ds((j * 2 + s) * (2 * HD), 2 * HD)]
                        rotate(pair, pair, s, l * 10 + j * 2 + s)
                dve.wait_ge(unit_done[1], l * PAIRS + AT_SW + 7)
                for s in range(2):
                    rotate(PS[:, 0:CHUNKS, s * 128:(s + 1) * 128], kv[:, :, s * 128:(s + 1) * 128], s, l * 10 + 8 + s)
                dve.sem_inc(sw_dve, 2)
                stage_end(dve, l, 2)

                def group_turned(n):
                    dve.wait_ge(qg_turned, n * 3 + 3)
                    for j in range(2):
                        part = slice(j * HD, (j + 1) * HD)
                        nc.vector.tensor_copy(kgT[part, j, :], PS[part, 2, :]).then_inc(qgT_dve, 1)

                def group(g, more):
                    n = l * GROUPS + g
                    snk_g = snk[:, bass.ds(l * 16 + g * GQ, GQ)]

                    def stats(b, m, sinks_of):
                        lo, hi = max(b - 1, 0), min(b + 2, CHUNKS)
                        dve.wait_ge(scores, m)
                        nc.vector.tensor_reduce(mx[:], PS[:, 0:hi - lo, :].rearrange("p j (q t) -> p q j t", q=GQ),
                                                mybir.AxisListType.XY, ALU.max).then_inc(stats_step, 1)
                        dve.wait_ge(stats_step, m * 4 - 3)
                        STT(mx[:], mx[:], ATT_SCALE, sinks_of, ALU.mult, ALU.max).then_inc(stats_step, 1)
                        dve.wait_ge(stats_step, m * 4 - 2)
                        TS(mn[:], mx[:], -1.0, None, ALU.mult).then_inc(stats_step, 1)
                        TT(es[:], sinks_of, mx[:], ALU.subtract).then_inc(stats_step, 1)
                    stats(0, n * 4 + 1, snk_g)
                    for b in range(CHUNKS):
                        lo, hi = max(b - 1, 0), min(b + 2, CHUNKS)
                        m = n * 4 + b + 1
                        dve.wait_ge(probs, m * 4)
                        dve.wait_ge(sink_exp, m)
                        TT(den[:], den[:], es[:], ALU.add).then_inc(den_step, 1)
                        dve.wait_ge(den_step, m * 2 - 1)
                        nc.vector.reciprocal(rd[:], den[:]).then_inc(den_step, 1)
                        if b < CHUNKS - 1:
                            stats(b + 1, m + 1, snk_g)
                        dve.wait_ge(p_turned, m)
                        for j in range(1, hi - lo):
                            ins = nc.vector.tensor_copy(pT[:, j, :], PS[:, 4 + j, :])
                        ins.then_inc(pT_dve, 1)
                        if b == CHUNKS - 1 and more:
                            group_turned(n + 1)
                        dve.wait_ge(den_step, m * 2)
                        dve.wait_ge(pv_mm, m)
                        TT(o_sw[:, b, bass.ds(g * GQ * HD, GQ * HD)].rearrange("p (q k) -> p q k", q=GQ),
                           PS[:, 7, 0:GQ * HD].rearrange("p (q k) -> p q k", q=GQ), cols(rd[:], HD),
                           ALU.mult).then_inc(o_scaled, 1)
                for j in range(2):
                    part = slice((1 - j) * HD, (2 - j) * HD)
                    nc.vector.memset(kgT[part, j, :], 0.0)
                group_turned(l * GROUPS)
                with dve.Fori(0, GROUPS - 1) as g:
                    group(g, True)
                group(GROUPS - 1, False)
                store_lo(osw_hi, l * 8, swh, swl, osw_lo)
                stage_end(dve, l, 3)

                with dve.Fori(0, KT // 2) as i:
                    for j in range(2):
                        n = (l * 4 + i) * 2 + j
                        pair = l * PAIRS + AT_MERGE + i * 2 + j
                        tile = i * 2 + j
                        ga, gb, hi, lo = (t[:, bass.ds(tile, 1), :].rearrange("p a t -> p (a t)")
                                          for t in (gate_a, gate_b, mgh, mgl))
                        dve.wait_ge(gate_sig, n * 2 + 2)
                        dve.wait_ge(unit_done[0], pair + 2)
                        TT(ga, ga, PS[:, 2 * j, :], ALU.mult).then_inc(mg_mul, 1)
                        dve.wait_ge(unit_done[1], pair + 2)
                        TT(gb, gb, PS[:, 2 * j + 1, :], ALU.mult).then_inc(mg_mul, 1)
                        dve.wait_ge(mg_mul, n * 2 + 6)
                        TT(gb, ga, gb, ALU.add).then_inc(mg_sum, 1)
                        dve.wait_ge(mg_sum, n + 1)
                        nc.vector.tensor_copy(hi, gb).then_inc(mg_hi, 1)
                        dve.wait_ge(mg_hi, n + 1)
                        TT(lo, gb, hi.bitcast(F32), ALU.subtract).then_inc(mg_lo, 1)
                        dve.wait_ge(mg_lo, n + 1)
                stage_end(dve, l, 4)

                def store_yT(n, dst):
                    dve.wait_ge(y_mm, l * 2 + n + 1)
                    for k in range(1, KT, 2):
                        nc.vector.tensor_copy(dst[:, k, :], PS[:, k, :]).then_inc(yT_dve, 1)

                def norm(n):
                    m = l * 2 + n
                    for c in range(CHUNKS):
                        dve.wait_ge(y_turned, m * 4 + c + 1)
                        STT(x[:, c, :].rearrange("p (b t) -> p b t", b=2), x[:, c, :].rearrange("p (b t) -> p b t", b=2),
                            ALPHA, PS[:, 2 * c:2 * c + 2, :], ALU.mult, ALU.add).then_inc(ln_dve, 1)
                    stage_end(dve, l, 5 + n)

                    def moments(c):
                        dve.wait_ge(ln_dve, m * LN_STEPS + c + 1)
                        for half in range(2):
                            nc.vector.bn_stats(ln_st[:, c, half * 6:half * 6 + 6],
                                               x[:, c, half * 512:(half + 1) * 512]).then_inc(ln_dve, 1)

                    def variance(c):
                        dve.wait_ge(ln_dve, m * LN_STEPS + LN_VARIANCE[c] - 2)
                        settle(dve)
                        nc.vector.bn_aggr(ln_mv[:, c, :], ln_st[:, c, :]).then_inc(ln_dve, 1)
                        dve.wait_ge(ln_dve, m * LN_STEPS + LN_VARIANCE[c] - 1)
                        TS(ln_rs[:, c, :], ln_mv[:, c, 1:2], LN_EPS, None, ALU.add).then_inc(ln_dve, 1)

                    def normed(c):
                        dve.wait_ge(ln_sqrt, m * 4 + c + 1)
                        nc.vector.reciprocal(ln_rs[:, c, :], ln_rs[:, c, :]).then_inc(ln_dve, 1)
                        dve.wait_ge(ln_dve, m * LN_STEPS + LN_NORMED[c] - 1)
                        TS(x[:, c, :], x[:, c, :], ln_mv[:, c, 0:1], ln_rs[:, c, :], ALU.subtract,
                           ALU.mult).then_inc(ln_dve, 1)
                    moments(0)
                    moments(1)
                    variance(0)
                    moments(2)
                    normed(0)
                    variance(1)
                    moments(3)
                    normed(1)
                    variance(2)
                    variance(3)
                    normed(2)
                    normed(3)

                    def scaled(k):
                        dve.wait_ge(x_t, m * 8 + 8 + k + 1)
                        dve.wait_ge(x_lo, m * 8 + 8 + k - 2)
                        gain, offset = (ln_c[:, bass.ds(m, 1), j, k].rearrange("p a -> p a") for j in range(2))
                        TS(xf[k % 3][:], PS[:, k, :], gain, offset, ALU.mult, ALU.add).then_inc(xf_dve, 1)

                    def low_part(k):
                        dve.wait_ge(x_hi, m * 8 + 8 + k + 1)
                        TT(xl[:, k, :], xf[k % 3][:], xh[:, k, :].bitcast(F32), ALU.subtract).then_inc(x_lo, 1)
                    scaled(1)
                    low_part(0)
                    scaled(3)
                    low_part(1)
                    low_part(2)
                    scaled(5)
                    low_part(3)
                    low_part(4)
                    scaled(7)
                    low_part(5)
                    low_part(6)
                    low_part(7)
                    dve.wait_ge(ln_loaded, m * 32 + 32)
                    for c in range(CHUNKS):
                        dve.wait_ge(ln_dve, m * LN_STEPS + LN_NORMED[c])
                        TT(x[:, c, :], x[:, c, :], ln_g[:], ALU.mult).then_inc(ln_dve, 1)
                    for c in range(CHUNKS):
                        dve.wait_ge(ln_dve, m * LN_STEPS + LN_NORMED[-1] + c + 1)
                        TT(x[:, c, :], x[:, c, :], ln_b[:], ALU.add).then_inc(ln_dve, 1)
                store_yT(0, yT_a)
                norm(0)

                with dve.Fori(0, FT // 2) as i:
                    for j in range(2):
                        n = (l * 11 + i) * 2 + j
                        dve.wait_ge(ff_silu, n + 1)
                        dve.wait_ge(unit_done[1], l * PAIRS + AT_GU + i * 2 + j + 2)
                        TT(hf[j][:], sg[j][:], PS[:, 2 * j + 1, :], ALU.mult).then_inc(ff_h, 1)
                        dve.wait_ge(ff_hi, n + 1)
                        hi = hh[:, bass.ds(i * 2 + j, 1), :].rearrange("p a t -> p (a t)")
                        lo = hl[:, bass.ds(i * 2 + j, 1), :].rearrange("p a t -> p (a t)")
                        TT(lo, hf[j][:], hi.bitcast(F32), ALU.subtract).then_inc(ff_lo, 1)
                dve.wait_ge(ff_lo, (l + 1) * FT)
                store_yT(1, yT_b)
                norm(1)


def constants():
    i = np.arange(P)
    tiles = [np.eye(P), i[:, None] <= i[None, :], i[:, None] >= i[None, :], np.ones((P, P))]
    lows = [((i[:, None] // (2 * s)) == (i[None, :] // (2 * s))) & ((i[:, None] // s) % 2 == 1)
            & ((i[None, :] // s) % 2 == 0) for s in LEVELS]
    lows[0] = lows[0] | (i[:, None] == i[None, :])
    tiles += lows + [m.T for m in lows]
    half = HD // 2
    inv_freq = np.float32(10000.0) ** (-np.arange(half, dtype=np.float32) / np.float32(half))
    ang = np.arange(SEQ, dtype=np.float32)[:, None] * inv_freq[None, :]
    for table in (np.cos(ang), np.sin(ang)):
        tiles.append(table.reshape(CHUNKS, P, half).transpose(1, 0, 2).reshape(P, CHUNKS * half))
    return np.concatenate([np.asarray(t, np.float32) for t in tiles], axis=1)


def feature_tiles(w):
    n = w.shape[1] // P
    return w.reshape(KT, P, n, P).transpose(2, 1, 0, 3).reshape(n, P, KT * P)


def kernel(x, w_in, conv_w, a_log, dt_bias, dn_norm_w, sinks, w_branch_a, w_branch_b, w_out,
           ln1_g, ln1_b, w_gate_up, w_down, ln2_g, ln2_b):
    import concourse.bacc as bacc
    from concourse.bass_utils import run_bass_kernel_spmd

    w_in, w_gate_up, w_down, w_out = (np.asarray(a) for a in (w_in, w_gate_up, w_down, w_out))
    w_branch_a, w_branch_b = np.asarray(w_branch_a), np.asarray(w_branch_b)
    units = []
    for l in range(DEPTH):
        qkv, z, ba_cols, sw_cols, gates = np.split(w_in[l], [3072, 4096, 4128, 5664], axis=1)
        units.append(feature_tiles(qkv))
        gate_tiles = feature_tiles(gates)
        units.append(np.stack([feature_tiles(z), gate_tiles[:KT]], axis=1).reshape(-1, P, 1024))
        units.append(sw_cols.reshape(KT // 2, 2, P, SWC // 512, 512).transpose(3, 0, 2, 1, 4).reshape(-1, P, 1024))
        units.append(gate_tiles[KT:])
        units.append(np.stack([feature_tiles(w_branch_a[l]), feature_tiles(w_branch_b[l])],
                              axis=1).reshape(-1, P, 1024))
        units.append(w_out[l].reshape(KT, P, 1024))
        gu = feature_tiles(w_gate_up[l])
        units.append(np.stack([gu[:FT], gu[FT:]], axis=1).reshape(-1, P, 1024))
        units.append(w_down[l].reshape(FT, P, 1024))
    stream = np.concatenate(units).reshape(DEPTH, PAIRS, 2, P, 1024)

    def row(a):
        return np.ascontiguousarray(np.asarray(a).reshape(-1))
    arrays = {
        "x_in": np.asarray(x).reshape(CHUNKS, P, D).transpose(1, 0, 2),
        "stream": stream,
        "w_ba": w_in[:, :, 4096:4128].reshape(DEPTH, KT, P, 32).transpose(0, 2, 1, 3),
        "conv_w": np.asarray(conv_w).reshape(DEPTH, CONV, U_QKV, P).transpose(3, 0, 2, 1).reshape(P, DEPTH * U_QKV, CONV),
        "a_log": row(a_log),
        "dt_bias": row(dt_bias),
        "dn_norm": np.asarray(dn_norm_w).transpose(1, 0),
        "sinks": row(sinks),
        "ln_rows": np.stack([np.asarray(a) for a in (ln1_g, ln1_b, ln2_g, ln2_b)], axis=1),
        "ln_cols": np.stack([np.asarray(a) for a in (ln1_g, ln1_b, ln2_g, ln2_b)], axis=1).reshape(
            DEPTH * 2, 2, KT, P).transpose(3, 0, 1, 2),
        "consts": constants(),
    }
    arrays = {k: np.ascontiguousarray(v) for k, v in arrays.items()}
    nc = bacc.Bacc("TRN2", target_bir_lowering=False, num_devices=1)
    args = [nc.dram_tensor(k, v.shape, mybir.dt.from_np(v.dtype), kind="ExternalInput").ap() for k, v in arrays.items()]
    out = nc.dram_tensor("out", (P, CHUNKS, D), F32, kind="ExternalOutput").ap()
    trunk(nc, *args, out)
    result = run_bass_kernel_spmd(nc, [arrays], core_ids=[0]).results[0]["out"]
    return result.transpose(1, 0, 2).reshape(1, SEQ, D)
```
